# Optimizing a Trainium2 kernel written in Bass

```python
import math
import jax
import jax.numpy as jnp
from jax import lax
import numpy as np

D_MODEL = 1024
BATCH = 1
SEQ = 512
DEPTH = 2
DEC_BATCH = 8
DEC_SEQ = 8
PAST_LEN = 1024
PAGE_SIZE = 128

HEAD_DIM = 64
GLA_HEADS = D_MODEL // 256
GLA_DV = 64
GLA_DK = 32
GLA_RANK = 16
GLA_TAU = 16.0
HGRN_HEADS = D_MODEL // 256
HGRN_DK = 64
HGRN_DV = 64
ATT_HEADS = D_MODEL // 128
DILATED_GROUPS = ((128, 1), (512, 4), (2048, 16))
WINDOW_MAX = 2048
ROT_DIM = HEAD_DIM // 4
ROPE_THETA = 500000.0
CHUNK = 64
D_FF = 2816
N_EXPERTS = 8
TOP_K = 2
D_FF_EXPERT = 1408
EPS = 1e-6

MIX_WIDTH = GLA_HEADS * GLA_DV + HGRN_HEADS * HGRN_DV + ATT_HEADS * HEAD_DIM
IN_SPLITS = (
    GLA_HEADS * GLA_DK,
    GLA_HEADS * GLA_DK,
    GLA_HEADS * GLA_DV,
    GLA_RANK,
    GLA_HEADS * GLA_DV,
    HGRN_HEADS * HGRN_DK,
    HGRN_HEADS * HGRN_DK,
    HGRN_HEADS * HGRN_DV,
    HGRN_HEADS * HGRN_DV,
    ATT_HEADS * HEAD_DIM,
    ATT_HEADS * HEAD_DIM,
    ATT_HEADS * HEAD_DIM,
)
N_IN = sum(IN_SPLITS)
N_DENSE = (DEPTH + 1) // 2
N_MOE = DEPTH // 2

kernel_name = 'hymba_gla_hgrn2_dilated_decoder_step'

def rmsnorm(x, g):
    xf = x.astype(jnp.float32)
    y = xf * lax.rsqrt(jnp.mean(xf * xf, axis=-1, keepdims=True) + EPS)
    return (y * g.astype(jnp.float32)).astype(x.dtype)

def rope_partial(x, pos):
    half = ROT_DIM // 2
    inv_freq = ROPE_THETA ** (-jnp.arange(0, ROT_DIM, 2, dtype=jnp.float32) / ROT_DIM)
    ang = pos.astype(jnp.float32)[:, None] * inv_freq[None, :]
    cos = jnp.cos(ang)[None, :, None, :]
    sin = jnp.sin(ang)[None, :, None, :]
    xf = x.astype(jnp.float32)
    x1, x2, rest = xf[..., :half], xf[..., half:ROT_DIM], xf[..., ROT_DIM:]
    return jnp.concatenate([x1 * cos - x2 * sin, x2 * cos + x1 * sin, rest], axis=-1).astype(x.dtype)

def gated_linear_chunked(q, k, v, log_a, s0, chunk):
    B, L, H, K = q.shape
    V = v.shape[-1]
    n = L // chunk

    def blocks(t):
        return t.astype(jnp.float32).reshape(B, n, chunk, H, t.shape[-1]).transpose(1, 0, 2, 3, 4)

    causal = jnp.tril(jnp.ones((chunk, chunk), dtype=bool))[None, :, :, None, None]

    def step(S, inp):
        qc, kc, vc, gc = inp
        b = jnp.cumsum(gc, axis=1)
        decay = jnp.exp(jnp.where(causal, b[:, :, None] - b[:, None, :], -jnp.inf))
        A = jnp.einsum('btshk,bshk->btsh', decay * qc[:, :, None], kc)
        o = (jnp.einsum('btsh,bshv->bthv', A, vc)
             + jnp.einsum('bthk,bhkv->bthv', qc * jnp.exp(b), S))
        b_last = b[:, -1]
        S = (jnp.exp(b_last)[..., None] * S
             + jnp.einsum('bshk,bshv->bhkv', kc * jnp.exp(b_last[:, None] - b), vc))
        return S, o

    S, o = lax.scan(step, s0.astype(jnp.float32), (blocks(q), blocks(k), blocks(v), blocks(log_a)))
    o = o.transpose(1, 0, 2, 3, 4).reshape(B, L, H, V)
    return o, S

def combine_dilations(parts):
    m_all = jnp.stack([p[0] for p in parts])
    m_top = jnp.max(m_all, axis=0)
    w = jnp.exp(m_all - m_top)
    den = jnp.sum(w * jnp.stack([p[1] for p in parts]), axis=0)
    num = jnp.sum(w[..., None] * jnp.stack([p[2] for p in parts]), axis=0)
    return num / den[..., None]

def dilated_attention_prompt(q, k, v):
    B, S, H, Dh = q.shape
    scale = Dh ** -0.5
    parts = []
    for window, dil in DILATED_GROUPS:
        band = window // dil
        L = S // dil
        nb = -(-L // band)
        Lp = nb * band

        def residues(t):
            t = t.reshape(B, L, dil, H, Dh).transpose(0, 2, 1, 3, 4)
            t = jnp.pad(t, ((0, 0), (0, 0), (0, Lp - L), (0, 0), (0, 0)))
            return t.reshape(B, dil, nb, band, H, Dh)

        def with_prev(t):
            prev = jnp.concatenate([jnp.zeros_like(t[:, :, :1]), t[:, :, :-1]], axis=2)
            return jnp.concatenate([prev, t], axis=3)

        qr = residues(q)
        kk = with_prev(residues(k))
        vv = with_prev(residues(v))
        s = jnp.einsum('brnqhd,brnkhd->brnhqk', qr, kk).astype(jnp.float32) * scale
        qi = jnp.arange(band)[:, None]
        ki = jnp.arange(2 * band)[None, :]
        rel = band + qi - ki
        valid = ((rel >= 0) & (rel <= band))[None] & ((jnp.arange(nb)[:, None, None] > 0) | (ki >= band)[None])
        s = jnp.where(valid[:, None], s, -jnp.inf)
        m = jnp.max(s, axis=-1)
        p = jnp.exp(s - m[..., None])
        den = jnp.sum(p, axis=-1)
        num = jnp.einsum('brnhqk,brnkhd->brnqhd', p, vv.astype(jnp.float32))

        def back(t):
            t = t.reshape((B, dil, Lp) + t.shape[4:])[:, :, :L]
            t = jnp.moveaxis(t, 1, 2)
            return t.reshape((B, S) + t.shape[3:])

        parts.append((back(jnp.moveaxis(m, 3, 4)), back(jnp.moveaxis(den, 3, 4)), back(num)))
    return combine_dilations(parts)

def dilated_attention_sample(q, k, v, kbuf, vbuf):
    B, T, H, Dh = q.shape
    buf = kbuf.shape[1]
    scale = Dh ** -0.5
    kc = jnp.concatenate([kbuf.astype(k.dtype), k], axis=1)
    vc = jnp.concatenate([vbuf.astype(v.dtype), v], axis=1)
    parts = []
    for window, dil in DILATED_GROUPS:
        band = window // dil
        idx = buf + jnp.arange(T)[:, None] - dil * jnp.arange(band + 1)[None, :]
        valid = idx >= 0
        idx = jnp.maximum(idx, 0)
        kg = kc[:, idx]
        vg = vc[:, idx]
        s = jnp.einsum('bthd,btkhd->bthk', q, kg).astype(jnp.float32) * scale
        s = jnp.where(valid[None, :, None, :], s, -jnp.inf)
        m = jnp.max(s, axis=-1)
        p = jnp.exp(s - m[..., None])
        parts.append((m, jnp.sum(p, axis=-1), jnp.einsum('bthk,btkhd->bthd', p, vg.astype(jnp.float32))))
    return combine_dilations(parts), kc[:, T:], vc[:, T:]

def token_mixers(h, pos, s_gla0, s_hgrn0, kbuf, vbuf, w_in, gla_w_gate_up, gla_b_gate, gla_norm_g,
                 lower_bound, hgrn_norm_g, q_norm_g, k_norm_g):
    B, L, _ = h.shape
    f32 = jnp.float32
    proj = h @ w_in
    offsets = [int(o) for o in np.cumsum(IN_SPLITS)[:-1]]
    (a_q, a_k, a_v, a_lr, a_g, b_q, b_f, b_i, b_g, c_q, c_k, c_v) = jnp.split(proj, offsets, axis=-1)

    def heads(t, n):
        return t.reshape(B, L, n, -1)

    chunk = CHUNK if L % CHUNK == 0 else L

    log_alpha = jax.nn.log_sigmoid((a_lr @ gla_w_gate_up + gla_b_gate).astype(f32)) / GLA_TAU
    o_a, s_gla = gated_linear_chunked(heads(a_q, GLA_HEADS).astype(f32) * GLA_DK ** -0.5,
                                      heads(a_k, GLA_HEADS), heads(a_v, GLA_HEADS),
                                      heads(log_alpha, GLA_HEADS), s_gla0, chunk)
    o_a = rmsnorm(o_a, gla_norm_g) * jax.nn.silu(heads(a_g, GLA_HEADS).astype(f32))

    lb = lower_bound.astype(f32)
    z = b_f.astype(f32)
    log_f = jnp.log(lb + (1.0 - lb) * jax.nn.sigmoid(z))
    key = (1.0 - lb) * jax.nn.sigmoid(-z)
    o_b, s_hgrn = gated_linear_chunked(heads(jax.nn.silu(b_q.astype(f32)), HGRN_HEADS),
                                       heads(key, HGRN_HEADS), heads(b_i, HGRN_HEADS),
                                       heads(log_f, HGRN_HEADS), s_hgrn0, chunk)
    o_b = rmsnorm(o_b, hgrn_norm_g) * jax.nn.silu(heads(b_g, HGRN_HEADS).astype(f32))

    q = rope_partial(rmsnorm(heads(c_q, ATT_HEADS), q_norm_g), pos)
    k = rope_partial(rmsnorm(heads(c_k, ATT_HEADS), k_norm_g), pos)
    v = heads(c_v, ATT_HEADS)
    if kbuf is None:
        o_c = dilated_attention_prompt(q, k, v)
        keep = min(WINDOW_MAX, L)
        k_new, v_new = k[:, L - keep:], v[:, L - keep:]
    else:
        o_c, k_new, v_new = dilated_attention_sample(q, k, v, kbuf, vbuf)

    mixed = jnp.concatenate([o_a.reshape(B, L, -1), o_b.reshape(B, L, -1), o_c.reshape(B, L, -1)],
                            axis=-1).astype(h.dtype)
    return mixed, s_gla.astype(s_gla0.dtype), s_hgrn.astype(s_hgrn0.dtype), k_new, v_new

def swiglu(h, w_gate, w_up, w_down):
    return (jax.nn.silu(h @ w_gate) * (h @ w_up)) @ w_down

def moe_swiglu(h, w_router, w_gate, w_up, w_down):
    logits = (h @ w_router).astype(jnp.float32)
    top_v, top_i = lax.top_k(logits, TOP_K)
    gates = jax.nn.softmax(top_v, axis=-1)
    combine_w = jnp.sum(jax.nn.one_hot(top_i, N_EXPERTS, dtype=jnp.float32) * gates[..., None], axis=-2)
    out = jnp.zeros(h.shape, jnp.float32)
    for e in range(N_EXPERTS):
        out = out + combine_w[..., e:e + 1] * swiglu(h, w_gate[e], w_up[e], w_down[e]).astype(jnp.float32)
    return out.astype(h.dtype)

def setup_inputs(seed: int = 0) -> dict:
    key = jax.random.key(seed)
    ks = jax.random.split(key, 24)
    buf = min(WINDOW_MAX, PAST_LEN)

    def nrm(k, shape, scale):
        return jax.random.normal(k, shape, jnp.float32) * scale

    return {
        'x_prompt': nrm(ks[0], (BATCH, SEQ, D_MODEL), 1.0),
        'x_sample': nrm(ks[1], (DEC_BATCH, DEC_SEQ, D_MODEL), 1.0),
        'state_gla': nrm(ks[2], (DEPTH, DEC_BATCH, GLA_HEADS, GLA_DK, GLA_DV), 0.5),
        'state_hgrn': nrm(ks[3], (DEPTH, DEC_BATCH, HGRN_HEADS, HGRN_DK, HGRN_DV), 0.5),
        'cache_k_win': nrm(ks[4], (DEPTH, DEC_BATCH, buf, ATT_HEADS, HEAD_DIM), 1.0),
        'cache_v_win': nrm(ks[5], (DEPTH, DEC_BATCH, buf, ATT_HEADS, HEAD_DIM), 1.0),
        'norm_mix_g': 1.0 + nrm(ks[6], (DEPTH, D_MODEL), 0.02),
        'w_in': nrm(ks[7], (DEPTH, D_MODEL, N_IN), D_MODEL ** -0.5),
        'gla_w_gate_up': nrm(ks[8], (DEPTH, GLA_RANK, GLA_HEADS * GLA_DK), GLA_RANK ** -0.5),
        'gla_b_gate': nrm(ks[9], (DEPTH, GLA_HEADS * GLA_DK), 0.1),
        'gla_norm_g': 1.0 + nrm(ks[10], (DEPTH, GLA_DV), 0.02),
        'hgrn_lb_logits': nrm(ks[11], (DEPTH, HGRN_HEADS * HGRN_DK), 0.5),
        'hgrn_norm_g': 1.0 + nrm(ks[12], (DEPTH, HGRN_DV), 0.02),
        'attn_q_norm_g': 1.0 + nrm(ks[13], (DEPTH, HEAD_DIM), 0.02),
        'attn_k_norm_g': 1.0 + nrm(ks[14], (DEPTH, HEAD_DIM), 0.02),
        'w_out': nrm(ks[15], (DEPTH, MIX_WIDTH, D_MODEL), MIX_WIDTH ** -0.5),
        'norm_ffn_g': 1.0 + nrm(ks[16], (DEPTH, D_MODEL), 0.02),
        'ffn_w_gate': nrm(ks[17], (N_DENSE, D_MODEL, D_FF), D_MODEL ** -0.5),
        'ffn_w_up': nrm(ks[18], (N_DENSE, D_MODEL, D_FF), D_MODEL ** -0.5),
        'ffn_w_down': nrm(ks[19], (N_DENSE, D_FF, D_MODEL), D_FF ** -0.5),
        'moe_w_router': nrm(ks[20], (N_MOE, D_MODEL, N_EXPERTS), D_MODEL ** -0.5),
        'moe_w_gate': nrm(ks[21], (N_MOE, N_EXPERTS, D_MODEL, D_FF_EXPERT), D_MODEL ** -0.5),
        'moe_w_up': nrm(ks[22], (N_MOE, N_EXPERTS, D_MODEL, D_FF_EXPERT), D_MODEL ** -0.5),
        'moe_w_down': nrm(ks[23], (N_MOE, N_EXPERTS, D_FF_EXPERT, D_MODEL), D_FF_EXPERT ** -0.5),
    }

def reference(x_prompt, x_sample, state_gla, state_hgrn, cache_k_win, cache_v_win, norm_mix_g, w_in,
              gla_w_gate_up, gla_b_gate, gla_norm_g, hgrn_lb_logits, hgrn_norm_g, attn_q_norm_g,
              attn_k_norm_g, w_out, norm_ffn_g, ffn_w_gate, ffn_w_up, ffn_w_down, moe_w_router,
              moe_w_gate, moe_w_up, moe_w_down):
    lb_w = jax.nn.softmax(hgrn_lb_logits.astype(jnp.float32), axis=0)
    lower_bounds = jnp.cumsum(lb_w, axis=0) - lb_w[0]

    b_p, l_p = x_prompt.shape[0], x_prompt.shape[1]
    pos_p = jnp.arange(l_p, dtype=jnp.int32)
    pos_s = PAST_LEN + jnp.arange(x_sample.shape[1], dtype=jnp.int32)
    zero_gla = jnp.zeros((b_p, GLA_HEADS, GLA_DK, GLA_DV), x_prompt.dtype)
    zero_hgrn = jnp.zeros((b_p, HGRN_HEADS, HGRN_DK, HGRN_DV), x_prompt.dtype)

    xp, xs = x_prompt, x_sample
    gla_p, hgrn_p, kw_p, vw_p = [], [], [], []
    gla_s, hgrn_s, kw_s, vw_s = [], [], [], []
    for layer in range(DEPTH):
        mix_w = (w_in[layer], gla_w_gate_up[layer], gla_b_gate[layer], gla_norm_g[layer],
                 lower_bounds[layer], hgrn_norm_g[layer], attn_q_norm_g[layer], attn_k_norm_g[layer])
        mixed, sg, sh, kw, vw = token_mixers(rmsnorm(xp, norm_mix_g[layer]), pos_p, zero_gla, zero_hgrn,
                                             None, None, *mix_w)
        xp = xp + mixed @ w_out[layer]
        gla_p.append(sg)
        hgrn_p.append(sh)
        kw_p.append(kw)
        vw_p.append(vw)
        mixed, sg, sh, kw, vw = token_mixers(rmsnorm(xs, norm_mix_g[layer]), pos_s, state_gla[layer],
                                             state_hgrn[layer], cache_k_win[layer], cache_v_win[layer], *mix_w)
        xs = xs + mixed @ w_out[layer]
        gla_s.append(sg)
        hgrn_s.append(sh)
        kw_s.append(kw)
        vw_s.append(vw)
        j = layer // 2
        if layer % 2 == 0:
            xp = xp + swiglu(rmsnorm(xp, norm_ffn_g[layer]), ffn_w_gate[j], ffn_w_up[j], ffn_w_down[j])
            xs = xs + swiglu(rmsnorm(xs, norm_ffn_g[layer]), ffn_w_gate[j], ffn_w_up[j], ffn_w_down[j])
        else:
            xp = xp + moe_swiglu(rmsnorm(xp, norm_ffn_g[layer]), moe_w_router[j], moe_w_gate[j], moe_w_up[j], moe_w_down[j])
            xs = xs + moe_swiglu(rmsnorm(xs, norm_ffn_g[layer]), moe_w_router[j], moe_w_gate[j], moe_w_up[j], moe_w_down[j])

    return (xp, xs, jnp.stack(gla_p), jnp.stack(hgrn_p), jnp.stack(kw_p), jnp.stack(vw_p),
            jnp.stack(gla_s), jnp.stack(hgrn_s), jnp.stack(kw_s), jnp.stack(vw_s))


_drawn_inputs = setup_inputs


def setup_inputs(seed=0):
    import zlib

    import numpy as np

    out = dict(_drawn_inputs(seed))
    spreads = {}
    factors = {'hgrn_norm_g': 2.97, 'attn_q_norm_g': 3.314, 'attn_k_norm_g': 2.849}
    for name, (base, spread) in spreads.items():
        noise = np.random.default_rng([zlib.crc32(name.encode()), seed]).standard_normal(out[name].shape)
        drawn = base * np.exp(spread * noise) if base else spread * noise
        out[name] = jnp.asarray(drawn.astype(out[name].dtype))
    for name, factor in factors.items():
        out[name] = (out[name] * factor).astype(out[name].dtype)
    return out
```

```python
from contextlib import ExitStack

import numpy as np
import concourse.bass as bass
from concourse import mybir

F32 = mybir.dt.float32
ALU = mybir.AluOpType
ACT = mybir.ActivationFunctionType
AX = mybir.AxisListType

P = 128
D_MODEL, SEQ, DEPTH, NB, DEC, PAST = 1024, 512, 2, 8, 8, 1024
NS = NB * DEC
T = SEQ + NS
HALF = T // 2
KC = D_MODEL // P
TT = SEQ // P
EPS = 1e-6
HEADS_A = HEADS_B = 4
DK_A, DK_B, DV, DH = 32, 64, 64, 64
AH = 8
GROUPS = ((128, 1), (512, 4), (2048, 16))
RANK = 16
FE = 11
EXPERTS = (2, 8)
BLK = 16
NBLK = P // BLK
R = 6
SLOT = FE * P

JOBS = [("lr", 0), ("bf", 0), ("bf", 1), ("aq", 0), ("gu", 0), ("ak", 0), ("bq", 0), ("bq", 1),
        ("g", 0), ("g", 1), ("g", 2), ("g", 3)]
for _i in range(8 + 2):
    if _i < 8:
        JOBS.append(("c", _i))
    if 0 <= _i - 1 < 8:
        JOBS.append(("s", _i - 1))
    if 0 <= _i - 2:
        JOBS.append(("r", _i - 2))
NJ = len(JOBS)
JOB_AT = {j: n for n, j in enumerate(JOBS)}
HAS_W = [k not in ("gu", "s", "r") for k, _ in JOBS]
HAS_ACT = [k in ("bf", "bq", "g", "c", "s") for k, _ in JOBS]
HAS_DVE = [k != "c" for k, _ in JOBS]
ACT_N = np.cumsum(HAS_ACT).tolist()
DVE_N = np.cumsum(HAS_DVE).tolist()
NFEAT = sum(HAS_W)
NV = 8
U_IN = NV + NFEAT
U_OUT = KC
U_EXP = 2 * FE + KC
RING0 = [0, U_IN + U_OUT + EXPERTS[0] * U_EXP]
NVU = NV - 2
UD0 = [0, NVU + U_OUT + EXPERTS[0] * U_EXP]
PF0 = [0, U_OUT + EXPERTS[0] * U_EXP]

ITEMS = ([("eb", 0), ("kd", 0), ("qt", 0)] + [("kt", i) for i in range(1, NBLK)]
         + [("pj", j) for j in range(BLK)] + [("sj", j) for j in range(DEC)])
NI = len(ITEMS)
ITEM_AT = {x: n for n, x in enumerate(ITEMS)}
CT = 3
CT_HEADS = (4, 2, 2)

CONSTS = [("lnc", SEQ), ("smask", PAST), ("smask_new", NB * NS), ("cos", T), ("sin", T), ("w16", P + BLK),
          ("w8", NS + DEC), ("mask16", P), ("mask8", NS), ("ident", P), ("ones", P), ("bones", P),
          ("rot", P), ("reset", T), ("maskb", NB), ("riota", 8)]
COFF, _o = {}, 0
for _n, _w in CONSTS:
    COFF[_n] = (_o, _w)
    _o += _w
NCONST = _o
VECS = [("g_mix", KC), ("g_ffn", KC), ("b_gate", 1), ("g_gla", 1), ("g_hgrn", 1), ("g_q", 1), ("g_k", 1)]
VOFF, _o = {}, 0
for _n, _w in VECS:
    VOFF[_n] = (_o, _w)
    _o += _w
NVEC = _o


def multiplicity(dist):
    n = np.zeros(dist.shape, np.float64)
    for window, dil in GROUPS:
        n += (dist >= 0) & (dist <= window) & (dist % dil == 0)
    return n


def log_mult(dist, valid):
    n = np.where(valid, multiplicity(dist), 0)
    return np.where(n > 0, np.log(np.maximum(n, 1)), -1e30).astype(np.float32)


def shape_constants():
    c = {}
    p = np.arange(P)[:, None]
    u = np.arange(SEQ)[None, :]
    c["lnc"] = log_mult(SEQ - P + p - u, SEQ - P + p - u >= 0)
    row = p % 32
    t = row % DEC
    live = row < 2 * DEC
    d = PAST + t - np.arange(PAST)[None, :]
    c["smask"] = np.where(live, log_mult(d, d >= 0), 0).astype(np.float32)
    key = np.arange(NS)[None, :]
    new = []
    for b in range(NB):
        d = t - key % DEC
        new.append(np.where(live, log_mult(d, (d >= 0) & (key // DEC == b)), 0).astype(np.float32))
    c["smask_new"] = np.concatenate(new, 1)
    pos = np.concatenate([np.arange(SEQ), np.tile(PAST + np.arange(DEC), NB)]).astype(np.float32)
    rot_dim = DH // 4
    inv = (np.float32(500000.0) ** (-np.arange(0, rot_dim, 2, dtype=np.float32) / np.float32(rot_dim))).astype(np.float32)
    ang = pos[:, None] * inv[None, :]
    cos, sin = np.ones((P, T), np.float32), np.zeros((P, T), np.float32)
    rot = np.zeros((P, P), np.float32)
    for h in range(2):
        for i in range(rot_dim // 2):
            a, b = h * DH + i, h * DH + rot_dim // 2 + i
            cos[a] = cos[b] = np.cos(ang[:, i])
            sin[a] = sin[b] = np.sin(ang[:, i])
            rot[b, a] = -1.0
            rot[a, b] = 1.0
    c["cos"], c["sin"], c["rot"] = cos, sin, rot
    c["w16"] = np.broadcast_to(np.arange(P + BLK)[None] % BLK == 0, (P, P + BLK)).astype(np.float32)
    c["w8"] = np.broadcast_to(np.arange(NS + DEC)[None] % DEC == 0, (P, NS + DEC)).astype(np.float32)
    q = np.arange(P)[None, :]
    c["mask16"] = ((p // BLK == q // BLK) & (q >= p)).astype(np.float32)
    q = np.arange(NS)[None, :]
    c["mask8"] = ((p // DEC == q // DEC) & (q >= p)).astype(np.float32)
    c["ident"] = np.eye(P, dtype=np.float32)
    c["ones"] = np.ones((P, P), np.float32)
    c["bones"] = (p // DH == np.arange(P)[None] // DH).astype(np.float32)
    reset = np.ones(T, np.float32)
    reset[0:SEQ:P] = 0
    reset[SEQ::DEC] = 0
    c["reset"] = np.broadcast_to(reset[None], (P, T))
    c["maskb"] = (p // DEC == np.arange(NB)[None]).astype(np.float32)
    c["riota"] = np.broadcast_to(8.0 - np.arange(8)[None], (P, 8))
    return np.ascontiguousarray(np.concatenate([c[n].astype(np.float32) for n, _ in CONSTS], 1))


def build(nc, d):
    ctx = ExitStack()
    with ctx:
        def sb(name, cols):
            return ctx.enter_context(nc.sbuf_tensor(name, [P, cols], F32))

        def sem(name):
            return ctx.enter_context(nc.semaphore(name))

        def tiles(ap, n):
            return ap.rearrange("p (n t) -> p n t", n=n)

        X = tiles(sb("residual", KC * T), KC)
        H = tiles(sb("normed_or_mixed", KC * T), KC)
        mix = H
        QK = tiles(sb("attn_qk", 8 * T), 8)
        V = tiles(sb("values", (TT + 1) * D_MODEL), TT + 1)
        LIN = sb("linear", 13 * T)
        Q, K, B = (tiles(LIN[:, i * 3 * T:(i + 1) * 3 * T], 3) for i in range(3))
        G = tiles(LIN[:, 9 * T:13 * T], 4)
        ring = tiles(sb("weight_ring", R * SLOT), R)
        C = sb("constants", NCONST)
        const = {n: C[:, o:o + w] for n, (o, w) in COFF.items()}
        VEC = sb("vectors", DEPTH * NVEC)
        LB = sb("lower_bounds", 32)
        WU = sb("gla_gate_up", DEPTH * P)
        SM = sb("small", 320)
        WRT = sb("router", 64)
        SCR = sb("scratch", 12736)

        def vec(L, name):
            o, w = VOFF[name]
            return VEC[:, L * NVEC + o:L * NVEC + o + w]

        def carve(base, *sizes):
            out, o = [], 0
            for s in sizes:
                out.append(base[:, o:o + s])
                o += s
            return out

        eps_col = SM[:, 32:33]
        negmax = SM[:, 40:48]
        den = SM[:, 48:56]
        rden = SM[:, 56:64]
        ebl = tiles(SM[:, 64:64 + CT * 12], CT)
        rt = SM[:, 128:320]
        lb = LB[:, 0:4]
        oml = LB[:, 4:8]
        e0, e1s, rinvs, qn = (tiles(x, 3) for x in carve(SCR, 3 * T, 3 * T, 3 * T, 3 * T))
        rtmp = SCR[:, 12 * T:13 * T]
        lr_sb = SCR[0:RANK, 13 * T:14 * T]
        sq = tiles(SCR[:, FE * T:(FE + 4) * T], 4)
        rinv = SCR[:, 4 * T:5 * T]
        (qe_, kdt_, kt_, qt, dring_, a_, kd, vbd, pring_) = carve(
            SCR, CT * T, (TT + 1) * P, (NBLK - 1) * SEQ, SEQ, 3 * T, 4 * T, T, 512, 2 * T)
        Qe = tiles(qe_, CT)
        KdT = tiles(kdt_, TT + 1)
        Kt = kt_.rearrange("p (i c s) -> p i c s", i=NBLK - 1, c=TT)
        Dr = tiles(dring_, 3)
        A = tiles(a_, 4)
        Pr = tiles(pring_, 2)
        osq, orinv = Pr[:, 0, :], Pr[:, 1, :]
        S = H[:, 4:8, :].rearrange("p a t -> p (a t)")[:, 0:CT * 4 * DV].rearrange("p (c k v) -> p c k v", c=CT, k=4)
        S0 = H[:, 4:8, :].rearrange("p a t -> p (a t)")[:, 768:768 + CT * NB * DV].rearrange(
            "p (c b v) -> p c b v", c=CT, b=NB)
        (p_, pt_, vc_) = carve(SCR, 2 * (PAST + NS), 2 * 9 * P, 4096)
        Pp = tiles(p_[:, 0:2048], 4)
        Ps = tiles(p_, 2)
        PTp = tiles(pt_[:, 0:1024], 2)
        PTs = tiles(pt_, 2)
        Vc = tiles(vc_, 8)
        Kc = tiles(LIN[:, 0:4096], 4)
        Qs = LIN[:, 4096:5120].rearrange("p (b h q) -> p b h q", b=NB, h=4)
        hid_, ft_ = carve(SCR, FE * T, 4 * T)
        hid, ft = tiles(hid_, FE), tiles(ft_, 4)
        cw = LIN[:, 0:8 * T].rearrange("p (e t) -> p e t", e=8)
        sqf = ft

        ps = ctx.enter_context(nc.psum_tensor("ps", [P, 8, 512], F32))

        def pair(k):
            return ps[:, 2 * k:2 * k + 2, 0:HALF]

        def split(ap):
            return ap.rearrange("p (a t) -> p a t", a=2)

        x_in, c_in, w_land = sem("x_in"), sem("consts_in"), [sem(f"weights_in{i}") for i in range(R)]
        s0_in = [sem("gla_state_in"), sem("hgrn_state_in")]
        kc_in, vc_in = sem("kcache_in"), sem("vcache_in")
        stored_s, stored_kc, stored_vc, stored_y = sem("states_out"), sem("kcache_out"), sem("vcache_out"), sem("y_out")
        stored_kv = sem("new_kv_out")
        lb_exp, lb_ready, eps_ready, kt_zero, qs_zero = (sem(n) for n in (
            "lb_exp", "lb_ready", "eps_ready", "kt_zeroed", "qs_zeroed"))
        sq_ready, sq_used, rinv_ready, h_ready = (sem(n) for n in ("sq_ready", "sq_used", "rinv_ready", "h_ready"))
        v_ready, v_half = sem("v_ready"), sem("v_product")
        unit_done, pe_job, act_job, dve_job = (sem(n) for n in ("unit_done", "pe_job", "act_job", "dve_job"))
        out_evac = sem("out_evac")
        dch, ach = sem("dve_chain"), sem("act_chain")
        lf_abs, lf_ready, b_ready = sem("lf_abs"), sem("logf_ready"), sem("b_ready")
        diff_ready, exp_ready, term_ready = sem("diff_ready"), sem("exp_ready"), sem("term_ready")
        prod_used, off_done, diag_done, samp_done = (sem(n) for n in ("prod_used", "off_done", "diag_done", "samp_done"))
        kdt_ps, kdt_ready, a_ready, as_ready = (sem(n) for n in ("kdt_ps", "kdt_ready", "a_ready", "as_ready"))
        upd_done, s_ready, vbd_ready, vbd_used, supd_done, sn_ready = (sem(n) for n in (
            "upd_done", "s_ready", "vbd_ready", "vbd_used", "supd_done", "sn_ready"))
        o_done, osq_ready, oss_done, orinv_ready, mixl_ready = (sem(n) for n in (
            "o_done", "osq_ready", "oss_done", "orinv_ready", "mixl_ready"))
        sc_done, sc_free, mx_ready, p_ready, pn_ready, pt_ps, pt_ready, pv_done, mixc_ready = (sem(n) for n in (
            "sc_done", "sc_free", "mx_ready", "p_ready", "pn_ready", "pt_ps", "pt_ready", "pv_done", "mixc_ready"))
        qs_ready = sem("qs_ready")
        ssc_done, ssc_free, smx_ready, sp_ready, spn_ready, spt_ps, spt_ready, spv_done, smix_ready = (sem(n) for n in (
            "ssc_done", "ssc_free", "smx_ready", "sp_ready", "spn_ready", "spt_ps", "spt_ready", "spv_done", "smix_ready"))
        sig_ready = sem("sig_ready")
        rl_done, rexp, rexp_done, cw_tok, cwb_done, cw_ready = (sem(n) for n in (
            "router_done", "rexp", "rexp_done", "cw_tok", "cwb_done", "cw_ready"))

        N_CI = 6
        block = ctx.enter_context(nc.Block())

        def ud_ffn(L):
            return UD0[L] + NVU + U_OUT

        def pf_ffn(L):
            return PF0[L] + U_OUT

        released = []
        for L in range(DEPTH):
            for half in range(2):
                released += [(unit_done, UD0[L] + 3 * half + u + 1) for u in range(3)] + [(v_half, 10 * L + 5 * half + 5)]
            released += [(pe_job, L * NJ + n + 1) for n in range(NJ) if HAS_W[n]]
            released += [(unit_done, UD0[L] + NVU + u + 1) for u in range(U_OUT + EXPERTS[L] * U_EXP)]
            assert len(released) == (RING0 + [RING0[1] + U_IN + U_OUT + 8 * U_EXP])[L + 1]

        def chunk_rows(h, n):
            w = P // n
            return slice(h * w, h * w + w)

        @block.sync
        def _(sp):
            sp.dma_start(X[:, :, :], d["x"]).then_inc(x_in, 16)
            for dst, src in ((C[:, :], d["consts"]), (VEC[:, :], d["vecs"]), (LB[:, 16:20], d["lb_logits"]),
                             (WU[0:RANK, :], d["w_up"]), (WRT[:, :], d["w_router"])):
                sp.dma_start(dst, src).then_inc(c_in, 16)

            def slot_for(n):
                if n >= R:
                    s, v = released[n - R]
                    sp.wait_ge(s, v)
                return n % R

            for L in range(DEPTH):
                n = RING0[L]
                for u in range(NV):
                    s = slot_for(n)
                    sp.dma_start(ring[:, s, 0:1024], d["w_v"][L, u]).then_inc(w_land[s], 16)
                    n += 1
                f = 0
                for kind, i in JOBS:
                    if kind in ("gu", "s", "r"):
                        continue
                    s = slot_for(n)
                    if kind == "lr":
                        sp.dma_start(ring[:, s, 0:KC * RANK], d["w_lr"][L]).then_inc(w_land[s], 16)
                    else:
                        sp.dma_start(ring[:, s, 0:1024], d["w_feat"][L, f]).then_inc(w_land[s], 16)
                        f += 1
                    n += 1
                for u in range(U_OUT):
                    s = slot_for(n)
                    sp.dma_start(ring[:, s, 0:1024], d["w_out"][L, u]).then_inc(w_land[s], 16)
                    n += 1
                    if u == R - 1:
                        for b in range(NB):
                            if b == 0:
                                sp.wait_ge(mixl_ready, 4 * (L + 1))
                                sp.wait_ge(a_ready, 8 * (L + 1))
                            else:
                                sp.wait_ge(ssc_done, L * NB + b)
                                sp.wait_ge(stored_kc, 16 * (L * NB + b))
                            sp.dma_start(Kc[:, :, :], d["kcache"][L, b]).then_inc(kc_in, 16)
                            if b:
                                sp.wait_ge(spv_done, L * NB + b)
                                sp.wait_ge(stored_vc, 16 * (L * NB + b))
                            sp.dma_start(Vc[:, :, :], d["vcache"][L, b]).then_inc(vc_in, 16)
                base_ud, base_ring, e0_ = ud_ffn(L), n, sum(EXPERTS[:L])
                with sp.Fori(0, EXPERTS[L]) as e:
                    for j in range(U_EXP):
                        s = (base_ring + j) % R
                        sp.wait_ge(unit_done, e * U_EXP + (base_ud + j - R + 1))
                        if j < 2 * FE:
                            src = d["w_gu"][bass.ds(e * (2 * FE) + (e0_ * 2 * FE + j), 1)].rearrange("o p c -> (o p) c")
                            sp.dma_start(ring[:, s, 0:1024], src).then_inc(w_land[s], 16)
                        else:
                            src = d["w_dn"][bass.ds(e * KC + (e0_ * KC + j - 2 * FE), 1)].rearrange("o p c -> (o p) c")
                            sp.dma_start(ring[:, s, :], src).then_inc(w_land[s], 16)
            sp.wait_ge(out_evac, pf_ffn(1) + 8 * U_EXP)
            sp.dma_start(d["y"], X[:, :, :]).then_inc(stored_y, 16)
            sp.wait_ge(stored_y, 16)

        @block.gpsimd
        def _(pool):
            pool.wait_ge(c_in, 16 * 5)
            for L in range(DEPTH):
                pool.wait_ge(pe_job, (L + 1) * NJ)
                pool.dma_start(S0[:, 0, :, :], d["s0_gla"][L]).then_inc(s0_in[0], 16)
                pool.dma_start(S0[:, 1:3, :, :], d["s0_hgrn"][L]).then_inc(s0_in[1], 16)
                pool.wait_ge(dve_job, (L + 1) * DVE_N[-1])
                pool.wait_ge(v_ready, 10 * (L + 1))
                pool.dma_start(d["ok_p"][L], QK[:, 4:8, 0:SEQ]).then_inc(stored_kv, 16)
                pool.dma_start(d["ov_p"][L], V[:, 0:TT, 512:1024]).then_inc(stored_kv, 16)
                pool.wait_ge(dve_job, (L + 1) * DVE_N[-1])
                nc.gpsimd.memset(kt_, 0.0).then_inc(kt_zero, 1)
                for ct in range(CT):
                    pool.wait_ge(b_ready, L * CT + ct + 1)
                    Bp = B[:, ct, 0:SEQ].rearrange("p (c s) -> p c s", c=TT)
                    Bs = B[:, ct, SEQ:T].rearrange("p (b s) -> p b s", b=NB)
                    Bb = B[:, ct, 0:SEQ].rearrange("p (n s) -> p n s", s=BLK)
                    for kind, i in ITEMS:
                        it = L * CT * NI + ct * NI + ITEM_AT[(kind, i)]
                        if kind == "eb":
                            continue
                        D = Dr[:, it % 3, :]
                        if it >= 3:
                            pool.wait_ge(term_ready, it - 2)
                        if kind == "kd" and ct == 0:
                            pool.wait_ge(b_ready, L * CT + CT)
                        Dp = D[:, 0:SEQ].rearrange("p (c s) -> p c s", c=TT)
                        Ds = D[:, SEQ:T].rearrange("p (b s) -> p b s", b=NB)
                        if kind == "kd":
                            nc.gpsimd.tensor_tensor(Dp, Bp[:, :, P - 1:P].to_broadcast([P, TT, P]), Bp, ALU.subtract)
                            op = nc.gpsimd.tensor_tensor(Ds, Bs[:, :, DEC - 1:DEC].to_broadcast([P, NB, DEC]), Bs, ALU.subtract)
                        elif kind == "qt":
                            for c in range(TT):
                                b1 = Bp[:, c, BLK:P].rearrange("p (n s) -> p n s", s=BLK)
                                r1 = Bp[:, c, 0:P - BLK].rearrange("p (n s) -> p n s", s=BLK)[:, :, BLK - 1:BLK]
                                op = nc.gpsimd.tensor_tensor(
                                    Dp[:, c, BLK:P].rearrange("p (n s) -> p n s", s=BLK), b1,
                                    r1.to_broadcast([P, NBLK - 1, BLK]), ALU.subtract)
                        elif kind == "kt":
                            w = BLK * i
                            op = nc.gpsimd.tensor_tensor(Dp[:, :, 0:w], Bp[:, :, w - 1:w].to_broadcast([P, TT, w]),
                                                         Bp[:, :, 0:w], ALU.subtract)
                        elif kind == "pj":
                            w = BLK - i
                            op = nc.gpsimd.tensor_tensor(
                                D[:, 0:32 * w].rearrange("p (n s) -> p n s", s=w), Bb[:, :, i:BLK],
                                Bb[:, :, i:i + 1].to_broadcast([P, SEQ // BLK, w]), ALU.subtract)
                        else:
                            w = DEC - i
                            op = nc.gpsimd.tensor_tensor(
                                D[:, 0:NB * w].rearrange("p (n s) -> p n s", s=w), Bs[:, :, i:DEC],
                                Bs[:, :, i:i + 1].to_broadcast([P, NB, w]), ALU.subtract)
                        op.then_inc(diff_ready, 1)
                    for h in range(CT_HEADS[ct]):
                        hh = (0, 4, 6)[ct] + h
                        if L * 8 + hh >= 1:
                            pool.wait_ge(vbd_used, L * 8 + hh)
                        v = V[0:NS, TT, hh * DV:hh * DV + DV].rearrange("p (o v) -> p o v", o=1)
                        nc.gpsimd.tensor_tensor(
                            vbd[0:NS, :].rearrange("p (b v) -> p b v", b=NB), v.to_broadcast([NS, NB, DV]),
                            const["maskb"][0:NS, :].rearrange("p (b o) -> p b o", o=1).to_broadcast([NS, NB, DV]),
                            ALU.mult).then_inc(vbd_ready, 1)
                pool.wait_ge(s_ready, CT * (L + 1))
                pool.dma_start(d["os_gla_p"][L], S[:, 0, 3, :]).then_inc(stored_s, 16)
                pool.dma_start(d["os_hgrn_p"][L], S[:, 1:3, 3, :]).then_inc(stored_s, 16)
                pool.wait_ge(sn_ready, CT * (L + 1))
                pool.dma_start(d["os_gla_s"][L], S0[:, 0, :, :]).then_inc(stored_s, 16)
                pool.dma_start(d["os_hgrn_s"][L], S0[:, 1:3, :, :]).then_inc(stored_s, 16)
                for b in range(NB):
                    pool.wait_ge(kc_in, 16 * (L * NB + b + 1))
                    pool.dma_start(d["ok_s"][L, b][:, :, 0:PAST - DEC], Kc[:, :, DEC:PAST]).then_inc(stored_kc, 16)
                    pool.wait_ge(vc_in, 16 * (L * NB + b + 1))
                    pool.dma_start(d["ov_s"][L, b][0:P - 1], Vc[1:P, :, :]).then_inc(stored_vc, 16)
                    s = SEQ + DEC * b
                    pool.dma_start(d["ok_s"][L, b][:, :, PAST - DEC:PAST], QK[:, 4:8, s:s + DEC]).then_inc(stored_kv, 16)
                    pool.dma_start(d["ov_s"][L, b][P - 1], V[DEC * b:DEC * b + DEC, TT, 512:1024]).then_inc(stored_kv, 16)
                pool.wait_ge(stored_kv, (L + 1) * 16 * (2 + 2 * NB))
                pool.wait_ge(stored_s, (L + 1) * 64)
                pool.wait_ge(stored_kc, (L + 1) * 16 * NB)
                pool.wait_ge(stored_vc, (L + 1) * 16 * NB)

        @block.scalar
        def _(act):
            chain = [0]

            def link(op):
                op.then_inc(ach, 1)
                chain[0] += 1
                act.wait_ge(ach, chain[0])

            def norm(k, buf, out, wait_x):
                for c in range(KC):
                    wait_x(c)
                    if c >= 4:
                        act.wait_ge(sq_used, KC * k + c - 3)
                    nc.scalar.activation(buf[:, c % 4, :], X[:, c, :], ACT.Square).then_inc(sq_ready, 1)
                act.wait_ge(sq_used, KC * k + KC)
                link(nc.scalar.activation(split(out), pair(0), ACT.Ln, bias=eps_col, scale=1.0 / D_MODEL))
                nc.scalar.activation(out, out, ACT.Exp, scale=-0.5).then_inc(rinv_ready, 1)

            act.wait_ge(c_in, 16 * 5)
            act.wait_ge(lb_ready, 1)
            nc.scalar.activation(LB[:, 20:24], LB[:, 24:28], ACT.Exp).then_inc(lb_exp, 1)
            act.wait_ge(eps_ready, 1)
            for L in range(DEPTH):
                def wait_mix(c, L=L):
                    if L == 0:
                        act.wait_ge(x_in, 16)
                    else:
                        act.wait_ge(out_evac, pf_ffn(0) + U_EXP + 2 * FE + c + 1)
                norm(2 * L, sq, rinv, wait_mix)
                for n in range(10):
                    act.wait_ge(v_half, 10 * L + n + 1)
                    half, tt = n // 5, n % 5
                    rows = P if tt < TT else NS
                    if L and n == 0:
                        act.wait_ge(stored_kv, 16 * (2 + 2 * NB))
                    nc.scalar.activation(V[0:rows, tt, half * 512:half * 512 + 512], ps[0:rows, n % 8, :],
                                         ACT.Copy).then_inc(v_ready, 1)
                for n, (kind, i) in enumerate(JOBS):
                    if not HAS_ACT[n]:
                        continue
                    act.wait_ge(pe_job, L * NJ + n + 1)
                    src = pair((n + 1) % 4)
                    if kind in ("bf", "bq", "g"):
                        act.wait_ge(dve_job, L * DVE_N[-1] + (DVE_N[n - 3] if n >= 3 else 0)) if n >= 3 else None
                        if kind == "bf":
                            nc.scalar.activation(split(e1s[:, n % 3, :]), src, ACT.Exp)
                        nc.scalar.activation(split(e0[:, n % 3, :]), src, ACT.Exp, scale=-1.0).then_inc(act_job, 1)
                    elif kind == "c":
                        if i < 3:
                            act.wait_ge(dve_job, L * DVE_N[-1] + DVE_N[JOB_AT[("g", 3)]])
                        else:
                            act.wait_ge(dve_job, L * DVE_N[-1] + DVE_N[JOB_AT[("s", i - 3)]])
                        nc.scalar.activation(split(e0[:, i % 3, :]), src, ACT.Copy)
                        nc.scalar.activation(split(e1s[:, i % 3, :]), src, ACT.Square).then_inc(act_job, 1)
                    else:
                        link(nc.scalar.activation(split(rinvs[:, i % 3, :]), src, ACT.Ln, bias=eps_col, scale=1.0 / DH))
                        nc.scalar.activation(rinvs[:, i % 3, :], rinvs[:, i % 3, :], ACT.Exp, scale=-0.5).then_inc(act_job, 1)
                act.wait_ge(dve_job, (L + 1) * DVE_N[-1])
                act.wait_ge(lf_abs, L + 1)
                link(nc.scalar.activation(Dr[:, 0, :], Dr[:, 0, :], ACT.Exp, scale=-1.0))
                nc.scalar.activation(Dr[:, 0, :], Dr[:, 0, :], ACT.Ln, bias=1.0).then_inc(lf_ready, 1)
                nc.scalar.activation(Dr[:, 1, :], B[:, 1, :], ACT.Ln).then_inc(lf_ready, 1)
                nc.scalar.activation(Dr[:, 2, :], B[:, 2, :], ACT.Ln).then_inc(lf_ready, 1)
                diffs = L * CT * (NI - 1)
                for ct in range(CT):
                    for kind, i in ITEMS:
                        n = L * CT * NI + ct * NI + ITEM_AT[(kind, i)]
                        D = Dr[:, n % 3, :]
                        if kind == "eb":
                            act.wait_ge(b_ready, CT * L + CT)
                            if n >= 3:
                                act.wait_ge(term_ready, n - 2)
                            nc.scalar.activation(D, B[:, ct, :], ACT.Exp).then_inc(exp_ready, 1)
                            continue
                        diffs += 1
                        act.wait_ge(diff_ready, diffs)
                        if kind == "kd":
                            v = D
                        elif kind == "qt":
                            v = D[:, 0:SEQ].rearrange("p (c s) -> p c s", c=TT)[:, :, BLK:P]
                        elif kind == "kt":
                            v = D[:, 0:SEQ].rearrange("p (c s) -> p c s", c=TT)[:, :, 0:BLK * i]
                        elif kind == "pj":
                            v = D[:, 0:32 * (BLK - i)]
                        else:
                            v = D[:, 0:NB * (DEC - i)]
                        nc.scalar.activation(v, v, ACT.Exp).then_inc(exp_ready, 1)
                        if (kind, i) == ("kt", 3):
                            act.wait_ge(kdt_ps, CT * L + ct + 1)
                            nc.scalar.activation(KdT[:, 0:TT, :], ps[:, 0, :].rearrange("p (c s) -> p c s", c=TT), ACT.Copy)
                            nc.scalar.activation(KdT[0:NS, TT, :], ps[0:NS, 1, 0:P], ACT.Copy).then_inc(kdt_ready, 1)
                    for k in range(CT_HEADS[ct] // 2):
                        m = (0, 2, 3)[ct] + k
                        bp, bs = 3 + 2 * k, 4 + 2 * k
                        act.wait_ge(o_done, 4 * L + m + 1)
                        if k:
                            act.wait_ge(mixl_ready, 4 * L + m)
                        act.wait_ge(term_ready, L * CT * NI + ct * NI + NI)
                        nc.scalar.activation(osq[:, 0:SEQ], ps[:, bp, :], ACT.Square)
                        nc.scalar.activation(osq[:, SEQ:T], ps[:, bs, 0:NS], ACT.Square).then_inc(osq_ready, 1)
                        act.wait_ge(oss_done, 4 * L + m + 1)
                        nc.scalar.activation(orinv[:, 0:SEQ], ps[:, 7, :], ACT.Ln, bias=eps_col, scale=1.0 / DV)
                        link(nc.scalar.activation(orinv[:, SEQ:T], ps[:, 0, 0:NS], ACT.Ln, bias=eps_col, scale=1.0 / DV))
                        nc.scalar.activation(orinv, orinv, ACT.Exp, scale=-0.5).then_inc(orinv_ready, 1)
                n0 = 32 * L
                for n in range(32 + 3):
                    if n < 32:
                        w = P * (n % 4 + 1)
                        act.wait_ge(mx_ready, n0 + n + 1)
                        nc.scalar.activation(Pp[:, n % 4, 0:w], Pp[:, n % 4, 0:w], ACT.Exp, bias=negmax[:, n % 4:n % 4 + 1],
                                             accum_out=den[:, n % 4:n % 4 + 1]).then_inc(p_ready, 1)
                    k = n - 2
                    if 0 <= k < 32:
                        w = P * (k % 4 + 1)
                        act.wait_ge(pt_ps, n0 + k + 1)
                        if k >= 2:
                            act.wait_ge(pv_done, n0 + k - 1)
                        nc.scalar.activation(PTp[:, k % 2, 0:w], ps[:, 2 + k % 2, 0:w], ACT.Copy).then_inc(pt_ready, 1)
                    k = n - 3
                    if 0 <= k < 32 and k % 8 == 7:
                        act.wait_ge(pv_done, n0 + k + 1)
                        hp = k // 8
                        if hp == 0:
                            act.wait_ge(stored_s, 64 * (L + 1))
                        nc.scalar.activation(mix[:, 4 + hp, 0:SEQ], ps[:, 4 + hp % 2, :], ACT.Copy).then_inc(mixc_ready, 1)
                for b in range(NB + 1):
                    if b < NB:
                        n = NB * L + b
                        act.wait_ge(smx_ready, n + 1)
                        nc.scalar.activation(Ps[:, b % 2, :], Ps[:, b % 2, :], ACT.Exp, bias=negmax[:, 4 + b % 2:5 + b % 2],
                                             accum_out=den[:, 4 + b % 2:5 + b % 2]).then_inc(sp_ready, 1)
                    if b >= 1:
                        n = NB * L + b - 1
                        act.wait_ge(spt_ps, n + 1)
                        pt = PTs[:, (b - 1) % 2, :]
                        nc.scalar.activation(pt[:, 0:1024], ps[:, 3:5, :].rearrange("p a t -> p (a t)"), ACT.Copy)
                        nc.scalar.activation(pt[0:NS, 1024:1152], ps[0:NS, 5, 0:P], ACT.Copy).then_inc(spt_ready, 1)
                act.wait_ge(stored_kc, 16 * NB * (L + 1))
                act.wait_ge(stored_vc, 16 * NB * (L + 1))
                norm(2 * L + 1, sqf, hid[:, 0, :], lambda c: act.wait_ge(out_evac, PF0[L] + c + 1))
                if L == 1:
                    act.wait_ge(rexp, 1)
                    nc.scalar.activation(rt[:, 80:85], rt[:, 80:85], ACT.Exp).then_inc(rexp_done, 1)
                with act.Fori(0, EXPERTS[L]) as e:
                    for i in range(FE):
                        act.wait_ge(unit_done, e * U_EXP + (ud_ffn(L) + 2 * i + 1))
                        if i >= 2:
                            act.wait_ge(out_evac, e * U_EXP + (pf_ffn(L) + 2 * i - 2))
                        nc.scalar.activation(split(ft[:, i % 2, :]), pair((2 * i) % 4), ACT.Exp, scale=-1.0).then_inc(sig_ready, 1)

        @block.tensor
        def _(pe):
            def gemm(out_pair, w, rhs, k, kn):
                for a in range(2):
                    op = nc.tensor.matmul(out_pair[:, a, :], w, rhs[:, a * HALF:a * HALF + HALF], start=k == 0, stop=k == kn - 1)
                return op

            def landed(n):
                pe.wait_ge(w_land[n % R], 16 * (n // R + 1))
                return ring[:, n % R, :]

            def norm(k, buf):
                for c in range(KC):
                    pe.wait_ge(sq_ready, KC * k + c + 1)
                    gemm(pair(0), const["ones"], buf[:, c % 4, :], c, KC).then_inc(sq_used, 1)

            pe.wait_ge(c_in, 16 * 5)
            for L in range(DEPTH):
                if L:
                    pe.wait_ge(out_evac, pf_ffn(0) + EXPERTS[0] * U_EXP)
                norm(2 * L, sq)
                ring_n = RING0[L]
                for half in range(2):
                    for u in range(4):
                        w = landed(ring_n)[:, 0:1024].rearrange("p (k c) -> p k c", k=2)
                        ring_n += 1
                        for kk in range(2):
                            k = 2 * u + kk
                            if half == 0:
                                pe.wait_ge(h_ready, 2 * L * KC + k + 1)
                            for tt in range(5):
                                n = half * 5 + tt
                                if k == 0 and n >= 8:
                                    pe.wait_ge(v_ready, 10 * L + n - 7)
                                rows = P if tt < TT else NS
                                op = nc.tensor.matmul(ps[0:rows, n % 8, :], H[:, k, tt * P:tt * P + rows], w[:, kk, :],
                                                      start=k == 0, stop=k == KC - 1)
                                if k == KC - 1:
                                    op.then_inc(v_half, 1)
                        if u < 3:
                            op.then_inc(unit_done, 1)
                for n, (kind, i) in enumerate(JOBS):
                    out = pair((n + 1) % 4)
                    if n < 4:
                        pe.wait_ge(v_ready, 10 * L + (4, 6, 8, 10)[n])
                    else:
                        m = n - 4
                        if JOBS[m][0] in ("bf", "c", "s"):
                            pe.wait_ge(act_job, L * ACT_N[-1] + ACT_N[m])
                        else:
                            pe.wait_ge(dve_job, L * DVE_N[-1] + DVE_N[m])
                    if HAS_W[n]:
                        w = landed(ring_n)
                        ring_n += 1
                        cols = RANK if kind == "lr" else P
                        w = w[:, 0:KC * cols].rearrange("p (k c) -> p k c", k=KC)
                        for k in range(KC):
                            op = gemm(out[0:cols], w[:, k, :], H[:, k, :], k, KC)
                    elif kind == "gu":
                        pe.wait_ge(dve_job, L * DVE_N[-1] + DVE_N[JOB_AT[("lr", 0)]])
                        op = gemm(out, WU[0:RANK, L * P:L * P + P], lr_sb, 0, 1)
                    elif kind == "s":
                        pe.wait_ge(act_job, L * ACT_N[-1] + ACT_N[JOB_AT[("c", i)]])
                        op = gemm(out, const["bones"], e1s[:, i % 3, :], 0, 1)
                    else:
                        pe.wait_ge(dve_job, L * DVE_N[-1] + DVE_N[JOB_AT[("s", i)]])
                        op = gemm(out, const["rot"], qn[:, i % 3, :], 0, 1)
                    op.then_inc(pe_job, 1)

                pe.wait_ge(s0_in[0], 16 * (L + 1))
                pe.wait_ge(s0_in[1], 16 * (L + 1))
                for ct in range(CT):
                    nh = CT_HEADS[ct]
                    it0 = L * CT * NI + ct * NI
                    heads = [(h, chunk_rows(h, nh), ((0, 4, 6)[ct] + h) * DV) for h in range(nh)]
                    pe.wait_ge(term_ready, it0 + ITEM_AT[("kd", 0)] + 1)
                    if ct == 0:
                        pe.wait_ge(dve_job, (L + 1) * DVE_N[-1])
                    else:
                        pe.wait_ge(mixl_ready, 4 * L + (2, 3)[ct - 1])
                    for c in range(TT):
                        nc.tensor.transpose(ps[:, 0, c * P:c * P + P], kd[:, c * P:c * P + P], const["ident"])
                    nc.tensor.transpose(ps[0:NS, 1, 0:P], kd[:, SEQ:T], const["ident"]).then_inc(kdt_ps, 1)
                    for i in range(1, NBLK):
                        pe.wait_ge(term_ready, it0 + ITEM_AT[("kt", i)] + 1)
                        for c in range(TT):
                            for h, r, _ in heads:
                                at = c * P + i * BLK
                                op = nc.tensor.matmul(ps[:, 4 + h, at:at + BLK], Kt[r, i - 1, c, :], qt[r, at:at + BLK],
                                                      start=True, stop=True)
                    op.then_inc(off_done, 1)
                    pe.wait_ge(kdt_ready, CT * L + ct + 1)
                    np_ = L * CT * (BLK + DEC) + ct * (BLK + DEC)
                    for j in range(BLK):
                        w = BLK - j
                        pe.wait_ge(term_ready, it0 + ITEM_AT[("pj", j)] + 1)
                        for h, r, _ in heads:
                            op = nc.tensor.matmul(
                                ps[:, h, :].rearrange("p (n s) -> p n s", s=BLK)[:, :, j:BLK],
                                const["w16"][r, w:w + P],
                                Pr[r, j % 2, 0:32 * w].rearrange("p (n s) -> p n s", s=w), start=j == 0, stop=j == BLK - 1)
                        op.then_inc(prod_used, 1)
                    pe.wait_ge(a_ready, 8 * L + (4, 6, 8)[ct])
                    for j in range(DEC):
                        w = DEC - j
                        pe.wait_ge(term_ready, it0 + ITEM_AT[("sj", j)] + 1)
                        for h, r, _ in heads:
                            op = nc.tensor.matmul(
                                ps[0:NS, h, 0:NS].rearrange("p (n s) -> p n s", s=DEC)[:, :, j:DEC],
                                const["w8"][r, w:w + NS],
                                Pr[r, j % 2, 0:NB * w].rearrange("p (n s) -> p n s", s=w),
                                start=j == 0, stop=j == DEC - 1)
                        op.then_inc(prod_used, 1)
                    pe.wait_ge(as_ready, CT * L + ct + 1)
                    for c in range(TT):
                        for h, r, vo in heads:
                            op = nc.tensor.matmul(ps[r, 1, c * DV:c * DV + DV], KdT[:, c, r], V[:, c, vo:vo + DV],
                                                  start=True, stop=True)
                    op.then_inc(upd_done, 1)
                    for h, r, vo in heads:
                        pe.wait_ge(vbd_ready, 8 * L + vo // DV + 1)
                        nc.tensor.matmul(ps[r, 2, :], KdT[0:NS, TT, r], vbd[0:NS, :], start=True, stop=True).then_inc(vbd_used, 1)
                    pe.wait_ge(s_ready, CT * L + ct + 1)
                    for k in range(nh // 2):
                        m = (0, 2, 3)[ct] + k
                        bp, bs = 3 + 2 * k, 4 + 2 * k
                        for hb in range(2):
                            h, r, vo = heads[2 * k + hb]
                            o = slice(hb * DV, hb * DV + DV)
                            for c in range(TT):
                                t = slice(c * P, c * P + P)
                                nc.tensor.matmul(ps[o, bp, t], V[:, c, vo:vo + DV], A[:, h, t], start=True, stop=c == 0)
                                if c:
                                    nc.tensor.matmul(ps[o, bp, t], S[r, ct, c - 1, :], Qe[r, ct, t], start=False, stop=True)
                            nc.tensor.matmul(ps[o, bs, 0:NS], V[:, TT, vo:vo + DV], A[:, h, SEQ:T],
                                             start=True, stop=False, skip_group_check=True)
                            for b in range(NB):
                                t = DEC * b
                                op = nc.tensor.matmul(ps[o, bs, t:t + DEC], S0[r, ct, b, :], Qe[r, ct, SEQ + t:SEQ + t + DEC],
                                                      start=False, stop=True, skip_group_check=True)
                        op.then_inc(o_done, 1)
                        pe.wait_ge(osq_ready, 4 * L + m + 1)
                        nc.tensor.matmul(ps[:, 7, :], const["bones"], osq[:, 0:SEQ], start=True, stop=True)
                        nc.tensor.matmul(ps[:, 0, 0:NS], const["bones"], osq[:, SEQ:T], start=True, stop=True).then_inc(oss_done, 1)

                pe.wait_ge(mixl_ready, 4 * (L + 1))
                pe.wait_ge(sn_ready, CT * (L + 1))
                n0 = 32 * L
                for n in range(32 + 3):
                    if n < 32:
                        h, qt_ = n // 4, n % 4
                        r = slice((h % 2) * DH, (h % 2) * DH + DH)
                        w = P * (qt_ + 1)
                        if n >= 2:
                            pe.wait_ge(sc_free, n0 + n - 1)
                        nc.tensor.matmul(ps[:, n % 2, 0:w], QK[r, h // 2, qt_ * P:qt_ * P + P], QK[r, 4 + h // 2, 0:w],
                                         start=True, stop=True).then_inc(sc_done, 1)
                    k = n - 2
                    if 0 <= k < 32:
                        pe.wait_ge(pn_ready, n0 + k + 1)
                        if k >= 2:
                            pe.wait_ge(pt_ready, n0 + k - 1)
                        for kb in range(k % 4 + 1):
                            op = nc.tensor.transpose(ps[:, 2 + k % 2, kb * P:kb * P + P], Pp[:, k % 4, kb * P:kb * P + P],
                                                     const["ident"])
                        op.then_inc(pt_ps, 1)
                    k = n - 3
                    if 0 <= k < 32:
                        h, qt_ = k // 4, k % 4
                        if k % 8 == 0 and k >= 16:
                            pe.wait_ge(mixc_ready, 4 * L + k // 8 - 1)
                        pe.wait_ge(pt_ready, n0 + k + 1)
                        o = slice((h % 2) * DH, (h % 2) * DH + DH)
                        for kb in range(qt_ + 1):
                            op = nc.tensor.matmul(ps[o, 4 + (h // 2) % 2, qt_ * P:qt_ * P + P], V[:, kb, 512 + h * DH:512 + h * DH + DH],
                                                  PTp[:, k % 2, kb * P:kb * P + P], start=kb == 0, stop=kb == qt_)
                        op.then_inc(pv_done, 1)
                pe.wait_ge(qs_ready, L + 1)
                pe.wait_ge(mixc_ready, 4 * (L + 1))
                for b in range(NB + 1):
                    if b < NB:
                        n = NB * L + b
                        pe.wait_ge(kc_in, 16 * (n + 1))
                        if b:
                            pe.wait_ge(ssc_free, n)
                        for hp in range(4):
                            o = slice(32 * hp, 32 * hp + 32)
                            for a in range(2):
                                nc.tensor.matmul(ps[o, a, :], Qs[:, b, hp, :], Kc[:, hp, a * 512:a * 512 + 512], start=True, stop=True)
                            op = nc.tensor.matmul(ps[o, 2, 0:NS], Qs[:, b, hp, :], QK[:, 4 + hp, SEQ:T], start=True, stop=True)
                        op.then_inc(ssc_done, 1)
                    if b >= 1:
                        n = NB * L + b - 1
                        q = (b - 1) % 2
                        pe.wait_ge(spn_ready, n + 1)
                        if b >= 2:
                            pe.wait_ge(spt_ready, n)
                        for c in range(8):
                            nc.tensor.transpose(ps[:, 3 + c // 4, (c % 4) * P:(c % 4) * P + P], Ps[:, q, c:PAST:8], const["ident"])
                        nc.tensor.transpose(ps[0:NS, 5, 0:P], Ps[:, q, PAST:PAST + NS], const["ident"]).then_inc(spt_ps, 1)
                        pe.wait_ge(spt_ready, n + 1)
                        pe.wait_ge(vc_in, 16 * (n + 1))
                        if b >= 3:
                            pe.wait_ge(smix_ready, n - 1)
                        pt = tiles(PTs[:, q, :], 9)
                        for hp in range(4):
                            out = ps[:, 6 + q, hp * 16:hp * 16 + 16]
                            for c in range(8):
                                nc.tensor.matmul(out, Vc[:, c, hp * P:hp * P + P], pt[:, c, 32 * hp:32 * hp + 16], start=c == 0, stop=False)
                            op = nc.tensor.matmul(out, V[0:NS, TT, 512 + hp * P:512 + hp * P + P], pt[0:NS, 8, 32 * hp:32 * hp + 16],
                                                  start=False, stop=True)
                        op.then_inc(spv_done, 1)
                pe.wait_ge(smix_ready, NB * (L + 1))
                for m in range(U_OUT):
                    w = landed(ring_n)[:, 0:1024].rearrange("p (k c) -> p k c", k=KC)
                    ring_n += 1
                    if m >= 4:
                        pe.wait_ge(out_evac, PF0[L] + m - 3)
                    for k in range(KC):
                        op = gemm(pair(m % 4), w[:, k, :], mix[:, k, :], k, KC)
                    op.then_inc(unit_done, 1)
                pe.wait_ge(out_evac, PF0[L] + U_OUT)
                norm(2 * L + 1, sqf)
                pe.wait_ge(h_ready, (2 * L + 2) * KC)
                if L == 1:
                    for tt in range(5):
                        rows = P if tt < TT else NS
                        for k in range(KC):
                            op = nc.tensor.matmul(ps[0:rows, 2, tt * 8:tt * 8 + 8], H[:, k, tt * P:tt * P + rows],
                                                  WRT[:, k * 8:k * 8 + 8], start=k == 0, stop=k == KC - 1)
                    op.then_inc(rl_done, 1)
                    pe.wait_ge(cw_tok, 1)
                    for e in range(8):
                        if e >= 4:
                            pe.wait_ge(cw_ready, e - 3)
                        for tt in range(5):
                            rows = P if tt < TT else NS
                            out = ps[:, 2 * (e % 4), tt * P:tt * P + P] if tt < TT else ps[:, 2 * (e % 4) + 1, 0:NS]
                            op = nc.tensor.matmul(out, rt[0:rows, tt * 8 + e:tt * 8 + e + 1].to_broadcast([rows, P]),
                                                  const["ident"][0:rows, 0:rows], start=True, stop=True)
                        op.then_inc(cwb_done, 1)
                    pe.wait_ge(cw_ready, 8)
                base, pf = ring_n, pf_ffn(L)
                with pe.Fori(0, EXPERTS[L]) as e:
                    for j in range(U_EXP):
                        n = base + j
                        pe.wait_ge(w_land[n % R], e * (16 * U_EXP // R) + 16 * (n // R + 1))
                        last = j - 4 if j >= 4 else (28, 29, 26, 27)[j] - U_EXP
                        pe.wait_ge(out_evac, e * U_EXP + (pf + last + 1))
                        if j < 2 * FE:
                            w = ring[:, n % R, 0:1024].rearrange("p (k c) -> p k c", k=KC)
                            for k in range(KC):
                                op = gemm(pair(j % 4), w[:, k, :], H[:, k, :], k, KC)
                        else:
                            w = ring[:, n % R, :].rearrange("p (k c) -> p k c", k=FE)
                            for k in range(FE):
                                if j == 2 * FE:
                                    pe.wait_ge(out_evac, e * U_EXP + (pf + 2 * k + 2))
                                op = gemm(pair(j % 4), w[:, k, :], hid[:, k, :], k, FE)
                        op.then_inc(unit_done, 1)

        @block.vector
        def _(dve):
            v = nc.vector
            n_chain = [0]

            def link(op):
                op.then_inc(dch, 1)
                n_chain[0] += 1
                dve.wait_ge(dch, n_chain[0])

            v.memset(V[NS:P, TT, :], 0.0)
            v.memset(eps_col, EPS).then_inc(eps_ready, 1)
            dve.wait_ge(c_in, 16 * 5)
            l0, l1 = LB[:, 16:18], LB[:, 18:20]
            link(v.tensor_tensor(LB[:, 28:30], l0, l1, ALU.max))
            link(v.tensor_tensor(LB[:, 24:26], l0, LB[:, 28:30], ALU.subtract))
            v.tensor_tensor(LB[:, 26:28], l1, LB[:, 28:30], ALU.subtract).then_inc(lb_ready, 1)
            dve.wait_ge(lb_exp, 1)
            w0, w1 = LB[:, 20:22], LB[:, 22:24]
            link(v.tensor_tensor(LB[:, 28:30], w0, w1, ALU.add))
            link(v.reciprocal(LB[:, 30:32], LB[:, 28:30]))
            link(v.tensor_tensor(w0, w0, LB[:, 30:32], ALU.mult))
            link(v.tensor_tensor(w1, w1, LB[:, 30:32], ALU.mult))
            link(v.tensor_tensor(LB[:, 0:2], w0, w0, ALU.subtract))
            link(v.tensor_tensor(LB[:, 28:30], w0, w1, ALU.add))
            link(v.tensor_tensor(LB[:, 2:4], LB[:, 28:30], w0, ALU.subtract))
            link(v.tensor_scalar(oml, lb, -1.0, 1.0, ALU.mult, ALU.add))

            def normed(k, r, gains):
                dve.wait_ge(rinv_ready, k + 1)
                for c in range(KC):
                    v.scalar_tensor_tensor(H[:, c, :], X[:, c, :], gains[:, c:c + 1], r, ALU.mult, ALU.mult).then_inc(h_ready, 1)

            def job(op):
                op.then_inc(dve_job, 1)

            for L in range(DEPTH):
                normed(2 * L, rinv, vec(L, "g_mix"))
                for n, (kind, i) in enumerate(JOBS):
                    if not HAS_DVE[n]:
                        continue
                    src = pair((n + 1) % 4)
                    s = n % 3
                    if kind in ("bf", "bq", "g", "s"):
                        dve.wait_ge(act_job, L * ACT_N[-1] + ACT_N[n])
                    else:
                        dve.wait_ge(pe_job, L * NJ + n + 1)
                    if kind == "lr":
                        job(v.tensor_copy(split(lr_sb), src[0:RANK]))
                    elif kind == "bf":
                        f, kk = e0[:, s, :], e1s[:, s, :]
                        link(v.tensor_scalar(f, f, 1.0, None, ALU.add))
                        link(v.tensor_scalar(kk, kk, 1.0, None, ALU.add))
                        link(v.reciprocal(f, f))
                        link(v.reciprocal(kk, kk))
                        v.tensor_scalar(B[:, 1 + i, :], f, oml[:, 2 * L + i:2 * L + i + 1], lb[:, 2 * L + i:2 * L + i + 1], ALU.mult, ALU.add)
                        job(v.tensor_scalar(K[:, 1 + i, :], kk, oml[:, 2 * L + i:2 * L + i + 1], None, ALU.mult))
                    elif kind == "aq":
                        job(v.tensor_scalar(split(Q[:, 0, :]), src, float(DK_A) ** -0.5, None, ALU.mult))
                    elif kind == "gu":
                        job(v.tensor_scalar(split(B[:, 0, :]), src, vec(L, "b_gate"), None, ALU.add))
                    elif kind == "ak":
                        job(v.tensor_copy(split(K[:, 0, :]), src))
                    elif kind in ("bq", "g"):
                        dst = Q[:, 1 + i, :] if kind == "bq" else G[:, i, :]
                        f = e0[:, s, :]
                        link(v.tensor_scalar(f, f, 1.0, None, ALU.add))
                        link(v.reciprocal(f, f))
                        job(v.tensor_tensor(split(dst), src, split(f), ALU.mult))
                    elif kind == "s":
                        gain = vec(L, "g_q" if i < 4 else "g_k")
                        job(v.scalar_tensor_tensor(qn[:, i % 3, :], e0[:, i % 3, :], gain, rinvs[:, i % 3, :], ALU.mult, ALU.mult))
                    else:
                        dst = QK[:, i, :]
                        if i:
                            dve.wait_ge(dve_job, L * DVE_N[-1] + DVE_N[n - 1])
                        v.tensor_tensor(split(rtmp), src, split(const["sin"]), ALU.mult)
                        link(v.tensor_tensor(dst, qn[:, i % 3, :], const["cos"], ALU.mult))
                        job(v.tensor_tensor(dst, dst, rtmp, ALU.add))
                dve.wait_ge(dve_job, (L + 1) * DVE_N[-1])
                link(v.tensor_scalar(Dr[:, 1, :], B[:, 0, :], -1.0, None, ALU.mult))
                v.tensor_tensor(Dr[:, 0, :], B[:, 0, :], Dr[:, 1, :], ALU.max).then_inc(lf_abs, 1)
                dve.wait_ge(lf_ready, 3 * L + 1)
                link(v.scalar_tensor_tensor(Dr[:, 0, :], B[:, 0, :], 0.0, Dr[:, 0, :], ALU.min, ALU.subtract))
                link(v.tensor_scalar(Dr[:, 0, :], Dr[:, 0, :], 1.0 / 16.0, None, ALU.mult))
                v.tensor_tensor_scan(B[:, 0, :], const["reset"], Dr[:, 0, :], 0.0, ALU.mult, ALU.add).then_inc(b_ready, 1)
                for ct in (1, 2):
                    dve.wait_ge(lf_ready, 3 * L + 1 + ct)
                    v.tensor_tensor_scan(B[:, ct, :], const["reset"], Dr[:, ct, :], 0.0, ALU.mult, ALU.add).then_inc(b_ready, 1)
                v.memset(A[NS:P, :, SEQ:T], 0.0)
                for ct in range(CT):
                    nh = CT_HEADS[ct]
                    it0 = L * CT * NI + ct * NI
                    np_ = L * CT * (BLK + DEC) + ct * (BLK + DEC)
                    Qp = Q[:, ct, 0:SEQ].rearrange("p (n s) -> p n s", s=BLK)
                    Kp = K[:, ct, 0:SEQ].rearrange("p (n s) -> p n s", s=BLK)
                    Qd = Q[:, ct, SEQ:T].rearrange("p (n s) -> p n s", s=DEC)
                    Kd_ = K[:, ct, SEQ:T].rearrange("p (n s) -> p n s", s=DEC)
                    for kind, i in ITEMS:
                        it = it0 + ITEM_AT[(kind, i)]
                        D = Dr[:, it % 3, :]
                        Dp = D[:, 0:SEQ].rearrange("p (c s) -> p c s", c=TT)
                        dve.wait_ge(exp_ready, it + 1)
                        if kind == "eb":
                            v.tensor_copy(ebl[:, ct, 0:TT], D[:, P - 1:SEQ:P])
                            v.tensor_copy(ebl[:, ct, TT:12], D[:, SEQ + DEC - 1:T:DEC])
                            op = v.tensor_tensor(Qe[:, ct, :], Q[:, ct, :], D, ALU.mult)
                        elif kind == "kd":
                            op = v.tensor_tensor(kd, K[:, ct, :], D, ALU.mult)
                        elif kind == "qt":
                            if ct:
                                dve.wait_ge(off_done, CT * L + ct)
                            op = v.tensor_tensor(qt.rearrange("p (c s) -> p c s", c=TT)[:, :, BLK:P],
                                                 Q[:, ct, 0:SEQ].rearrange("p (c s) -> p c s", c=TT)[:, :, BLK:P], Dp[:, :, BLK:P], ALU.mult)
                        elif kind == "kt":
                            w = BLK * i
                            if i == 1:
                                dve.wait_ge(kt_zero, L + 1)
                            op = v.tensor_tensor(Kt[:, i - 1, :, 0:w], K[:, ct, 0:SEQ].rearrange("p (c s) -> p c s", c=TT)[:, :, 0:w],
                                                 Dp[:, :, 0:w], ALU.mult)
                        else:
                            blk, nblk, q_, k_ = (BLK, SEQ // BLK, Qp, Kp) if kind == "pj" else (DEC, NB, Qd, Kd_)
                            w = blk - i
                            m = i if kind == "pj" else BLK + i
                            if m >= 2:
                                dve.wait_ge(prod_used, np_ + m - 1)
                            prod = Pr[:, m % 2, 0:nblk * w].rearrange("p (n s) -> p n s", s=w)
                            dd = D[:, 0:nblk * w].rearrange("p (n s) -> p n s", s=w)
                            link(v.tensor_tensor(prod, dd, k_[:, :, i:i + 1].to_broadcast([P, nblk, w]), ALU.mult))
                            op = v.tensor_tensor(prod, prod, q_[:, :, i:blk], ALU.mult)
                        op.then_inc(term_ready, 1)
                        if (kind, i) == ("pj", BLK - 1):
                            dve.wait_ge(prod_used, np_ + BLK)
                            dve.wait_ge(off_done, CT * L + ct + 1)
                            for h in range(nh):
                                a3 = A[:, h, 0:SEQ].rearrange("p (c s) -> p c s", c=TT)
                                link(v.tensor_tensor(a3, ps[:, h, :].rearrange("p (c s) -> p c s", c=TT),
                                                     const["mask16"].rearrange("p (o s) -> p o s", o=1).to_broadcast([P, TT, P]), ALU.mult))
                                v.tensor_tensor(a3[:, :, BLK:P], a3[:, :, BLK:P],
                                                ps[:, 4 + h, :].rearrange("p (c s) -> p c s", c=TT)[:, :, BLK:P], ALU.add).then_inc(a_ready, 1)
                    dve.wait_ge(prod_used, np_ + BLK + DEC)
                    v.tensor_tensor(A[0:NS, 0:nh, SEQ:T], ps[0:NS, 0:nh, 0:NS],
                                    const["mask8"][0:NS, :].rearrange("p (o s) -> p o s", o=1).to_broadcast([NS, nh, NS]),
                                    ALU.mult).then_inc(as_ready, 1)
                    dve.wait_ge(upd_done, CT * L + ct + 1)
                    link(v.tensor_copy(S[:, ct, 0, :], ps[:, 1, 0:DV]))
                    for c in range(1, TT):
                        op = v.scalar_tensor_tensor(S[:, ct, c, :], S[:, ct, c - 1, :], ebl[:, ct, c:c + 1],
                                                    ps[:, 1, c * DV:c * DV + DV], ALU.mult, ALU.add)
                        if c < TT - 1:
                            link(op)
                    op.then_inc(s_ready, 1)
                    for k in range(nh // 2):
                        m = (0, 2, 3)[ct] + k
                        bp, bs = 3 + 2 * k, 4 + 2 * k
                        dve.wait_ge(orinv_ready, 4 * L + m + 1)
                        gain = vec(L, "g_gla" if ct == 0 else "g_hgrn")
                        v.scalar_tensor_tensor(mix[:, m, 0:SEQ], ps[:, bp, :], gain, orinv[:, 0:SEQ], ALU.mult, ALU.mult)
                        link(v.scalar_tensor_tensor(mix[:, m, SEQ:T], ps[:, bs, 0:NS], gain, orinv[:, SEQ:T], ALU.mult, ALU.mult))
                        v.tensor_tensor(mix[:, m, :], mix[:, m, :], G[:, m, :], ALU.mult).then_inc(mixl_ready, 1)
                    dve.wait_ge(vbd_used, 8 * L + (4, 6, 8)[ct])
                    s0 = S0[:, ct, :, :]
                    link(v.tensor_tensor(s0, s0, ebl[:, ct, TT:12].rearrange("p (b o) -> p b o", o=1).to_broadcast([P, NB, DV]), ALU.mult))
                    v.tensor_tensor(s0, s0, ps[:, 2, :].rearrange("p (b v) -> p b v", b=NB), ALU.add).then_inc(sn_ready, 1)
                dve.wait_ge(mixl_ready, 4 * (L + 1))
                link(v.memset(LIN[:, 4096:5120], 0.0))
                for hb in range(2):
                    r = slice(hb * DH, hb * DH + DH)
                    for hp in range(4):
                        op = v.tensor_copy(Qs[r, :, hp, hb * DEC:hb * DEC + DEC], QK[r, hp, SEQ:T].rearrange("p (b t) -> p b t", b=NB))
                op.then_inc(qs_ready, 1)
                n0 = 32 * L
                for n in range(32 + 1):
                    if n < 32:
                        w = P * (n % 4 + 1)
                        pn, s = Pp[:, n % 4, 0:w], n % 4
                        dve.wait_ge(sc_done, n0 + n + 1)
                        if n >= 4:
                            dve.wait_ge(pt_ps, n0 + n - 3)
                        v.scalar_tensor_tensor(pn, ps[:, n % 2, 0:w], DH ** -0.5, const["lnc"][:, SEQ - w:SEQ],
                                               ALU.mult, ALU.add).then_inc(sc_free, 1)
                        dve.wait_ge(sc_free, n0 + n + 1)
                        v.tensor_reduce(negmax[:, s:s + 1], pn, AX.X, ALU.max, negate=True).then_inc(mx_ready, 1)
                    k = n - 1
                    if k >= 0:
                        w = P * (k % 4 + 1)
                        pk, s = Pp[:, k % 4, 0:w], k % 4
                        dve.wait_ge(p_ready, n0 + k + 1)
                        link(v.reciprocal(rden[:, s:s + 1], den[:, s:s + 1]))
                        v.tensor_scalar(pk, pk, rden[:, s:s + 1], None, ALU.mult).then_inc(pn_ready, 1)
                for b in range(NB + 2):
                    if b < NB:
                        n = NB * L + b
                        pn, s = Ps[:, b % 2, :], 4 + b % 2
                        dve.wait_ge(ssc_done, n + 1)
                        if b >= 2:
                            dve.wait_ge(spt_ps, n - 1)
                        v.scalar_tensor_tensor(pn[:, 0:PAST], ps[:, 0:2, :].rearrange("p a t -> p (a t)"), DH ** -0.5,
                                               const["smask"], ALU.mult, ALU.add)
                        v.scalar_tensor_tensor(pn[:, PAST:PAST + NS], ps[:, 2, 0:NS], DH ** -0.5,
                                               const["smask_new"][:, b * NS:b * NS + NS], ALU.mult, ALU.add).then_inc(ssc_free, 1)
                        dve.wait_ge(ssc_free, n + 1)
                        v.tensor_reduce(negmax[:, s:s + 1], pn, AX.X, ALU.max, negate=True).then_inc(smx_ready, 1)
                        dve.wait_ge(sp_ready, n + 1)
                        link(v.reciprocal(rden[:, s:s + 1], den[:, s:s + 1]))
                        v.tensor_scalar(pn, pn, rden[:, s:s + 1], None, ALU.mult).then_inc(spn_ready, 1)
                    if b >= 2:
                        bb = b - 2
                        dve.wait_ge(spv_done, NB * L + bb + 1)
                        o = ps[:, 6 + bb % 2, 0:64].rearrange("p (h q) -> p h q", h=4)
                        t = SEQ + DEC * bb
                        v.tensor_copy(mix[0:DH, 4:8, t:t + DEC], o[0:DH, :, 0:DEC])
                        v.tensor_copy(mix[DH:P, 4:8, t:t + DEC], o[DH:P, :, DEC:2 * DEC]).then_inc(smix_ready, 1)
                for m in range(U_OUT):
                    dve.wait_ge(unit_done, UD0[L] + NVU + m + 1)
                    v.tensor_tensor(split(X[:, m, :]), split(X[:, m, :]), pair(m % 4), ALU.add).then_inc(out_evac, 1)
                normed(2 * L + 1, hid[:, 0, :], vec(L, "g_ffn"))
                if L == 1:
                    def t3(o):
                        return rt[:, o:o + 40].rearrange("p (t e) -> p t e", e=8)

                    def t1(o):
                        return rt[:, o:o + 5]

                    def over_e(o):
                        return t1(o).rearrange("p (t o) -> p t o", o=1).to_broadcast([P, 5, 8])
                    lg, eq, first, second = t3(0), t3(40), t3(95), t3(135)
                    riota = const["riota"].rearrange("p (o e) -> p o e", o=1).to_broadcast([P, 5, 8])
                    link(v.memset(rt[:, 0:40], 0.0))
                    dve.wait_ge(rl_done, 1)
                    v.tensor_copy(rt[:, 0:32], ps[:, 2, 0:32])
                    link(v.tensor_copy(rt[0:NS, 32:40], ps[0:NS, 2, 32:40]))
                    for o_m, pick in ((85, first), (90, second)):
                        link(v.tensor_reduce(t1(o_m), lg, AX.X, ALU.max))
                        link(v.tensor_tensor(eq, lg, over_e(o_m), ALU.is_equal))
                        link(v.tensor_tensor(eq, eq, riota, ALU.mult))
                        link(v.tensor_reduce(t1(80), eq, AX.X, ALU.max))
                        link(v.tensor_tensor(pick, eq, over_e(80), ALU.is_equal))
                        if pick is first:
                            link(v.scalar_tensor_tensor(lg, pick, -3e38, lg, ALU.mult, ALU.add))
                    v.tensor_tensor(t1(80), t1(90), t1(85), ALU.subtract).then_inc(rexp, 1)
                    dve.wait_ge(rexp_done, 1)
                    link(v.tensor_scalar(t1(85), t1(80), 1.0, None, ALU.add))
                    link(v.reciprocal(t1(85), t1(85)))
                    link(v.tensor_tensor(t1(90), t1(80), t1(85), ALU.mult))
                    link(v.tensor_tensor(first, first, over_e(85), ALU.mult))
                    link(v.tensor_tensor(second, second, over_e(90), ALU.mult))
                    v.tensor_tensor(lg, first, second, ALU.add).then_inc(cw_tok, 1)
                    for e in range(8):
                        dve.wait_ge(cwb_done, e + 1)
                        v.tensor_copy(cw[:, e, 0:SEQ], ps[:, 2 * (e % 4), :])
                        v.tensor_copy(cw[:, e, SEQ:T], ps[:, 2 * (e % 4) + 1, 0:NS]).then_inc(cw_ready, 1)
                    dve.wait_ge(cw_ready, 8)
                steps = 3 if L else 2
                c0, pf, sg = n_chain[0], pf_ffn(L), FE * EXPERTS[0] * L
                with dve.Fori(0, EXPERTS[L]) as e:
                    for i in range(FE):
                        def step(op, k):
                            op.then_inc(dch, 1)
                            dve.wait_ge(dch, e * (FE * steps) + (c0 + i * steps + k))
                        t = ft[:, i % 2, :]
                        dve.wait_ge(sig_ready, e * FE + (sg + i + 1))
                        step(v.tensor_scalar(t, t, 1.0, None, ALU.add), 1)
                        step(v.reciprocal(t, t), 2)
                        v.tensor_tensor(split(t), pair((2 * i) % 4), split(t), ALU.mult).then_inc(out_evac, 1)
                        dve.wait_ge(out_evac, e * U_EXP + (pf + 2 * i + 1))
                        if L:
                            w = cw[:, bass.ds(e, 1), :].rearrange("p o t -> p (o t)")
                            step(v.tensor_tensor(t, t, w, ALU.mult), 3)
                        dve.wait_ge(unit_done, e * U_EXP + (ud_ffn(L) + 2 * i + 2))
                        v.tensor_tensor(split(hid[:, i, :]), pair((2 * i + 1) % 4), split(t), ALU.mult).then_inc(out_evac, 1)
                    for m in range(KC):
                        dve.wait_ge(unit_done, e * U_EXP + (ud_ffn(L) + 2 * FE + m + 1))
                        v.tensor_tensor(split(X[:, m, :]), split(X[:, m, :]), pair((2 * FE + m) % 4), ALU.add).then_inc(out_evac, 1)
                n_chain[0] = c0 + EXPERTS[L] * FE * steps


NH = 8


def lay_inputs(i):
    f = np.ascontiguousarray

    def unit(w):
        k, n = w.shape
        return f(w.reshape(k // P, P, n // P, P).transpose(2, 1, 0, 3).reshape(n // P, P, k))

    out = {"consts": shape_constants()}
    x = np.concatenate([i["x_prompt"].reshape(SEQ, D_MODEL), i["x_sample"].reshape(NS, D_MODEL)], 0)
    out["x"] = f(x.T.reshape(KC, P, T).transpose(1, 0, 2))
    w_in = i["w_in"]
    widths = [128, 128, 256, 16, 256, 256, 256, 256, 256, 512, 512, 512]
    cuts = np.cumsum(widths)[:-1].tolist()
    parts = [np.split(w_in[L], cuts, axis=1) for L in range(DEPTH)]
    feat, val, lr = [], [], []
    for L in range(DEPTH):
        a_q, a_k, a_v, a_lr, a_g, b_q, b_f, b_i, b_g, c_q, c_k, c_v = parts[L]
        feat.append(unit(np.concatenate([b_f, a_q, a_k, b_q, a_g, b_g, c_q, c_k], 1)))
        v = np.concatenate([a_v, b_i, c_v], 1)
        val.append(v.reshape(4, 2, P, 2, 512).transpose(3, 0, 2, 1, 4).reshape(NV, P, 1024))
        lr.append(a_lr.reshape(KC, P, RANK).transpose(1, 0, 2).reshape(P, KC * RANK))
    out["w_feat"], out["w_v"], out["w_lr"] = (f(np.stack(a)) for a in (feat, val, lr))
    out["w_out"] = np.stack([unit(i["w_out"][L]) for L in range(DEPTH)])
    half = FE * P
    gates, ups, downs = [], [], []
    for h in range(2):
        gates.append(i["ffn_w_gate"][0][:, h * half:(h + 1) * half])
        ups.append(i["ffn_w_up"][0][:, h * half:(h + 1) * half])
        downs.append(i["ffn_w_down"][0][h * half:(h + 1) * half])
    gates += list(i["moe_w_gate"][0])
    ups += list(i["moe_w_up"][0])
    downs += list(i["moe_w_down"][0])
    out["w_gu"] = np.concatenate([np.stack([unit(g), unit(u)], 1).reshape(2 * FE, P, D_MODEL) for g, u in zip(gates, ups)], 0)
    out["w_dn"] = np.concatenate([unit(w) for w in downs], 0)
    out["w_router"] = f(i["moe_w_router"][0].reshape(KC, P, 8).transpose(1, 0, 2).reshape(P, 64))
    out["w_up"] = f(i["gla_w_gate_up"].transpose(1, 0, 2).reshape(RANK, DEPTH * P))
    out["lb_logits"] = f(i["hgrn_lb_logits"].reshape(DEPTH, 2, P).transpose(2, 0, 1).reshape(P, 4))
    cols = []
    for L in range(DEPTH):
        cols += [i["norm_mix_g"][L].reshape(KC, P).T, i["norm_ffn_g"][L].reshape(KC, P).T, i["gla_b_gate"][L].reshape(P, 1)]
        cols += [np.tile(i[n][L], 2).reshape(P, 1) for n in ("gla_norm_g", "hgrn_norm_g", "attn_q_norm_g", "attn_k_norm_g")]
    out["vecs"] = f(np.concatenate(cols, 1))
    out["s0_gla"] = f(i["state_gla"].transpose(0, 2, 3, 1, 4).reshape(DEPTH, P, NB, DV))
    out["s0_hgrn"] = f(i["state_hgrn"].transpose(0, 2, 3, 1, 4).reshape(DEPTH, 2, P, NB, DV).transpose(0, 2, 1, 3, 4))
    out["kcache"] = f(i["cache_k_win"].reshape(DEPTH, NB, PAST, 4, P).transpose(0, 1, 4, 3, 2))
    out["vcache"] = f(i["cache_v_win"].reshape(DEPTH, NB, P, 8, 512))
    return out


OUTS = {
    "y": (P, KC, T), "os_gla_p": (DEPTH, P, DV), "os_hgrn_p": (DEPTH, P, 2, DV),
    "ok_p": (DEPTH, P, 4, SEQ), "ov_p": (DEPTH, P, TT, 512),
    "os_gla_s": (DEPTH, P, NB, DV), "os_hgrn_s": (DEPTH, P, 2, NB, DV),
    "ok_s": (DEPTH, NB, P, 4, PAST), "ov_s": (DEPTH, NB, P, 8, 512),
}


def lay_outputs(r):
    y = r["y"].transpose(1, 0, 2).reshape(D_MODEL, T).T
    return (
        np.ascontiguousarray(y[:SEQ]).reshape(1, SEQ, D_MODEL),
        np.ascontiguousarray(y[SEQ:]).reshape(NB, DEC, D_MODEL),
        r["os_gla_p"].reshape(DEPTH, 1, HEADS_A, DK_A, DV),
        r["os_hgrn_p"].transpose(0, 2, 1, 3).reshape(DEPTH, 1, HEADS_B, DK_B, DV),
        r["ok_p"].transpose(0, 3, 2, 1).reshape(DEPTH, 1, SEQ, AH, DH),
        r["ov_p"].transpose(0, 2, 1, 3).reshape(DEPTH, 1, SEQ, AH, DH),
        r["os_gla_s"].reshape(DEPTH, HEADS_A, DK_A, NB, DV).transpose(0, 3, 1, 2, 4),
        r["os_hgrn_s"].transpose(0, 2, 1, 3, 4).reshape(DEPTH, HEADS_B, DK_B, NB, DV).transpose(0, 3, 1, 2, 4),
        r["ok_s"].transpose(0, 1, 4, 3, 2).reshape(DEPTH, NB, PAST, AH, DH),
        r["ov_s"].reshape(DEPTH, NB, PAST, AH, DH),
    )


def kernel(**inputs):
    import concourse.bacc as bacc
    from concourse.bass_utils import run_bass_kernel_spmd

    nc = bacc.Bacc("TRN2", target_bir_lowering=False, num_devices=1)
    arrays = lay_inputs({n: np.asarray(a) for n, a in inputs.items()})
    d = {n: nc.dram_tensor(n, a.shape, F32, kind="ExternalInput").ap() for n, a in arrays.items()}
    d |= {n: nc.dram_tensor(n, s, F32, kind="ExternalOutput").ap() for n, s in OUTS.items()}
    build(nc, d)
    r = run_bass_kernel_spmd(nc, [arrays], core_ids=[0])
    return lay_outputs({n: np.asarray(r.results[0][n]) for n in OUTS})
```

```python
from contextlib import ExitStack

import numpy as np
import concourse.bass as bass
from concourse import mybir

F32 = mybir.dt.float32
ALU = mybir.AluOpType
ACT = mybir.ActivationFunctionType
AX = mybir.AxisListType

P = 128
D_MODEL, SEQ, DEPTH, NB, DEC, PAST = 1024, 512, 2, 8, 8, 1024
NS = NB * DEC
T = SEQ + NS
HALF = T // 2
KC = D_MODEL // P
TT = SEQ // P
EPS = 1e-6
HEADS_A = HEADS_B = 4
DK_A, DK_B, DV, DH = 32, 64, 64, 64
AH = 8
GROUPS = ((128, 1), (512, 4), (2048, 16))
RANK = 16
FE = 11
EXPERTS = (2, 8)
BLK = 16
NBLK = P // BLK
R = 6
SLOT = FE * P

JOBS = [("lr", 0), ("bf", 0), ("bf", 1), ("aq", 0), ("gu", 0), ("ak", 0), ("bq", 0), ("bq", 1),
        ("g", 0), ("g", 1), ("g", 2), ("g", 3)]
for _i in range(8 + 2):
    if _i < 8:
        JOBS.append(("c", _i))
    if 0 <= _i - 1 < 8:
        JOBS.append(("s", _i - 1))
    if 0 <= _i - 2:
        JOBS.append(("r", _i - 2))
NJ = len(JOBS)
JOB_AT = {j: n for n, j in enumerate(JOBS)}
HAS_W = [k not in ("gu", "s", "r") for k, _ in JOBS]
HAS_ACT = [k in ("bf", "bq", "g", "c", "s") for k, _ in JOBS]
HAS_DVE = [k not in ("c", "bq", "g") for k, _ in JOBS]
ACT_N = np.cumsum(HAS_ACT).tolist()
DVE_N = np.cumsum(HAS_DVE).tolist()
NFEAT = sum(HAS_W)
NV = 8
U_IN = NV + NFEAT
U_OUT = KC
U_EXP = 2 * FE + KC
RING0 = [0, U_IN + U_OUT + EXPERTS[0] * U_EXP]
NVU = NV - 2
UD0 = [0, NVU + U_OUT + EXPERTS[0] * U_EXP]
UD_ITEMS = UD0[1] + NVU + U_OUT
PF0 = [0, U_OUT + EXPERTS[0] * U_EXP]

ITEMS = ([("eb", 0), ("kd", 0), ("qt", 0)] + [("kt", i) for i in range(1, NBLK)]
         + [("pj", j) for j in range(BLK)] + [("sj", j) for j in range(DEC)])
NI = len(ITEMS)
ITEM_AT = {x: n for n, x in enumerate(ITEMS)}
CAP = 160
N_EXP = 8
PER_EXP = -(-T // CAP)
MAX_ITEMS = N_EXP + 2 * T // CAP
CAP2 = CAP - P
UNITS = []
for _f in range(FE + 1):
    if _f < FE:
        UNITS += [("gate", _f), ("up", _f)]
    if _f >= 1:
        UNITS.append(("down", _f - 1))
U_ITEM = len(UNITS)
UNIT_AT = {u: n for n, u in enumerate(UNITS)}
SLOT_USES = [len(range(s, U_ITEM, R)) for s in range(R)]
CT = 3
CT_HEADS = (4, 2, 2)

CONSTS = [("lnc", SEQ), ("smask", PAST), ("smask_new", NB * NS), ("cos", T), ("sin", T), ("w16", P + BLK),
          ("w8", NS + DEC), ("mask16", P), ("mask8", NS), ("ident", P), ("ones", P), ("bones", P),
          ("rot", P), ("reset", T), ("maskb", NB), ("riota", 8), ("before", P), ("slots", CAP), ("rows", 2)]
COFF, _o = {}, 0
for _n, _w in CONSTS:
    COFF[_n] = (_o, _w)
    _o += _w
NCONST = _o
VECS = [("g_mix", KC), ("g_ffn", KC), ("b_gate", 1), ("g_gla", 1), ("g_hgrn", 1), ("g_q", 1), ("g_k", 1)]
VOFF, _o = {}, 0
for _n, _w in VECS:
    VOFF[_n] = (_o, _w)
    _o += _w
NVEC = _o


def multiplicity(dist):
    n = np.zeros(dist.shape, np.float64)
    for window, dil in GROUPS:
        n += (dist >= 0) & (dist <= window) & (dist % dil == 0)
    return n


def log_mult(dist, valid):
    n = np.where(valid, multiplicity(dist), 0)
    return np.where(n > 0, np.log(np.maximum(n, 1)), -1e30).astype(np.float32)


def shape_constants():
    c = {}
    p = np.arange(P)[:, None]
    u = np.arange(SEQ)[None, :]
    c["lnc"] = log_mult(SEQ - P + p - u, SEQ - P + p - u >= 0)
    row = p % 32
    t = row % DEC
    live = row < 2 * DEC
    d = PAST + t - np.arange(PAST)[None, :]
    c["smask"] = np.where(live, log_mult(d, d >= 0), 0).astype(np.float32)
    key = np.arange(NS)[None, :]
    new = []
    for b in range(NB):
        d = t - key % DEC
        new.append(np.where(live, log_mult(d, (d >= 0) & (key // DEC == b)), 0).astype(np.float32))
    c["smask_new"] = np.concatenate(new, 1)
    pos = np.concatenate([np.arange(SEQ), np.tile(PAST + np.arange(DEC), NB)]).astype(np.float32)
    rot_dim = DH // 4
    inv = (np.float32(500000.0) ** (-np.arange(0, rot_dim, 2, dtype=np.float32) / np.float32(rot_dim))).astype(np.float32)
    ang = pos[:, None] * inv[None, :]
    cos, sin = np.ones((P, T), np.float32), np.zeros((P, T), np.float32)
    rot = np.zeros((P, P), np.float32)
    for h in range(2):
        for i in range(rot_dim // 2):
            a, b = h * DH + i, h * DH + rot_dim // 2 + i
            cos[a] = cos[b] = np.cos(ang[:, i])
            sin[a] = sin[b] = np.sin(ang[:, i])
            rot[b, a] = -1.0
            rot[a, b] = 1.0
    c["cos"], c["sin"], c["rot"] = cos, sin, rot
    c["w16"] = np.broadcast_to(np.arange(P + BLK)[None] % BLK == 0, (P, P + BLK)).astype(np.float32)
    c["w8"] = np.broadcast_to(np.arange(NS + DEC)[None] % DEC == 0, (P, NS + DEC)).astype(np.float32)
    q = np.arange(P)[None, :]
    c["mask16"] = ((p // BLK == q // BLK) & (q >= p)).astype(np.float32)
    q = np.arange(NS)[None, :]
    c["mask8"] = ((p // DEC == q // DEC) & (q >= p)).astype(np.float32)
    c["ident"] = np.eye(P, dtype=np.float32)
    c["ones"] = np.ones((P, P), np.float32)
    c["bones"] = (p // DH == np.arange(P)[None] // DH).astype(np.float32)
    reset = np.ones(T, np.float32)
    reset[0:SEQ:P] = 0
    reset[SEQ::DEC] = 0
    c["reset"] = np.broadcast_to(reset[None], (P, T))
    c["maskb"] = (p // DEC == np.arange(NB)[None]).astype(np.float32)
    c["riota"] = np.broadcast_to(8.0 - np.arange(8)[None], (P, 8))
    c["before"] = (p < np.arange(P)[None]).astype(np.float32)
    c["slots"] = np.broadcast_to(np.arange(CAP)[None], (P, CAP))
    c["rows"] = np.concatenate([p, P + p], 1)
    return np.ascontiguousarray(np.concatenate([c[n].astype(np.float32) for n, _ in CONSTS], 1))


def build(nc, d):
    ctx = ExitStack()
    with ctx:
        def sb(name, cols):
            return ctx.enter_context(nc.sbuf_tensor(name, [P, cols], F32))

        def sem(name):
            return ctx.enter_context(nc.semaphore(name))

        def tiles(ap, n):
            return ap.rearrange("p (n t) -> p n t", n=n)

        X = tiles(sb("residual", KC * T), KC)
        H = tiles(sb("normed_or_mixed", KC * T), KC)
        mix = H
        QK = tiles(sb("attn_qk", 8 * T), 8)
        V = tiles(sb("values", (TT + 1) * D_MODEL), TT + 1)
        LIN = sb("linear", 13 * T)
        Q, K, B = (tiles(LIN[:, i * 3 * T:(i + 1) * 3 * T], 3) for i in range(3))
        G = tiles(LIN[:, 9 * T:13 * T], 4)
        ring = tiles(sb("weight_ring", R * SLOT), R)
        C = sb("constants", NCONST)
        const = {n: C[:, o:o + w] for n, (o, w) in COFF.items()}
        VEC = sb("vectors", DEPTH * NVEC)
        LB = sb("lower_bounds", 32)
        WU = sb("gla_gate_up", DEPTH * P)
        SM = sb("small", 64 + CT * 12)
        WRT = sb("router", 64)
        SCR = sb("scratch", 12736)

        def vec(L, name):
            o, w = VOFF[name]
            return VEC[:, L * NVEC + o:L * NVEC + o + w]

        def carve(base, *sizes):
            out, o = [], 0
            for s in sizes:
                out.append(base[:, o:o + s])
                o += s
            return out

        eps_col = SM[:, 32:33]
        negmax = SM[:, 40:48]
        den = SM[:, 48:56]
        rden = SM[:, 56:64]
        ebl = tiles(SM[:, 64:64 + CT * 12], CT)
        lb = LB[:, 0:4]
        oml = LB[:, 4:8]
        e0, e1s, rinvs, qn = (tiles(x, 3) for x in carve(SCR, 3 * T, 3 * T, 3 * T, 3 * T))
        rtmp = SCR[:, 12 * T:13 * T]
        lr_sb = SCR[0:RANK, 13 * T:14 * T]
        sq = tiles(SCR[:, FE * T:(FE + 4) * T], 4)
        rinv = SCR[:, 4 * T:5 * T]
        (qe_, kdt_, kt_, qt, dring_, a_, kd, vbd, pring_) = carve(
            SCR, CT * T, (TT + 1) * P, (NBLK - 1) * SEQ, SEQ, 3 * T, 4 * T, T, 512, 2 * T)
        Qe = tiles(qe_, CT)
        KdT = tiles(kdt_, TT + 1)
        Kt = kt_.rearrange("p (i c s) -> p i c s", i=NBLK - 1, c=TT)
        Dr = tiles(dring_, 3)
        A = tiles(a_, 4)
        Pr = tiles(pring_, 2)
        osq, orinv = Pr[:, 0, :], Pr[:, 1, :]
        S = H[:, 4:8, :].rearrange("p a t -> p (a t)")[:, 0:CT * 4 * DV].rearrange("p (c k v) -> p c k v", c=CT, k=4)
        S0 = H[:, 4:8, :].rearrange("p a t -> p (a t)")[:, 768:768 + CT * NB * DV].rearrange(
            "p (c b v) -> p c b v", c=CT, b=NB)
        (p_, pt_, *pieces) = carve(SCR, 2 * (PAST + NS), 2 * 9 * P, 2048, 2048, 2048, 2048)
        pieces += carve(LIN, 2048, 2048, 2048)
        NPC = len(pieces)
        Pp = tiles(p_[:, 0:2048], 4)
        Ps = tiles(p_, 2)
        PTp = tiles(pt_[:, 0:1024], 2)
        PTs = tiles(pt_, 2)
        Qs = LIN[:, 6144:7168].rearrange("p (b h q) -> p b h q", b=NB, h=4)
        hid_, ft_ = carve(SCR, FE * T, 4 * T)
        hid, ft = tiles(hid_, FE), tiles(ft_, 4)
        H_tok = V
        xg_, hidg_, tg_, yt_, ytok_, sel_, selw_, selt = carve(
            SCR, KC * CAP, FE * CAP, 2 * CAP, KC * CAP, 2 * D_MODEL, (TT + 1) * CAP, 2 * T, T)
        Xg, hidg, tg, Yt = tiles(xg_, KC), tiles(hidg_, FE), tiles(tg_, 2), tiles(yt_, KC)
        Ytok, Sel, SelW = tiles(ytok_, 2), tiles(sel_, TT + 1), tiles(selw_, 2)
        rows4 = tiles(LIN[:, 0:4 * T], 4)
        RW = LIN[:, 4 * T:4 * T + 512]
        item_tab = ctx.enter_context(nc.sbuf_tensor("item_table", [1, MAX_ITEMS + 1], mybir.dt.int32))
        sqf = ft

        ps = ctx.enter_context(nc.psum_tensor("ps", [P, 8, 512], F32))

        def pair(k):
            return ps[:, 2 * k:2 * k + 2, 0:HALF]

        def split(ap):
            return ap.rearrange("p (a t) -> p a t", a=2)

        x_in, c_in, w_land = sem("x_in"), sem("consts_in"), [sem(f"weights_in{i}") for i in range(R)]
        s0_in = [sem("gla_state_in"), sem("hgrn_state_in")]
        piece_in = [sem(f"cache_piece_in{i}") for i in range(NPC)]
        stored_s, shifted, stored_y = sem("states_out"), sem("caches_shifted"), sem("y_out")
        stored_kv = sem("new_kv_out")
        lb_exp, lb_ready, eps_ready, kt_zero, qs_zero = (sem(n) for n in (
            "lb_exp", "lb_ready", "eps_ready", "kt_zeroed", "qs_zeroed"))
        sq_ready, sq_used, rinv_ready, h_ready = (sem(n) for n in ("sq_ready", "sq_used", "rinv_ready", "h_ready"))
        v_ready, v_half = sem("v_ready"), sem("v_product")
        unit_done, pe_job, act_job, dve_job = (sem(n) for n in ("unit_done", "pe_job", "act_job", "dve_job"))
        out_evac = sem("out_evac")
        dch, ach = sem("dve_chain"), sem("act_chain")
        lf_abs, lf_ready, b_ready = sem("lf_abs"), sem("logf_ready"), sem("b_ready")
        diff_ready, exp_ready, term_ready = sem("diff_ready"), sem("exp_ready"), sem("term_ready")
        prod_used, off_done, diag_done, samp_done = (sem(n) for n in ("prod_used", "off_done", "diag_done", "samp_done"))
        kdt_ps, kdt_ready, a_ready, as_ready = (sem(n) for n in ("kdt_ps", "kdt_ready", "a_ready", "as_ready"))
        upd_done, s_ready, vbd_ready, vbd_used, supd_done, sn_ready = (sem(n) for n in (
            "upd_done", "s_ready", "vbd_ready", "vbd_used", "supd_done", "sn_ready"))
        o_done, osq_ready, oss_done, orinv_ready, mixl_ready = (sem(n) for n in (
            "o_done", "osq_ready", "oss_done", "orinv_ready", "mixl_ready"))
        sc_done, sc_free, mx_ready, p_ready, pn_ready, pt_ps, pt_ready, pv_done, mixc_ready = (sem(n) for n in (
            "sc_done", "sc_free", "mx_ready", "p_ready", "pn_ready", "pt_ps", "pt_ready", "pv_done", "mixc_ready"))
        qs_ready = sem("qs_ready")
        ssc_done, ssc_free, smx_ready, sp_ready, spn_ready, spt_ps, spt_ready, spv_done, smix_ready = (sem(n) for n in (
            "ssc_done", "ssc_free", "smx_ready", "sp_ready", "spn_ready", "spt_ps", "spt_ready", "spv_done", "smix_ready"))
        sig_ready = sem("sig_ready")
        htok_ps, htok_ready, rl_done, rexp, rexp_done, chosen, ranked, coded, rows_ps, rows_ready, items_ready = (
            sem(n) for n in ("htok_ps", "htok_ready", "logits_done", "gate_diff", "gate_exp", "chosen", "ranked", "coded",
                             "rows_ps", "rows_ready", "items_ready"))
        silu_ready, hid_ready, yt_ready, ytok_ps, ytok_ready = (sem(n) for n in (
            "silu_ready", "hid_ready", "yt_ready", "ytok_ps", "ytok_ready"))
        sel_ready, selw_ready, gathered, xg_ready, scattered, experts_done = (sem(n) for n in (
            "sel_ready", "selw_ready", "gathered", "xg_ready", "scattered", "experts_done"))

        N_CI = 6
        block = ctx.enter_context(nc.Block())

        def ud_ffn(L):
            return UD0[L] + NVU + U_OUT

        def pf_ffn(L):
            return PF0[L] + U_OUT

        released = []
        for L in range(DEPTH):
            for half in range(2):
                released += [(unit_done, UD0[L] + 3 * half + u + 1) for u in range(3)] + [(v_half, 10 * L + 5 * half + 5)]
            released += [(pe_job, L * NJ + n + 1) for n in range(NJ) if HAS_W[n]]
            released += [(unit_done, UD0[L] + NVU + u + 1) for u in range(U_OUT + (EXPERTS[0] * U_EXP if L == 0 else 0))]
        landings = [len(range(s, len(released), R)) for s in range(R)]

        def cache_piece(L, b, part):
            return (L * NB + b) * 4 + part, (b * 4 + part) % NPC

        last_piece, piece_count = {}, {}
        uses, user = [0] * NPC, [None] * NPC
        for L in range(DEPTH):
            for b in range(NB):
                for part in range(4):
                    m, slot = cache_piece(L, b, part)
                    last_piece[m] = user[slot]
                    user[slot] = (L, b, part)
                    uses[slot] += 1
                    piece_count[m] = uses[slot]

        def piece_landed(eng, L, b, part):
            m, slot = cache_piece(L, b, part)
            eng.wait_ge(piece_in[slot], 16 * piece_count[m])
            return pieces[slot]

        def chunk_rows(h, n):
            w = P // n
            return slice(h * w, h * w + w)

        @block.sync
        def _(sp):
            sp.dma_start(X[:, :, :], d["x"]).then_inc(x_in, 16)
            for dst, src in ((C[:, :], d["consts"]), (VEC[:, :], d["vecs"]), (LB[:, 16:20], d["lb_logits"]),
                             (WU[0:RANK, :], d["w_up"]), (WRT[:, :], d["w_router"])):
                sp.dma_start(dst, src).then_inc(c_in, 16)

            def slot_for(n):
                if n >= R:
                    s, v = released[n - R]
                    sp.wait_ge(s, v)
                return n % R

            old_k, new_k = (d[x].rearrange("l b p h s -> (l b) p h s") for x in ("kcache", "ok_s"))
            old_v, new_v = (d[x].rearrange("l b p c e -> (l b) p c e") for x in ("vcache", "ov_s"))

            def shift(q, values):
                if values:
                    o, n_ = (x[bass.ds(q, 1)].rearrange("o p c e -> (o p) (c e)") for x in (old_v, new_v))
                    sp.dma_start(n_[0:P - 1], o[1:P]).then_inc(shifted, 16)
                else:
                    o, n_ = (x[bass.ds(q, 1)].rearrange("o p h s -> (o p) h s") for x in (old_k, new_k))
                    sp.dma_start(n_[:, :, 0:PAST - DEC], o[:, :, DEC:PAST]).then_inc(shifted, 16)

            for L in range(DEPTH):
                n = RING0[L]
                for u in range(NV):
                    s = slot_for(n)
                    sp.dma_start(ring[:, s, 0:1024], d["w_v"][L, u]).then_inc(w_land[s], 16)
                    n += 1
                f = 0
                for kind, i in JOBS:
                    if kind in ("gu", "s", "r"):
                        continue
                    s = slot_for(n)
                    if kind == "lr":
                        sp.dma_start(ring[:, s, 0:KC * RANK], d["w_lr"][L]).then_inc(w_land[s], 16)
                    else:
                        sp.dma_start(ring[:, s, 0:1024], d["w_feat"][L, f]).then_inc(w_land[s], 16)
                        f += 1
                    n += 1
                    if f % 3 == 0 and 1 <= f // 3 <= 6:
                        k = f // 3 - 1
                        shift((0, 13)[L] + k // 2, k % 2)
                for u in range(U_OUT):
                    s = slot_for(n)
                    sp.dma_start(ring[:, s, 0:1024], d["w_out"][L, u]).then_inc(w_land[s], 16)
                    n += 1
                    if u == R - 1:
                        sp.wait_ge(sn_ready, CT * (L + 1))
                        sp.wait_ge(mixl_ready, 4 * (L + 1))
                        for b in range(NB):
                            for part in range(4):
                                m, slot = cache_piece(L, b, part)
                                if b * 4 + part >= NPC:
                                    _, bb, pp = last_piece[m]
                                    sp.wait_ge(*((ssc_done, L * NB + bb + 1) if pp < 2 else (spv_done, L * NB + bb + 1)))
                                if part < 2:
                                    sp.dma_start(tiles(pieces[slot], 2), d["kcache"][L, b][:, 2 * part:2 * part + 2]).then_inc(piece_in[slot], 16)
                                else:
                                    k = 4 * (part - 2)
                                    sp.dma_start(tiles(pieces[slot], 4), d["vcache"][L, b][:, k:k + 4]).then_inc(piece_in[slot], 16)
                if L:
                    continue
                base_ud, base_ring = ud_ffn(L), n
                with sp.Fori(0, EXPERTS[L]) as e:
                    for j in range(U_EXP):
                        s = (base_ring + j) % R
                        sp.wait_ge(unit_done, e * U_EXP + (base_ud + j - R + 1))
                        if j < 2 * FE:
                            src = d["w_gu"][bass.ds(e * (2 * FE) + j, 1)].rearrange("o p c -> (o p) c")
                            sp.dma_start(ring[:, s, 0:1024], src).then_inc(w_land[s], 16)
                            if j % 2 == 0 and j < 20:
                                shift(e * 5 + (3 + j // 4), (j // 2) % 2)
                        else:
                            src = d["w_dn"][bass.ds(e * KC + (j - 2 * FE), 1)].rearrange("o p c -> (o p) c")
                            sp.dma_start(ring[:, s, :], src).then_inc(w_land[s], 16)
            sp.wait_ge(unit_done, UD_ITEMS)
            sp.wait_ge(items_ready, 1)
            n_items = sp.value_load(item_tab[0:1, MAX_ITEMS:MAX_ITEMS + 1], min_val=N_EXP, max_val=MAX_ITEMS)
            with sp.Fori(0, n_items) as i:
                x = sp.value_load(item_tab[0:1, bass.ds(i, 1)], min_val=0, max_val=N_EXP - 1)
                for j, (kind, f) in enumerate(UNITS):
                    s = j % R
                    last = j - R if j >= R else max(range(s, U_ITEM, R)) - U_ITEM
                    sp.wait_ge(unit_done, i * U_ITEM + (UD_ITEMS + last + 1))
                    if kind == "down":
                        src = d["w_dn_moe"][bass.ds(x * FE + f, 1)]
                    else:
                        src = d["w_gu"][bass.ds(x * (2 * FE) + (EXPERTS[0] * 2 * FE + 2 * f + (kind == "up")), 1)]
                    sp.dma_start(ring[:, s, 0:1024], src.rearrange("o p c -> (o p) c")).then_inc(w_land[s], 16)
            sp.wait_ge(experts_done, 1)
            sp.wait_ge(shifted, 16 * 2 * DEPTH * NB)
            sp.dma_start(d["y"], X[:, :, :]).then_inc(stored_y, 16)
            sp.wait_ge(stored_y, 16)

        @block.gpsimd
        def _(pool):
            pool.wait_ge(c_in, 16 * 5)
            for L in range(DEPTH):
                pool.wait_ge(pe_job, (L + 1) * NJ)
                pool.dma_start(S0[:, 0, :, :], d["s0_gla"][L]).then_inc(s0_in[0], 16)
                pool.dma_start(S0[:, 1:3, :, :], d["s0_hgrn"][L]).then_inc(s0_in[1], 16)
                pool.wait_ge(dve_job, (L + 1) * DVE_N[-1])
                pool.wait_ge(v_ready, 10 * (L + 1))
                pool.dma_start(d["ok_p"][L], QK[:, 4:8, 0:SEQ]).then_inc(stored_kv, 16)
                pool.dma_start(d["ov_p"][L], V[:, 0:TT, 512:1024]).then_inc(stored_kv, 16)
                pool.wait_ge(dve_job, (L + 1) * DVE_N[-1])
                nc.gpsimd.memset(kt_, 0.0).then_inc(kt_zero, 1)
                for ct in range(CT):
                    pool.wait_ge(b_ready, L * CT + ct + 1)
                    Bp = B[:, ct, 0:SEQ].rearrange("p (c s) -> p c s", c=TT)
                    Bs = B[:, ct, SEQ:T].rearrange("p (b s) -> p b s", b=NB)
                    Bb = B[:, ct, 0:SEQ].rearrange("p (n s) -> p n s", s=BLK)
                    for kind, i in ITEMS:
                        it = L * CT * NI + ct * NI + ITEM_AT[(kind, i)]
                        if kind == "eb":
                            continue
                        D = Dr[:, it % 3, :]
                        if it >= 3:
                            pool.wait_ge(term_ready, it - 2)
                        if kind == "kd" and ct == 0:
                            pool.wait_ge(b_ready, L * CT + CT)
                        Dp = D[:, 0:SEQ].rearrange("p (c s) -> p c s", c=TT)
                        Ds = D[:, SEQ:T].rearrange("p (b s) -> p b s", b=NB)
                        if kind == "kd":
                            nc.gpsimd.tensor_tensor(Dp, Bp[:, :, P - 1:P].to_broadcast([P, TT, P]), Bp, ALU.subtract)
                            op = nc.gpsimd.tensor_tensor(Ds, Bs[:, :, DEC - 1:DEC].to_broadcast([P, NB, DEC]), Bs, ALU.subtract)
                        elif kind == "qt":
                            for c in range(TT):
                                b1 = Bp[:, c, BLK:P].rearrange("p (n s) -> p n s", s=BLK)
                                r1 = Bp[:, c, 0:P - BLK].rearrange("p (n s) -> p n s", s=BLK)[:, :, BLK - 1:BLK]
                                op = nc.gpsimd.tensor_tensor(
                                    Dp[:, c, BLK:P].rearrange("p (n s) -> p n s", s=BLK), b1,
                                    r1.to_broadcast([P, NBLK - 1, BLK]), ALU.subtract)
                        elif kind == "kt":
                            w = BLK * i
                            op = nc.gpsimd.tensor_tensor(Dp[:, :, 0:w], Bp[:, :, w - 1:w].to_broadcast([P, TT, w]),
                                                         Bp[:, :, 0:w], ALU.subtract)
                        elif kind == "pj":
                            w = BLK - i
                            op = nc.gpsimd.tensor_tensor(
                                D[:, 0:32 * w].rearrange("p (n s) -> p n s", s=w), Bb[:, :, i:BLK],
                                Bb[:, :, i:i + 1].to_broadcast([P, SEQ // BLK, w]), ALU.subtract)
                        else:
                            w = DEC - i
                            op = nc.gpsimd.tensor_tensor(
                                D[:, 0:NB * w].rearrange("p (n s) -> p n s", s=w), Bs[:, :, i:DEC],
                                Bs[:, :, i:i + 1].to_broadcast([P, NB, w]), ALU.subtract)
                        op.then_inc(diff_ready, 1)
                    for h in range(CT_HEADS[ct]):
                        hh = (0, 4, 6)[ct] + h
                        if L * 8 + hh >= 1:
                            pool.wait_ge(vbd_used, L * 8 + hh)
                        v = V[0:NS, TT, hh * DV:hh * DV + DV].rearrange("p (o v) -> p o v", o=1)
                        nc.gpsimd.tensor_tensor(
                            vbd[0:NS, :].rearrange("p (b v) -> p b v", b=NB), v.to_broadcast([NS, NB, DV]),
                            const["maskb"][0:NS, :].rearrange("p (b o) -> p b o", o=1).to_broadcast([NS, NB, DV]),
                            ALU.mult).then_inc(vbd_ready, 1)
                pool.wait_ge(s_ready, CT * (L + 1))
                pool.dma_start(d["os_gla_p"][L], S[:, 0, 3, :]).then_inc(stored_s, 16)
                pool.dma_start(d["os_hgrn_p"][L], S[:, 1:3, 3, :]).then_inc(stored_s, 16)
                pool.wait_ge(sn_ready, CT * (L + 1))
                pool.dma_start(d["os_gla_s"][L], S0[:, 0, :, :]).then_inc(stored_s, 16)
                pool.dma_start(d["os_hgrn_s"][L], S0[:, 1:3, :, :]).then_inc(stored_s, 16)
                for b in range(NB):
                    s = SEQ + DEC * b
                    pool.dma_start(d["ok_s"][L, b][:, :, PAST - DEC:PAST], QK[:, 4:8, s:s + DEC]).then_inc(stored_kv, 16)
                    pool.dma_start(d["ov_s"][L, b][P - 1], V[DEC * b:DEC * b + DEC, TT, 512:1024]).then_inc(stored_kv, 16)
                pool.wait_ge(stored_kv, (L + 1) * 16 * (2 + 2 * NB))
                pool.wait_ge(stored_s, (L + 1) * 64)

        @block.scalar
        def _(act):
            chain = [0]

            def link(op):
                op.then_inc(ach, 1)
                chain[0] += 1
                act.wait_ge(ach, chain[0])

            def norm(k, buf, out, wait_x):
                for c in range(KC):
                    wait_x(c)
                    if c >= 4:
                        act.wait_ge(sq_used, KC * k + c - 3)
                    nc.scalar.activation(buf[:, c % 4, :], X[:, c, :], ACT.Square).then_inc(sq_ready, 1)
                act.wait_ge(sq_used, KC * k + KC)
                link(nc.scalar.activation(split(out), pair(0), ACT.Ln, bias=eps_col, scale=1.0 / D_MODEL))
                nc.scalar.activation(out, out, ACT.Exp, scale=-0.5).then_inc(rinv_ready, 1)

            act.wait_ge(c_in, 16 * 5)
            act.wait_ge(lb_ready, 1)
            nc.scalar.activation(LB[:, 20:24], LB[:, 24:28], ACT.Exp).then_inc(lb_exp, 1)
            act.wait_ge(eps_ready, 1)
            for L in range(DEPTH):
                def wait_mix(c, L=L):
                    if L == 0:
                        act.wait_ge(x_in, 16)
                    else:
                        act.wait_ge(out_evac, pf_ffn(0) + U_EXP + 2 * FE + c + 1)
                norm(2 * L, sq, rinv, wait_mix)
                for n in range(10):
                    act.wait_ge(v_half, 10 * L + n + 1)
                    half, tt = n // 5, n % 5
                    rows = P if tt < TT else NS
                    if L and n == 0:
                        act.wait_ge(stored_kv, 16 * (2 + 2 * NB))
                    nc.scalar.activation(V[0:rows, tt, half * 512:half * 512 + 512], ps[0:rows, n % 8, :],
                                         ACT.Copy).then_inc(v_ready, 1)
                for n, (kind, i) in enumerate(JOBS):
                    if not HAS_ACT[n]:
                        continue
                    act.wait_ge(pe_job, L * NJ + n + 1)
                    src = pair((n + 1) % 4)
                    if kind in ("bf", "bq", "g"):
                        act.wait_ge(dve_job, L * DVE_N[-1] + (DVE_N[n - 3] if n >= 3 else 0)) if n >= 3 else None
                        if kind == "bf":
                            nc.scalar.activation(split(e1s[:, n % 3, :]), src, ACT.Exp)
                            op = nc.scalar.activation(split(e0[:, n % 3, :]), src, ACT.Exp, scale=-1.0)
                        else:
                            dst = Q[:, 1 + i, :] if kind == "bq" else G[:, i, :]
                            op = nc.scalar.activation(split(dst), src, ACT.Silu)
                        op.then_inc(act_job, 1)
                    elif kind == "c":
                        if i < 3:
                            act.wait_ge(dve_job, L * DVE_N[-1] + DVE_N[JOB_AT[("g", 3)]])
                        else:
                            act.wait_ge(dve_job, L * DVE_N[-1] + DVE_N[JOB_AT[("s", i - 3)]])
                        nc.scalar.activation(split(e0[:, i % 3, :]), src, ACT.Copy)
                        nc.scalar.activation(split(e1s[:, i % 3, :]), src, ACT.Square).then_inc(act_job, 1)
                    else:
                        link(nc.scalar.activation(split(rinvs[:, i % 3, :]), src, ACT.Ln, bias=eps_col, scale=1.0 / DH))
                        nc.scalar.activation(rinvs[:, i % 3, :], rinvs[:, i % 3, :], ACT.Exp, scale=-0.5).then_inc(act_job, 1)
                act.wait_ge(dve_job, (L + 1) * DVE_N[-1])
                act.wait_ge(lf_abs, L + 1)
                link(nc.scalar.activation(Dr[:, 0, :], Dr[:, 0, :], ACT.Exp, scale=-1.0))
                nc.scalar.activation(Dr[:, 0, :], Dr[:, 0, :], ACT.Ln, bias=1.0).then_inc(lf_ready, 1)
                nc.scalar.activation(Dr[:, 1, :], B[:, 1, :], ACT.Ln).then_inc(lf_ready, 1)
                nc.scalar.activation(Dr[:, 2, :], B[:, 2, :], ACT.Ln).then_inc(lf_ready, 1)
                diffs = L * CT * (NI - 1)
                for ct in range(CT):
                    for kind, i in ITEMS:
                        n = L * CT * NI + ct * NI + ITEM_AT[(kind, i)]
                        D = Dr[:, n % 3, :]
                        if kind == "eb":
                            act.wait_ge(b_ready, CT * L + CT)
                            if n >= 3:
                                act.wait_ge(term_ready, n - 2)
                            nc.scalar.activation(D, B[:, ct, :], ACT.Exp).then_inc(exp_ready, 1)
                            continue
                        diffs += 1
                        act.wait_ge(diff_ready, diffs)
                        if kind == "kd":
                            v = D
                        elif kind == "qt":
                            v = D[:, 0:SEQ].rearrange("p (c s) -> p c s", c=TT)[:, :, BLK:P]
                        elif kind == "kt":
                            v = D[:, 0:SEQ].rearrange("p (c s) -> p c s", c=TT)[:, :, 0:BLK * i]
                        elif kind == "pj":
                            v = D[:, 0:32 * (BLK - i)]
                        else:
                            v = D[:, 0:NB * (DEC - i)]
                        nc.scalar.activation(v, v, ACT.Exp).then_inc(exp_ready, 1)
                        if (kind, i) == ("kt", 3):
                            act.wait_ge(kdt_ps, CT * L + ct + 1)
                            nc.scalar.activation(KdT[:, 0:TT, :], ps[:, 0, :].rearrange("p (c s) -> p c s", c=TT), ACT.Copy)
                            nc.scalar.activation(KdT[0:NS, TT, :], ps[0:NS, 1, 0:P], ACT.Copy).then_inc(kdt_ready, 1)
                    for k in range(CT_HEADS[ct] // 2):
                        m = (0, 2, 3)[ct] + k
                        bp, bs = 3 + 2 * k, 4 + 2 * k
                        act.wait_ge(o_done, 4 * L + m + 1)
                        if k:
                            act.wait_ge(mixl_ready, 4 * L + m)
                        act.wait_ge(term_ready, L * CT * NI + ct * NI + NI)
                        nc.scalar.activation(osq[:, 0:SEQ], ps[:, bp, :], ACT.Square)
                        nc.scalar.activation(osq[:, SEQ:T], ps[:, bs, 0:NS], ACT.Square).then_inc(osq_ready, 1)
                        act.wait_ge(oss_done, 4 * L + m + 1)
                        nc.scalar.activation(orinv[:, 0:SEQ], ps[:, 7, :], ACT.Ln, bias=eps_col, scale=1.0 / DV)
                        link(nc.scalar.activation(orinv[:, SEQ:T], ps[:, 0, 0:NS], ACT.Ln, bias=eps_col, scale=1.0 / DV))
                        nc.scalar.activation(orinv, orinv, ACT.Exp, scale=-0.5).then_inc(orinv_ready, 1)
                n0 = 32 * L
                for n in range(32 + 3):
                    if n < 32:
                        w = P * (n % 4 + 1)
                        act.wait_ge(mx_ready, n0 + n + 1)
                        nc.scalar.activation(Pp[:, n % 4, 0:w], Pp[:, n % 4, 0:w], ACT.Exp, bias=negmax[:, n % 4:n % 4 + 1],
                                             accum_out=den[:, n % 4:n % 4 + 1]).then_inc(p_ready, 1)
                    k = n - 2
                    if 0 <= k < 32:
                        w = P * (k % 4 + 1)
                        act.wait_ge(pt_ps, n0 + k + 1)
                        if k >= 2:
                            act.wait_ge(pv_done, n0 + k - 1)
                        nc.scalar.activation(PTp[:, k % 2, 0:w], ps[:, 2 + k % 2, 0:w], ACT.Copy).then_inc(pt_ready, 1)
                    k = n - 3
                    if 0 <= k < 32 and k % 8 == 7:
                        act.wait_ge(pv_done, n0 + k + 1)
                        hp = k // 8
                        if hp == 0:
                            act.wait_ge(stored_s, 64 * (L + 1))
                        nc.scalar.activation(mix[:, 4 + hp, 0:SEQ], ps[:, 4 + hp % 2, :], ACT.Copy).then_inc(mixc_ready, 1)
                for b in range(NB + 1):
                    if b < NB:
                        n = NB * L + b
                        act.wait_ge(smx_ready, n + 1)
                        nc.scalar.activation(Ps[:, b % 2, :], Ps[:, b % 2, :], ACT.Exp, bias=negmax[:, 4 + b % 2:5 + b % 2],
                                             accum_out=den[:, 4 + b % 2:5 + b % 2]).then_inc(sp_ready, 1)
                    if b >= 1:
                        n = NB * L + b - 1
                        act.wait_ge(spt_ps, n + 1)
                        pt = PTs[:, (b - 1) % 2, :]
                        nc.scalar.activation(pt[:, 0:1024], ps[:, 3:5, :].rearrange("p a t -> p (a t)"), ACT.Copy)
                        nc.scalar.activation(pt[0:NS, 1024:1152], ps[0:NS, 5, 0:P], ACT.Copy).then_inc(spt_ready, 1)
                norm(2 * L + 1, sqf, hid[:, 0, :], lambda c: act.wait_ge(out_evac, PF0[L] + c + 1))
                if L == 0:
                    with act.Fori(0, EXPERTS[L]) as e:
                        for i in range(FE):
                            act.wait_ge(unit_done, e * U_EXP + (ud_ffn(L) + 2 * i + 1))
                            if i >= 2:
                                act.wait_ge(out_evac, e * U_EXP + (pf_ffn(L) + 2 * i - 2))
                            nc.scalar.activation(split(ft[:, i % 2, :]), pair((2 * i) % 4), ACT.Silu).then_inc(sig_ready, 1)
            act.wait_ge(stored_kv, 2 * 16 * (2 + 2 * NB))
            for tt in range(TT + 1):
                rows = P if tt < TT else NS
                act.wait_ge(htok_ps, tt + 1)
                k = 2 * (tt % 2)
                nc.scalar.activation(H_tok[0:rows, tt, :].rearrange("p (a c) -> p a c", a=2), ps[0:rows, 4 + k:6 + k, :],
                                     ACT.Copy).then_inc(htok_ready, 1)
            act.wait_ge(rexp, 1)
            nc.scalar.activation(RW[:, 80:85], RW[:, 80:85], ACT.Exp).then_inc(rexp_done, 1)

            def copy_xg(count):
                act.wait_ge(gathered, count)
                for k in range(0, KC, 3):
                    m = min(3, KC - k)
                    op = nc.scalar.activation(Xg[:, k:k + m, :], ps[:, 3 + k // 3, 0:m * CAP].rearrange("p (k s) -> p k s", k=m), ACT.Copy)
                op.then_inc(xg_ready, 1)

            copy_xg(1)
            act.wait_ge(items_ready, 1)
            n_items = act.value_load(item_tab[0:1, MAX_ITEMS:MAX_ITEMS + 1], min_val=N_EXP, max_val=MAX_ITEMS)
            with act.Fori(0, n_items) as i:
                for f in range(FE):
                    act.wait_ge(unit_done, i * U_ITEM + (UD_ITEMS + UNIT_AT[("gate", f)] + 1))
                    if f >= 2:
                        act.wait_ge(hid_ready, i * FE + (f - 1))
                    nc.scalar.activation(tg[:, f % 2, :], ps[:, 3 + 2 * (f % 2), 0:CAP], ACT.Silu).then_inc(silu_ready, 1)
                act.wait_ge(unit_done, i * U_ITEM + (UD_ITEMS + U_ITEM))
                for k in range(0, KC, 3):
                    m = min(3, KC - k)
                    op = nc.scalar.activation(Yt[:, k:k + m, :], ps[:, k // 3, 0:m * CAP].rearrange("p (k s) -> p k s", k=m), ACT.Copy)
                op.then_inc(yt_ready, 1)
                copy_xg(i + 2)
                act.wait_ge(ytok_ps, i + 1)
                nc.scalar.activation(Ytok[:, 0, :].rearrange("p (a c) -> p a c", a=2), ps[:, 6:8, :], ACT.Copy)
                nc.scalar.activation(Ytok[0:CAP2, 1, :].rearrange("p (a c) -> p a c", a=2), ps[0:CAP2, 0:2, :], ACT.Copy).then_inc(ytok_ready, 1)

        @block.tensor
        def _(pe):
            def gemm(out_pair, w, rhs, k, kn):
                for a in range(2):
                    op = nc.tensor.matmul(out_pair[:, a, :], w, rhs[:, a * HALF:a * HALF + HALF], start=k == 0, stop=k == kn - 1)
                return op

            def landed(n):
                pe.wait_ge(w_land[n % R], 16 * (n // R + 1))
                return ring[:, n % R, :]

            def norm(k, buf):
                for c in range(KC):
                    pe.wait_ge(sq_ready, KC * k + c + 1)
                    gemm(pair(0), const["ones"], buf[:, c % 4, :], c, KC).then_inc(sq_used, 1)

            pe.wait_ge(c_in, 16 * 5)
            for L in range(DEPTH):
                if L:
                    pe.wait_ge(out_evac, pf_ffn(0) + EXPERTS[0] * U_EXP)
                norm(2 * L, sq)
                ring_n = RING0[L]
                for half in range(2):
                    for u in range(4):
                        w = landed(ring_n)[:, 0:1024].rearrange("p (k c) -> p k c", k=2)
                        ring_n += 1
                        for kk in range(2):
                            k = 2 * u + kk
                            if half == 0:
                                pe.wait_ge(h_ready, 2 * L * KC + k + 1)
                            for tt in range(5):
                                n = half * 5 + tt
                                if k == 0 and n >= 8:
                                    pe.wait_ge(v_ready, 10 * L + n - 7)
                                rows = P if tt < TT else NS
                                op = nc.tensor.matmul(ps[0:rows, n % 8, :], H[:, k, tt * P:tt * P + rows], w[:, kk, :],
                                                      start=k == 0, stop=k == KC - 1)
                                if k == KC - 1:
                                    op.then_inc(v_half, 1)
                        if u < 3:
                            op.then_inc(unit_done, 1)
                for n, (kind, i) in enumerate(JOBS):
                    out = pair((n + 1) % 4)
                    if n < 4:
                        pe.wait_ge(v_ready, 10 * L + (4, 6, 8, 10)[n])
                    else:
                        m = n - 4
                        if JOBS[m][0] in ("bf", "bq", "g", "c", "s"):
                            pe.wait_ge(act_job, L * ACT_N[-1] + ACT_N[m])
                        else:
                            pe.wait_ge(dve_job, L * DVE_N[-1] + DVE_N[m])
                    if HAS_W[n]:
                        w = landed(ring_n)
                        ring_n += 1
                        cols = RANK if kind == "lr" else P
                        w = w[:, 0:KC * cols].rearrange("p (k c) -> p k c", k=KC)
                        for k in range(KC):
                            op = gemm(out[0:cols], w[:, k, :], H[:, k, :], k, KC)
                    elif kind == "gu":
                        pe.wait_ge(dve_job, L * DVE_N[-1] + DVE_N[JOB_AT[("lr", 0)]])
                        op = gemm(out, WU[0:RANK, L * P:L * P + P], lr_sb, 0, 1)
                    elif kind == "s":
                        pe.wait_ge(act_job, L * ACT_N[-1] + ACT_N[JOB_AT[("c", i)]])
                        op = gemm(out, const["bones"], e1s[:, i % 3, :], 0, 1)
                    else:
                        pe.wait_ge(dve_job, L * DVE_N[-1] + DVE_N[JOB_AT[("s", i)]])
                        op = gemm(out, const["rot"], qn[:, i % 3, :], 0, 1)
                    op.then_inc(pe_job, 1)

                pe.wait_ge(s0_in[0], 16 * (L + 1))
                pe.wait_ge(s0_in[1], 16 * (L + 1))
                for ct in range(CT):
                    nh = CT_HEADS[ct]
                    it0 = L * CT * NI + ct * NI
                    heads = [(h, chunk_rows(h, nh), ((0, 4, 6)[ct] + h) * DV) for h in range(nh)]
                    pe.wait_ge(term_ready, it0 + ITEM_AT[("kd", 0)] + 1)
                    if ct == 0:
                        pe.wait_ge(dve_job, (L + 1) * DVE_N[-1])
                    else:
                        pe.wait_ge(mixl_ready, 4 * L + (2, 3)[ct - 1])
                    for c in range(TT):
                        nc.tensor.transpose(ps[:, 0, c * P:c * P + P], kd[:, c * P:c * P + P], const["ident"])
                    nc.tensor.transpose(ps[0:NS, 1, 0:P], kd[:, SEQ:T], const["ident"]).then_inc(kdt_ps, 1)
                    for i in range(1, NBLK):
                        pe.wait_ge(term_ready, it0 + ITEM_AT[("kt", i)] + 1)
                        for c in range(TT):
                            for h, r, _ in heads:
                                at = c * P + i * BLK
                                op = nc.tensor.matmul(ps[:, 4 + h, at:at + BLK], Kt[r, i - 1, c, :], qt[r, at:at + BLK],
                                                      start=True, stop=True)
                    op.then_inc(off_done, 1)
                    pe.wait_ge(kdt_ready, CT * L + ct + 1)
                    np_ = L * CT * (BLK + DEC) + ct * (BLK + DEC)
                    for j in range(BLK):
                        w = BLK - j
                        pe.wait_ge(term_ready, it0 + ITEM_AT[("pj", j)] + 1)
                        for h, r, _ in heads:
                            op = nc.tensor.matmul(
                                ps[:, h, :].rearrange("p (n s) -> p n s", s=BLK)[:, :, j:BLK],
                                const["w16"][r, w:w + P],
                                Pr[r, j % 2, 0:32 * w].rearrange("p (n s) -> p n s", s=w), start=j == 0, stop=j == BLK - 1)
                        op.then_inc(prod_used, 1)
                    pe.wait_ge(a_ready, 8 * L + (4, 6, 8)[ct])
                    for j in range(DEC):
                        w = DEC - j
                        pe.wait_ge(term_ready, it0 + ITEM_AT[("sj", j)] + 1)
                        for h, r, _ in heads:
                            op = nc.tensor.matmul(
                                ps[0:NS, h, 0:NS].rearrange("p (n s) -> p n s", s=DEC)[:, :, j:DEC],
                                const["w8"][r, w:w + NS],
                                Pr[r, j % 2, 0:NB * w].rearrange("p (n s) -> p n s", s=w),
                                start=j == 0, stop=j == DEC - 1)
                        op.then_inc(prod_used, 1)
                    pe.wait_ge(as_ready, CT * L + ct + 1)
                    for c in range(TT):
                        for h, r, vo in heads:
                            op = nc.tensor.matmul(ps[r, 1, c * DV:c * DV + DV], KdT[:, c, r], V[:, c, vo:vo + DV],
                                                  start=True, stop=True)
                    op.then_inc(upd_done, 1)
                    for h, r, vo in heads:
                        pe.wait_ge(vbd_ready, 8 * L + vo // DV + 1)
                        nc.tensor.matmul(ps[r, 2, :], KdT[0:NS, TT, r], vbd[0:NS, :], start=True, stop=True).then_inc(vbd_used, 1)
                    pe.wait_ge(s_ready, CT * L + ct + 1)
                    for k in range(nh // 2):
                        m = (0, 2, 3)[ct] + k
                        bp, bs = 3 + 2 * k, 4 + 2 * k
                        for hb in range(2):
                            h, r, vo = heads[2 * k + hb]
                            o = slice(hb * DV, hb * DV + DV)
                            for c in range(TT):
                                t = slice(c * P, c * P + P)
                                nc.tensor.matmul(ps[o, bp, t], V[:, c, vo:vo + DV], A[:, h, t], start=True, stop=c == 0)
                                if c:
                                    nc.tensor.matmul(ps[o, bp, t], S[r, ct, c - 1, :], Qe[r, ct, t], start=False, stop=True)
                            nc.tensor.matmul(ps[o, bs, 0:NS], V[:, TT, vo:vo + DV], A[:, h, SEQ:T],
                                             start=True, stop=False, skip_group_check=True)
                            for b in range(NB):
                                t = DEC * b
                                op = nc.tensor.matmul(ps[o, bs, t:t + DEC], S0[r, ct, b, :], Qe[r, ct, SEQ + t:SEQ + t + DEC],
                                                      start=False, stop=True, skip_group_check=True)
                        op.then_inc(o_done, 1)
                        pe.wait_ge(osq_ready, 4 * L + m + 1)
                        nc.tensor.matmul(ps[:, 7, :], const["bones"], osq[:, 0:SEQ], start=True, stop=True)
                        nc.tensor.matmul(ps[:, 0, 0:NS], const["bones"], osq[:, SEQ:T], start=True, stop=True).then_inc(oss_done, 1)

                pe.wait_ge(mixl_ready, 4 * (L + 1))
                pe.wait_ge(sn_ready, CT * (L + 1))
                n0 = 32 * L
                for n in range(32 + 3):
                    if n < 32:
                        h, qt_ = n // 4, n % 4
                        r = slice((h % 2) * DH, (h % 2) * DH + DH)
                        w = P * (qt_ + 1)
                        if n >= 2:
                            pe.wait_ge(sc_free, n0 + n - 1)
                        nc.tensor.matmul(ps[:, n % 2, 0:w], QK[r, h // 2, qt_ * P:qt_ * P + P], QK[r, 4 + h // 2, 0:w],
                                         start=True, stop=True).then_inc(sc_done, 1)
                    k = n - 2
                    if 0 <= k < 32:
                        pe.wait_ge(pn_ready, n0 + k + 1)
                        if k >= 2:
                            pe.wait_ge(pt_ready, n0 + k - 1)
                        for kb in range(k % 4 + 1):
                            op = nc.tensor.transpose(ps[:, 2 + k % 2, kb * P:kb * P + P], Pp[:, k % 4, kb * P:kb * P + P],
                                                     const["ident"])
                        op.then_inc(pt_ps, 1)
                    k = n - 3
                    if 0 <= k < 32:
                        h, qt_ = k // 4, k % 4
                        if k % 8 == 0 and k >= 16:
                            pe.wait_ge(mixc_ready, 4 * L + k // 8 - 1)
                        pe.wait_ge(pt_ready, n0 + k + 1)
                        o = slice((h % 2) * DH, (h % 2) * DH + DH)
                        for kb in range(qt_ + 1):
                            op = nc.tensor.matmul(ps[o, 4 + (h // 2) % 2, qt_ * P:qt_ * P + P], V[:, kb, 512 + h * DH:512 + h * DH + DH],
                                                  PTp[:, k % 2, kb * P:kb * P + P], start=kb == 0, stop=kb == qt_)
                        op.then_inc(pv_done, 1)
                pe.wait_ge(qs_ready, L + 1)
                pe.wait_ge(mixc_ready, 4 * (L + 1))
                for b in range(NB + 1):
                    if b < NB:
                        n = NB * L + b
                        kc = [tiles(piece_landed(pe, L, b, part), 2) for part in range(2)]
                        if b:
                            pe.wait_ge(ssc_free, n)
                        for hp in range(4):
                            o = slice(32 * hp, 32 * hp + 32)
                            for a in range(2):
                                nc.tensor.matmul(ps[o, a, :], Qs[:, b, hp, :], kc[hp // 2][:, hp % 2, a * 512:a * 512 + 512], start=True, stop=True)
                            op = nc.tensor.matmul(ps[o, 2, 0:NS], Qs[:, b, hp, :], QK[:, 4 + hp, SEQ:T], start=True, stop=True)
                        op.then_inc(ssc_done, 1)
                    if b >= 1:
                        n = NB * L + b - 1
                        q = (b - 1) % 2
                        pe.wait_ge(spn_ready, n + 1)
                        if b >= 2:
                            pe.wait_ge(spt_ready, n)
                        for c in range(8):
                            nc.tensor.transpose(ps[:, 3 + c // 4, (c % 4) * P:(c % 4) * P + P], Ps[:, q, c:PAST:8], const["ident"])
                        nc.tensor.transpose(ps[0:NS, 5, 0:P], Ps[:, q, PAST:PAST + NS], const["ident"]).then_inc(spt_ps, 1)
                        pe.wait_ge(spt_ready, n + 1)
                        vc = [tiles(piece_landed(pe, L, b - 1, part), 4) for part in (2, 3)]
                        if b >= 3:
                            pe.wait_ge(smix_ready, n - 1)
                        pt = tiles(PTs[:, q, :], 9)
                        for hp in range(4):
                            out = ps[:, 6 + q, hp * 16:hp * 16 + 16]
                            for c in range(8):
                                nc.tensor.matmul(out, vc[c // 4][:, c % 4, hp * P:hp * P + P], pt[:, c, 32 * hp:32 * hp + 16], start=c == 0, stop=False)
                            op = nc.tensor.matmul(out, V[0:NS, TT, 512 + hp * P:512 + hp * P + P], pt[0:NS, 8, 32 * hp:32 * hp + 16],
                                                  start=False, stop=True)
                        op.then_inc(spv_done, 1)
                pe.wait_ge(smix_ready, NB * (L + 1))
                for m in range(U_OUT):
                    w = landed(ring_n)[:, 0:1024].rearrange("p (k c) -> p k c", k=KC)
                    ring_n += 1
                    if m >= 4:
                        pe.wait_ge(out_evac, PF0[L] + m - 3)
                    for k in range(KC):
                        op = gemm(pair(m % 4), w[:, k, :], mix[:, k, :], k, KC)
                    op.then_inc(unit_done, 1)
                pe.wait_ge(out_evac, PF0[L] + U_OUT)
                norm(2 * L + 1, sqf)
                pe.wait_ge(h_ready, (2 * L + 2) * KC)
                if L:
                    continue
                base, pf = ring_n, pf_ffn(L)
                with pe.Fori(0, EXPERTS[L]) as e:
                    for j in range(U_EXP):
                        n = base + j
                        pe.wait_ge(w_land[n % R], e * (16 * U_EXP // R) + 16 * (n // R + 1))
                        last = j - 4 if j >= 4 else (28, 29, 26, 27)[j] - U_EXP
                        pe.wait_ge(out_evac, e * U_EXP + (pf + last + 1))
                        if j < 2 * FE:
                            w = ring[:, n % R, 0:1024].rearrange("p (k c) -> p k c", k=KC)
                            for k in range(KC):
                                op = gemm(pair(j % 4), w[:, k, :], H[:, k, :], k, KC)
                        else:
                            w = ring[:, n % R, :].rearrange("p (k c) -> p k c", k=FE)
                            for k in range(FE):
                                if j == 2 * FE:
                                    pe.wait_ge(out_evac, e * U_EXP + (pf + 2 * k + 2))
                                op = gemm(pair(j % 4), w[:, k, :], hid[:, k, :], k, FE)
                        op.then_inc(unit_done, 1)
            for tt in range(TT + 1):
                rows = P if tt < TT else NS
                for k in range(KC):
                    op = nc.tensor.matmul(ps[0:rows, 2, tt * 8:tt * 8 + 8], H[:, k, tt * P:tt * P + rows],
                                          WRT[:, k * 8:k * 8 + 8], start=k == 0, stop=k == KC - 1)
            op.then_inc(rl_done, 1)
            for tt in range(TT + 1):
                rows = P if tt < TT else NS
                if tt >= 2:
                    pe.wait_ge(htok_ready, tt - 1)
                for k in range(KC):
                    op = nc.tensor.transpose(ps[0:rows, 4 + 2 * (tt % 2) + k // 4, (k % 4) * P:(k % 4) * P + P],
                                             H[:, k, tt * P:tt * P + rows], const["ident"])
                op.then_inc(htok_ps, 1)
            pe.wait_ge(chosen, 1)
            M = RW[:, 176:216]
            for tt in range(TT + 1):
                for t2 in range(tt):
                    nc.tensor.matmul(ps[:, 0, tt * 8:tt * 8 + 8], const["ones"], M[:, t2 * 8:t2 * 8 + 8], start=t2 == 0, stop=False)
                nc.tensor.matmul(ps[:, 0, tt * 8:tt * 8 + 8], const["before"], M[:, tt * 8:tt * 8 + 8], start=tt == 0, stop=True)
            for tt in range(TT + 1):
                op = nc.tensor.matmul(ps[:, 0, 40:48], const["ones"], M[:, tt * 8:tt * 8 + 8], start=tt == 0, stop=tt == TT)
            op.then_inc(ranked, 1)
            pe.wait_ge(coded, 1)
            pe.wait_ge(htok_ready, TT + 1)
            for r in range(4):
                if r == 3:
                    pe.wait_ge(rows_ready, 1)
                a = (r % 3) * 2
                for tt in range(TT + 1):
                    rows = P if tt < TT else NS
                    out = ps[:, 2 + a, tt * P:tt * P + P] if tt < TT else ps[:, 3 + a, 0:NS]
                    op = nc.tensor.matmul(out, RW[0:rows, 256 + 5 * r + tt:257 + 5 * r + tt].to_broadcast([rows, P]),
                                          const["ident"][0:rows, 0:rows], start=True, stop=True)
                op.then_inc(rows_ps, 1)
            pe.wait_ge(rows_ready, 4)

            def gather(count):
                pe.wait_ge(sel_ready, count)
                for k in range(KC):
                    out = ps[:, 3 + k // 3, (k % 3) * CAP:(k % 3) * CAP + CAP]
                    for tt in range(TT + 1):
                        rows = P if tt < TT else NS
                        op = nc.tensor.matmul(out, H_tok[0:rows, tt, k * P:k * P + P], Sel[0:rows, tt, :],
                                              start=tt == 0, stop=tt == TT)
                op.then_inc(gathered, 1)

            gather(1)
            pe.wait_ge(items_ready, 1)
            n_items = pe.value_load(item_tab[0:1, MAX_ITEMS:MAX_ITEMS + 1], min_val=N_EXP, max_val=MAX_ITEMS)
            pfi = pf_ffn(1)
            with pe.Fori(0, n_items) as i:
                pe.wait_ge(xg_ready, i + 1)
                pe.wait_ge(out_evac, i * KC + pfi)
                for j, (kind, f) in enumerate(UNITS):
                    s = j % R
                    pe.wait_ge(w_land[s], i * (16 * SLOT_USES[s]) + 16 * (landings[s] + j // R + 1))
                    w = ring[:, s, 0:1024].rearrange("p (k c) -> p k c", k=KC)
                    if kind != "down":
                        if f >= 2:
                            pe.wait_ge(hid_ready, i * FE + (f - 1))
                        out = ps[:, 3 + 2 * (f % 2) + (kind == "up"), 0:CAP]
                        for k in range(KC):
                            op = nc.tensor.matmul(out, w[:, k, :], Xg[:, k, :], start=k == 0, stop=k == KC - 1)
                    else:
                        pe.wait_ge(hid_ready, i * FE + (f + 1))
                        for k in range(KC):
                            op = nc.tensor.matmul(ps[:, k // 3, (k % 3) * CAP:(k % 3) * CAP + CAP], w[:, k, :], hidg[:, f, :],
                                                  start=f == 0 and k % 3 == 0, stop=f == FE - 1, skip_group_check=True)
                    op.then_inc(unit_done, 1)
                gather(i + 2)
                pe.wait_ge(yt_ready, i + 1)
                for k in range(KC):
                    nc.tensor.transpose(ps[:, 6 + k // 4, (k % 4) * P:(k % 4) * P + P], Yt[:, k, 0:P], const["ident"])
                for k in range(KC):
                    op = nc.tensor.transpose(ps[0:CAP2, k // 4, (k % 4) * P:(k % 4) * P + P], Yt[:, k, P:CAP], const["ident"])
                op.then_inc(ytok_ps, 1)
                pe.wait_ge(ytok_ready, i + 1)
                pe.wait_ge(selw_ready, i + 1)
                pe.wait_ge(xg_ready, i + 2)
                for k in range(KC):
                    if k >= 3:
                        pe.wait_ge(out_evac, i * KC + (pfi + k - 2))
                    for a in range(2):
                        t = slice(a * HALF, a * HALF + HALF)
                        nc.tensor.matmul(pair(1 + k % 3)[:, a, :], Ytok[:, 0, k * P:k * P + P], SelW[:, 0, t], start=True, stop=False)
                        op = nc.tensor.matmul(pair(1 + k % 3)[:, a, :], Ytok[0:CAP2, 1, k * P:k * P + P], SelW[0:CAP2, 1, t],
                                              start=False, stop=True)
                    op.then_inc(scattered, 1)

        @block.vector
        def _(dve):
            v = nc.vector
            n_chain = [0]

            def link(op):
                op.then_inc(dch, 1)
                n_chain[0] += 1
                dve.wait_ge(dch, n_chain[0])

            v.memset(V[NS:P, TT, :], 0.0)
            v.memset(eps_col, EPS).then_inc(eps_ready, 1)
            dve.wait_ge(c_in, 16 * 5)
            l0, l1 = LB[:, 16:18], LB[:, 18:20]
            link(v.tensor_tensor(LB[:, 28:30], l0, l1, ALU.max))
            link(v.tensor_tensor(LB[:, 24:26], l0, LB[:, 28:30], ALU.subtract))
            v.tensor_tensor(LB[:, 26:28], l1, LB[:, 28:30], ALU.subtract).then_inc(lb_ready, 1)
            dve.wait_ge(lb_exp, 1)
            w0, w1 = LB[:, 20:22], LB[:, 22:24]
            link(v.tensor_tensor(LB[:, 28:30], w0, w1, ALU.add))
            link(v.reciprocal(LB[:, 30:32], LB[:, 28:30]))
            link(v.tensor_tensor(w0, w0, LB[:, 30:32], ALU.mult))
            link(v.tensor_tensor(w1, w1, LB[:, 30:32], ALU.mult))
            link(v.tensor_tensor(LB[:, 0:2], w0, w0, ALU.subtract))
            link(v.tensor_tensor(LB[:, 28:30], w0, w1, ALU.add))
            link(v.tensor_tensor(LB[:, 2:4], LB[:, 28:30], w0, ALU.subtract))
            link(v.tensor_scalar(oml, lb, -1.0, 1.0, ALU.mult, ALU.add))

            def normed(k, r, gains):
                dve.wait_ge(rinv_ready, k + 1)
                for c in range(KC):
                    v.scalar_tensor_tensor(H[:, c, :], X[:, c, :], gains[:, c:c + 1], r, ALU.mult, ALU.mult).then_inc(h_ready, 1)

            def job(op):
                op.then_inc(dve_job, 1)

            for L in range(DEPTH):
                normed(2 * L, rinv, vec(L, "g_mix"))
                for n, (kind, i) in enumerate(JOBS):
                    if not HAS_DVE[n]:
                        continue
                    src = pair((n + 1) % 4)
                    s = n % 3
                    if kind in ("bf", "bq", "g", "s"):
                        dve.wait_ge(act_job, L * ACT_N[-1] + ACT_N[n])
                    else:
                        dve.wait_ge(pe_job, L * NJ + n + 1)
                    if kind == "lr":
                        job(v.tensor_copy(split(lr_sb), src[0:RANK]))
                    elif kind == "bf":
                        f, kk = e0[:, s, :], e1s[:, s, :]
                        link(v.tensor_scalar(f, f, 1.0, None, ALU.add))
                        link(v.tensor_scalar(kk, kk, 1.0, None, ALU.add))
                        link(v.reciprocal(f, f))
                        link(v.reciprocal(kk, kk))
                        v.tensor_scalar(B[:, 1 + i, :], f, oml[:, 2 * L + i:2 * L + i + 1], lb[:, 2 * L + i:2 * L + i + 1], ALU.mult, ALU.add)
                        job(v.tensor_scalar(K[:, 1 + i, :], kk, oml[:, 2 * L + i:2 * L + i + 1], None, ALU.mult))
                    elif kind == "aq":
                        job(v.tensor_scalar(split(Q[:, 0, :]), src, float(DK_A) ** -0.5, None, ALU.mult))
                    elif kind == "gu":
                        job(v.tensor_scalar(split(B[:, 0, :]), src, vec(L, "b_gate"), None, ALU.add))
                    elif kind == "ak":
                        job(v.tensor_copy(split(K[:, 0, :]), src))
                    elif kind == "s":
                        gain = vec(L, "g_q" if i < 4 else "g_k")
                        job(v.scalar_tensor_tensor(qn[:, i % 3, :], e0[:, i % 3, :], gain, rinvs[:, i % 3, :], ALU.mult, ALU.mult))
                    else:
                        dst = QK[:, i, :]
                        if i:
                            dve.wait_ge(dve_job, L * DVE_N[-1] + DVE_N[n - 1])
                        v.tensor_tensor(split(rtmp), src, split(const["sin"]), ALU.mult)
                        link(v.tensor_tensor(dst, qn[:, i % 3, :], const["cos"], ALU.mult))
                        job(v.tensor_tensor(dst, dst, rtmp, ALU.add))
                dve.wait_ge(dve_job, (L + 1) * DVE_N[-1])
                link(v.tensor_scalar(Dr[:, 1, :], B[:, 0, :], -1.0, None, ALU.mult))
                v.tensor_tensor(Dr[:, 0, :], B[:, 0, :], Dr[:, 1, :], ALU.max).then_inc(lf_abs, 1)
                dve.wait_ge(lf_ready, 3 * L + 1)
                link(v.scalar_tensor_tensor(Dr[:, 0, :], B[:, 0, :], 0.0, Dr[:, 0, :], ALU.min, ALU.subtract))
                link(v.tensor_scalar(Dr[:, 0, :], Dr[:, 0, :], 1.0 / 16.0, None, ALU.mult))
                v.tensor_tensor_scan(B[:, 0, :], const["reset"], Dr[:, 0, :], 0.0, ALU.mult, ALU.add).then_inc(b_ready, 1)
                for ct in (1, 2):
                    dve.wait_ge(lf_ready, 3 * L + 1 + ct)
                    v.tensor_tensor_scan(B[:, ct, :], const["reset"], Dr[:, ct, :], 0.0, ALU.mult, ALU.add).then_inc(b_ready, 1)
                v.memset(A[NS:P, :, SEQ:T], 0.0)
                for ct in range(CT):
                    nh = CT_HEADS[ct]
                    it0 = L * CT * NI + ct * NI
                    np_ = L * CT * (BLK + DEC) + ct * (BLK + DEC)
                    Qp = Q[:, ct, 0:SEQ].rearrange("p (n s) -> p n s", s=BLK)
                    Kp = K[:, ct, 0:SEQ].rearrange("p (n s) -> p n s", s=BLK)
                    Qd = Q[:, ct, SEQ:T].rearrange("p (n s) -> p n s", s=DEC)
                    Kd_ = K[:, ct, SEQ:T].rearrange("p (n s) -> p n s", s=DEC)
                    for kind, i in ITEMS:
                        it = it0 + ITEM_AT[(kind, i)]
                        D = Dr[:, it % 3, :]
                        Dp = D[:, 0:SEQ].rearrange("p (c s) -> p c s", c=TT)
                        dve.wait_ge(exp_ready, it + 1)
                        if kind == "eb":
                            v.tensor_copy(ebl[:, ct, 0:TT], D[:, P - 1:SEQ:P])
                            v.tensor_copy(ebl[:, ct, TT:12], D[:, SEQ + DEC - 1:T:DEC])
                            op = v.tensor_tensor(Qe[:, ct, :], Q[:, ct, :], D, ALU.mult)
                        elif kind == "kd":
                            op = v.tensor_tensor(kd, K[:, ct, :], D, ALU.mult)
                        elif kind == "qt":
                            if ct:
                                dve.wait_ge(off_done, CT * L + ct)
                            op = v.tensor_tensor(qt.rearrange("p (c s) -> p c s", c=TT)[:, :, BLK:P],
                                                 Q[:, ct, 0:SEQ].rearrange("p (c s) -> p c s", c=TT)[:, :, BLK:P], Dp[:, :, BLK:P], ALU.mult)
                        elif kind == "kt":
                            w = BLK * i
                            if i == 1:
                                dve.wait_ge(kt_zero, L + 1)
                            op = v.tensor_tensor(Kt[:, i - 1, :, 0:w], K[:, ct, 0:SEQ].rearrange("p (c s) -> p c s", c=TT)[:, :, 0:w],
                                                 Dp[:, :, 0:w], ALU.mult)
                        else:
                            blk, nblk, q_, k_ = (BLK, SEQ // BLK, Qp, Kp) if kind == "pj" else (DEC, NB, Qd, Kd_)
                            w = blk - i
                            m = i if kind == "pj" else BLK + i
                            if m >= 2:
                                dve.wait_ge(prod_used, np_ + m - 1)
                            prod = Pr[:, m % 2, 0:nblk * w].rearrange("p (n s) -> p n s", s=w)
                            dd = D[:, 0:nblk * w].rearrange("p (n s) -> p n s", s=w)
                            link(v.tensor_tensor(prod, dd, k_[:, :, i:i + 1].to_broadcast([P, nblk, w]), ALU.mult))
                            op = v.tensor_tensor(prod, prod, q_[:, :, i:blk], ALU.mult)
                        op.then_inc(term_ready, 1)
                        if (kind, i) == ("pj", BLK - 1):
                            dve.wait_ge(prod_used, np_ + BLK)
                            dve.wait_ge(off_done, CT * L + ct + 1)
                            for h in range(nh):
                                a3 = A[:, h, 0:SEQ].rearrange("p (c s) -> p c s", c=TT)
                                link(v.tensor_tensor(a3, ps[:, h, :].rearrange("p (c s) -> p c s", c=TT),
                                                     const["mask16"].rearrange("p (o s) -> p o s", o=1).to_broadcast([P, TT, P]), ALU.mult))
                                v.tensor_tensor(a3[:, :, BLK:P], a3[:, :, BLK:P],
                                                ps[:, 4 + h, :].rearrange("p (c s) -> p c s", c=TT)[:, :, BLK:P], ALU.add).then_inc(a_ready, 1)
                    dve.wait_ge(prod_used, np_ + BLK + DEC)
                    v.tensor_tensor(A[0:NS, 0:nh, SEQ:T], ps[0:NS, 0:nh, 0:NS],
                                    const["mask8"][0:NS, :].rearrange("p (o s) -> p o s", o=1).to_broadcast([NS, nh, NS]),
                                    ALU.mult).then_inc(as_ready, 1)
                    dve.wait_ge(upd_done, CT * L + ct + 1)
                    link(v.tensor_copy(S[:, ct, 0, :], ps[:, 1, 0:DV]))
                    for c in range(1, TT):
                        op = v.scalar_tensor_tensor(S[:, ct, c, :], S[:, ct, c - 1, :], ebl[:, ct, c:c + 1],
                                                    ps[:, 1, c * DV:c * DV + DV], ALU.mult, ALU.add)
                        if c < TT - 1:
                            link(op)
                    op.then_inc(s_ready, 1)
                    for k in range(nh // 2):
                        m = (0, 2, 3)[ct] + k
                        bp, bs = 3 + 2 * k, 4 + 2 * k
                        dve.wait_ge(orinv_ready, 4 * L + m + 1)
                        gain = vec(L, "g_gla" if ct == 0 else "g_hgrn")
                        v.scalar_tensor_tensor(mix[:, m, 0:SEQ], ps[:, bp, :], gain, orinv[:, 0:SEQ], ALU.mult, ALU.mult)
                        link(v.scalar_tensor_tensor(mix[:, m, SEQ:T], ps[:, bs, 0:NS], gain, orinv[:, SEQ:T], ALU.mult, ALU.mult))
                        v.tensor_tensor(mix[:, m, :], mix[:, m, :], G[:, m, :], ALU.mult).then_inc(mixl_ready, 1)
                    dve.wait_ge(vbd_used, 8 * L + (4, 6, 8)[ct])
                    s0 = S0[:, ct, :, :]
                    link(v.tensor_tensor(s0, s0, ebl[:, ct, TT:12].rearrange("p (b o) -> p b o", o=1).to_broadcast([P, NB, DV]), ALU.mult))
                    v.tensor_tensor(s0, s0, ps[:, 2, :].rearrange("p (b v) -> p b v", b=NB), ALU.add).then_inc(sn_ready, 1)
                dve.wait_ge(mixl_ready, 4 * (L + 1))
                link(v.memset(LIN[:, 6144:7168], 0.0))
                for hb in range(2):
                    r = slice(hb * DH, hb * DH + DH)
                    for hp in range(4):
                        op = v.tensor_copy(Qs[r, :, hp, hb * DEC:hb * DEC + DEC], QK[r, hp, SEQ:T].rearrange("p (b t) -> p b t", b=NB))
                op.then_inc(qs_ready, 1)
                n0 = 32 * L
                for n in range(32 + 1):
                    if n < 32:
                        w = P * (n % 4 + 1)
                        pn, s = Pp[:, n % 4, 0:w], n % 4
                        dve.wait_ge(sc_done, n0 + n + 1)
                        if n >= 4:
                            dve.wait_ge(pt_ps, n0 + n - 3)
                        v.scalar_tensor_tensor(pn, ps[:, n % 2, 0:w], DH ** -0.5, const["lnc"][:, SEQ - w:SEQ],
                                               ALU.mult, ALU.add).then_inc(sc_free, 1)
                        dve.wait_ge(sc_free, n0 + n + 1)
                        v.tensor_reduce(negmax[:, s:s + 1], pn, AX.X, ALU.max, negate=True).then_inc(mx_ready, 1)
                    k = n - 1
                    if k >= 0:
                        w = P * (k % 4 + 1)
                        pk, s = Pp[:, k % 4, 0:w], k % 4
                        dve.wait_ge(p_ready, n0 + k + 1)
                        link(v.reciprocal(rden[:, s:s + 1], den[:, s:s + 1]))
                        v.tensor_scalar(pk, pk, rden[:, s:s + 1], None, ALU.mult).then_inc(pn_ready, 1)
                for b in range(NB + 2):
                    if b < NB:
                        n = NB * L + b
                        pn, s = Ps[:, b % 2, :], 4 + b % 2
                        dve.wait_ge(ssc_done, n + 1)
                        if b >= 2:
                            dve.wait_ge(spt_ps, n - 1)
                        v.scalar_tensor_tensor(pn[:, 0:PAST], ps[:, 0:2, :].rearrange("p a t -> p (a t)"), DH ** -0.5,
                                               const["smask"], ALU.mult, ALU.add)
                        v.scalar_tensor_tensor(pn[:, PAST:PAST + NS], ps[:, 2, 0:NS], DH ** -0.5,
                                               const["smask_new"][:, b * NS:b * NS + NS], ALU.mult, ALU.add).then_inc(ssc_free, 1)
                        dve.wait_ge(ssc_free, n + 1)
                        v.tensor_reduce(negmax[:, s:s + 1], pn, AX.X, ALU.max, negate=True).then_inc(smx_ready, 1)
                        dve.wait_ge(sp_ready, n + 1)
                        link(v.reciprocal(rden[:, s:s + 1], den[:, s:s + 1]))
                        v.tensor_scalar(pn, pn, rden[:, s:s + 1], None, ALU.mult).then_inc(spn_ready, 1)
                    if b >= 2:
                        bb = b - 2
                        dve.wait_ge(spv_done, NB * L + bb + 1)
                        o = ps[:, 6 + bb % 2, 0:64].rearrange("p (h q) -> p h q", h=4)
                        t = SEQ + DEC * bb
                        v.tensor_copy(mix[0:DH, 4:8, t:t + DEC], o[0:DH, :, 0:DEC])
                        v.tensor_copy(mix[DH:P, 4:8, t:t + DEC], o[DH:P, :, DEC:2 * DEC]).then_inc(smix_ready, 1)
                for m in range(U_OUT):
                    dve.wait_ge(unit_done, UD0[L] + NVU + m + 1)
                    v.tensor_tensor(split(X[:, m, :]), split(X[:, m, :]), pair(m % 4), ALU.add).then_inc(out_evac, 1)
                normed(2 * L + 1, hid[:, 0, :], vec(L, "g_ffn"))
                if L:
                    continue
                sg, pf = FE * EXPERTS[0] * L, pf_ffn(L)
                with dve.Fori(0, EXPERTS[L]) as e:
                    for i in range(FE):
                        t = ft[:, i % 2, :]
                        dve.wait_ge(sig_ready, e * FE + (sg + i + 1))
                        dve.wait_ge(unit_done, e * U_EXP + (ud_ffn(L) + 2 * i + 2))
                        v.tensor_tensor(split(hid[:, i, :]), pair((2 * i + 1) % 4), split(t), ALU.mult).then_inc(out_evac, 2)
                    for m in range(KC):
                        dve.wait_ge(unit_done, e * U_EXP + (ud_ffn(L) + 2 * FE + m + 1))
                        v.tensor_tensor(split(X[:, m, :]), split(X[:, m, :]), pair((2 * FE + m) % 4), ALU.add).then_inc(out_evac, 1)

            def t3(o):
                return RW[:, o:o + 40].rearrange("p (t e) -> p t e", e=8)

            def t1(o):
                return RW[:, o:o + 5]

            def over_e(o):
                return t1(o).rearrange("p (t o) -> p t o", o=1).to_broadcast([P, 5, 8])

            def over_t(ap):
                return ap.rearrange("p (o e) -> p o e", o=1).to_broadcast([P, 5, 8])

            lg, eq, first, second, both, code = t3(0), t3(40), t3(95), t3(135), t3(176), t3(216)
            code1, code2, w1_, w2_ = (t1(256 + 5 * r) for r in range(4))
            m1, m2, dif = t1(85), t1(90), t1(80)
            link(v.memset(RW[:, 0:40], 0.0))
            dve.wait_ge(rl_done, 1)
            v.tensor_copy(RW[:, 0:32], ps[:, 2, 0:32])
            link(v.tensor_copy(RW[0:NS, 32:40], ps[0:NS, 2, 32:40]))
            for o_m, pick in ((85, first), (90, second)):
                link(v.tensor_reduce(t1(o_m), lg, AX.X, ALU.max))
                link(v.tensor_tensor(eq, lg, over_e(o_m), ALU.is_equal))
                link(v.tensor_tensor(eq, eq, over_t(const["riota"]), ALU.mult))
                link(v.tensor_reduce(dif, eq, AX.X, ALU.max))
                link(v.tensor_tensor(pick, eq, over_e(80), ALU.is_equal))
                if pick is first:
                    link(v.scalar_tensor_tensor(lg, pick, -3e38, lg, ALU.mult, ALU.add))
            v.tensor_tensor(dif, m2, m1, ALU.subtract).then_inc(rexp, 1)
            link(v.tensor_tensor(both, first, second, ALU.add))
            v.memset(RW[NS:P, 176 + 32:176 + 40], 0.0).then_inc(chosen, 1)
            dve.wait_ge(rexp_done, 1)
            link(v.tensor_scalar(w2_, dif, 1.0, None, ALU.add))
            link(v.reciprocal(w1_, w2_))
            link(v.tensor_tensor(w2_, dif, w1_, ALU.mult))
            dve.wait_ge(ranked, 1)
            cnt, npass, upto, start = (RW[:, 280 + 8 * r:288 + 8 * r] for r in range(4))
            link(v.tensor_copy(cnt, ps[:, 0, 40:48]))
            link(v.memset(npass, 1.0))
            for m in range(1, PER_EXP):
                link(v.scalar_tensor_tensor(npass, cnt, float(m * CAP), npass, ALU.is_gt, ALU.add))
            link(v.tensor_tensor_scan(upto, const["ones"][:, 0:8], npass, 0.0, ALU.mult, ALU.add))
            link(v.tensor_tensor(start, upto, npass, ALU.subtract))
            link(v.tensor_scalar(start, start, float(CAP), None, ALU.mult))
            link(v.tensor_tensor(code, ps[:, 0, 0:40].rearrange("p (t e) -> p t e", e=8), over_t(start), ALU.add))
            link(v.tensor_tensor(first, first, code, ALU.mult))
            link(v.tensor_reduce(code1, first, AX.X, ALU.add))
            link(v.tensor_tensor(second, second, code, ALU.mult))
            v.tensor_reduce(code2, second, AX.X, ALU.add).then_inc(coded, 1)
            tab = RW[0:1, 320:320 + MAX_ITEMS * 8].rearrange("p (i e) -> p i e", e=8)
            link(v.tensor_tensor(tab, upto[0:1].rearrange("p (o e) -> p o e", o=1).to_broadcast([1, MAX_ITEMS, 8]),
                                 const["slots"][0:1, 0:MAX_ITEMS].rearrange("p (i o) -> p i o", o=1).to_broadcast([1, MAX_ITEMS, 8]), ALU.is_le))
            of_item = RW[0:1, 320 + MAX_ITEMS * 8:320 + MAX_ITEMS * 9]
            link(v.tensor_reduce(of_item, tab, AX.X, ALU.add))
            link(v.tensor_scalar(of_item, of_item, float(N_EXP - 1), None, ALU.min))
            v.tensor_copy(item_tab[0:1, 0:MAX_ITEMS], of_item)
            v.tensor_copy(item_tab[0:1, MAX_ITEMS:MAX_ITEMS + 1], upto[0:1, 7:8]).then_inc(items_ready, 1)
            dve.wait_ge(coded, 1)

            rows_col = LB[:, 8:10]
            link(v.tensor_copy(rows_col, const["rows"]))
            lnk = [n_chain[0]]

            def sel_steps(chained):
                out = []
                for tt in range(TT + 1):
                    out.append(lambda tt=tt: chained(v.tensor_scalar(Sel[:, tt, :], const["slots"], code1[:, tt:tt + 1], None, ALU.is_equal)))
                    out.append(lambda tt=tt: v.scalar_tensor_tensor(Sel[:, tt, :], const["slots"], code2[:, tt:tt + 1], Sel[:, tt, :],
                                                                    ALU.is_equal, ALU.add))
                return out

            for r in range(4):
                dve.wait_ge(rows_ps, r + 1)
                a = (r % 3) * 2
                v.tensor_copy(rows4[:, r, 0:SEQ], ps[:, 2 + a, :])
                v.tensor_copy(rows4[:, r, SEQ:T], ps[:, 3 + a, 0:NS]).then_inc(rows_ready, 1)
            dve.wait_ge(rows_ready, 4)
            for s in sel_steps(link):
                op = s()
            op.then_inc(sel_ready, 1)
            dve.wait_ge(items_ready, 1)
            n_items = dve.value_load(item_tab[0:1, MAX_ITEMS:MAX_ITEMS + 1], min_val=N_EXP, max_val=MAX_ITEMS)
            c0, pfi = n_chain[0], pf_ffn(1)
            PER_ITEM = 4 + 2 + (TT + 1)
            with dve.Fori(0, n_items) as i:
                k_chain = [0]

                def chained(op):
                    op.then_inc(dch, 1)
                    k_chain[0] += 1
                    dve.wait_ge(dch, i * PER_ITEM + (c0 + k_chain[0]))

                def weighted(st):
                    w = P if st == 0 else CAP2
                    a, b = SelW[0:w, st, :], selt[0:w, :]
                    col = rows_col[0:w, st:st + 1]
                    chained(v.scalar_tensor_tensor(a, rows4[0:w, 0, :], col, rows4[0:w, 2, :], ALU.is_equal, ALU.mult))
                    chained(v.scalar_tensor_tensor(b, rows4[0:w, 1, :], col, rows4[0:w, 3, :], ALU.is_equal, ALU.mult))
                    op = v.tensor_tensor(a, a, b, ALU.add)
                    if st:
                        op.then_inc(selw_ready, 1)
                        dve.wait_ge(selw_ready, i + 1)

                def move_on():
                    chained(v.tensor_scalar(rows_col, rows_col, float(CAP), None, ALU.add))
                    dve.wait_ge(gathered, i + 1)
                    chained(v.tensor_scalar(RW[:, 256:266], RW[:, 256:266], float(-CAP), None, ALU.add))

                sels = sel_steps(chained)
                between = [lambda: weighted(0), lambda: weighted(1), move_on]
                between += [lambda a=a: [s() for s in sels[2 * a:2 * a + 2]][-1] for a in range(TT + 1)]
                for f in range(FE):
                    dve.wait_ge(silu_ready, i * FE + (f + 1))
                    dve.wait_ge(unit_done, i * U_ITEM + (UD_ITEMS + UNIT_AT[("up", f)] + 1))
                    v.tensor_tensor(hidg[:, f, :], tg[:, f % 2, :], ps[:, 4 + 2 * (f % 2), 0:CAP], ALU.mult).then_inc(hid_ready, 1)
                    if f < len(between):
                        op = between[f]()
                        if f == len(between) - 1:
                            op.then_inc(sel_ready, 1)
                for k in range(KC):
                    dve.wait_ge(scattered, i * KC + (k + 1))
                    v.tensor_tensor(split(X[:, k, :]), split(X[:, k, :]), pair(1 + k % 3), ALU.add).then_inc(out_evac, 1)
            v.tensor_copy(rows_col, const["rows"]).then_inc(experts_done, 1)


NH = 8


def lay_inputs(i):
    f = np.ascontiguousarray

    def unit(w):
        k, n = w.shape
        return f(w.reshape(k // P, P, n // P, P).transpose(2, 1, 0, 3).reshape(n // P, P, k))

    out = {"consts": shape_constants()}
    x = np.concatenate([i["x_prompt"].reshape(SEQ, D_MODEL), i["x_sample"].reshape(NS, D_MODEL)], 0)
    out["x"] = f(x.T.reshape(KC, P, T).transpose(1, 0, 2))
    w_in = i["w_in"]
    widths = [128, 128, 256, 16, 256, 256, 256, 256, 256, 512, 512, 512]
    cuts = np.cumsum(widths)[:-1].tolist()
    parts = [np.split(w_in[L], cuts, axis=1) for L in range(DEPTH)]
    feat, val, lr = [], [], []
    for L in range(DEPTH):
        a_q, a_k, a_v, a_lr, a_g, b_q, b_f, b_i, b_g, c_q, c_k, c_v = parts[L]
        feat.append(unit(np.concatenate([b_f, a_q, a_k, b_q, a_g, b_g, c_q, c_k], 1)))
        v = np.concatenate([a_v, b_i, c_v], 1)
        val.append(v.reshape(4, 2, P, 2, 512).transpose(3, 0, 2, 1, 4).reshape(NV, P, 1024))
        lr.append(a_lr.reshape(KC, P, RANK).transpose(1, 0, 2).reshape(P, KC * RANK))
    out["w_feat"], out["w_v"], out["w_lr"] = (f(np.stack(a)) for a in (feat, val, lr))
    out["w_out"] = np.stack([unit(i["w_out"][L]) for L in range(DEPTH)])
    half = FE * P
    gates, ups, downs = [], [], []
    for h in range(2):
        gates.append(i["ffn_w_gate"][0][:, h * half:(h + 1) * half])
        ups.append(i["ffn_w_up"][0][:, h * half:(h + 1) * half])
        downs.append(i["ffn_w_down"][0][h * half:(h + 1) * half])
    gates += list(i["moe_w_gate"][0])
    ups += list(i["moe_w_up"][0])
    out["w_gu"] = np.concatenate([np.stack([unit(g), unit(u)], 1).reshape(2 * FE, P, D_MODEL) for g, u in zip(gates, ups)], 0)
    out["w_dn"] = np.concatenate([unit(w) for w in downs], 0)
    out["w_dn_moe"] = f(i["moe_w_down"][0].reshape(N_EXP * FE, P, D_MODEL))
    out["w_router"] = f(i["moe_w_router"][0].reshape(KC, P, 8).transpose(1, 0, 2).reshape(P, 64))
    out["w_up"] = f(i["gla_w_gate_up"].transpose(1, 0, 2).reshape(RANK, DEPTH * P))
    out["lb_logits"] = f(i["hgrn_lb_logits"].reshape(DEPTH, 2, P).transpose(2, 0, 1).reshape(P, 4))
    cols = []
    for L in range(DEPTH):
        cols += [i["norm_mix_g"][L].reshape(KC, P).T, i["norm_ffn_g"][L].reshape(KC, P).T, i["gla_b_gate"][L].reshape(P, 1)]
        cols += [np.tile(i[n][L], 2).reshape(P, 1) for n in ("gla_norm_g", "hgrn_norm_g", "attn_q_norm_g", "attn_k_norm_g")]
    out["vecs"] = f(np.concatenate(cols, 1))
    out["s0_gla"] = f(i["state_gla"].transpose(0, 2, 3, 1, 4).reshape(DEPTH, P, NB, DV))
    out["s0_hgrn"] = f(i["state_hgrn"].transpose(0, 2, 3, 1, 4).reshape(DEPTH, 2, P, NB, DV).transpose(0, 2, 1, 3, 4))
    out["kcache"] = f(i["cache_k_win"].reshape(DEPTH, NB, PAST, 4, P).transpose(0, 1, 4, 3, 2))
    out["vcache"] = f(i["cache_v_win"].reshape(DEPTH, NB, P, 8, 512))
    return out


OUTS = {
    "y": (P, KC, T), "os_gla_p": (DEPTH, P, DV), "os_hgrn_p": (DEPTH, P, 2, DV),
    "ok_p": (DEPTH, P, 4, SEQ), "ov_p": (DEPTH, P, TT, 512),
    "os_gla_s": (DEPTH, P, NB, DV), "os_hgrn_s": (DEPTH, P, 2, NB, DV),
    "ok_s": (DEPTH, NB, P, 4, PAST), "ov_s": (DEPTH, NB, P, 8, 512),
}


def lay_outputs(r):
    y = r["y"].transpose(1, 0, 2).reshape(D_MODEL, T).T
    return (
        np.ascontiguousarray(y[:SEQ]).reshape(1, SEQ, D_MODEL),
        np.ascontiguousarray(y[SEQ:]).reshape(NB, DEC, D_MODEL),
        r["os_gla_p"].reshape(DEPTH, 1, HEADS_A, DK_A, DV),
        r["os_hgrn_p"].transpose(0, 2, 1, 3).reshape(DEPTH, 1, HEADS_B, DK_B, DV),
        r["ok_p"].transpose(0, 3, 2, 1).reshape(DEPTH, 1, SEQ, AH, DH),
        r["ov_p"].transpose(0, 2, 1, 3).reshape(DEPTH, 1, SEQ, AH, DH),
        r["os_gla_s"].reshape(DEPTH, HEADS_A, DK_A, NB, DV).transpose(0, 3, 1, 2, 4),
        r["os_hgrn_s"].transpose(0, 2, 1, 3, 4).reshape(DEPTH, HEADS_B, DK_B, NB, DV).transpose(0, 3, 1, 2, 4),
        r["ok_s"].transpose(0, 1, 4, 3, 2).reshape(DEPTH, NB, PAST, AH, DH),
        r["ov_s"].reshape(DEPTH, NB, PAST, AH, DH),
    )


def kernel(**inputs):
    import concourse.bacc as bacc
    from concourse.bass_utils import run_bass_kernel_spmd

    nc = bacc.Bacc("TRN2", target_bir_lowering=False, num_devices=1)
    arrays = lay_inputs({n: np.asarray(a) for n, a in inputs.items()})
    d = {n: nc.dram_tensor(n, a.shape, F32, kind="ExternalInput").ap() for n, a in arrays.items()}
    d |= {n: nc.dram_tensor(n, s, F32, kind="ExternalOutput").ap() for n, s in OUTS.items()}
    build(nc, d)
    r = run_bass_kernel_spmd(nc, [arrays], core_ids=[0])
    return lay_outputs({n: np.asarray(r.results[0][n]) for n in OUTS})
```

```python
from contextlib import ExitStack

import numpy as np
import concourse.bass as bass
from concourse import mybir

F32 = mybir.dt.float32
F32R = mybir.dt.float32r
ALU = mybir.AluOpType
ACT = mybir.ActivationFunctionType
AX = mybir.AxisListType

P = 128
D_MODEL, SEQ, DEPTH, NB, DEC, PAST = 1024, 512, 2, 8, 8, 1024
NS = NB * DEC
T = SEQ + NS
HALF = T // 2
KC = D_MODEL // P
TT = SEQ // P
EPS = 1e-6
HEADS_A = HEADS_B = 4
DK_A, DK_B, DV, DH = 32, 64, 64, 64
AH = 8
GROUPS = ((128, 1), (512, 4), (2048, 16))
RANK = 16
FE = 11
EXPERTS = (2, 8)
BLK = 16
NBLK = P // BLK
R = 6
SLOT = FE * P

JOBS = [("lr", 0), ("bf", 0), ("bq", 1), ("aq", 0), ("bf", 1), ("gu", 0), ("bq", 0), ("ak", 0),
        ("g", 0), ("g", 1), ("g", 2), ("g", 3)]
for _i in range(8 + 2):
    if _i < 8:
        JOBS.append(("c", _i))
    if 0 <= _i - 1 < 8:
        JOBS.append(("s", _i - 1))
    if 0 <= _i - 2:
        JOBS.append(("r", _i - 2))
NJ = len(JOBS)
JOB_AT = {j: n for n, j in enumerate(JOBS)}
HAS_W = [k not in ("gu", "s", "r") for k, _ in JOBS]
HAS_ACT = [k in ("bf", "bq", "g", "c", "s") for k, _ in JOBS]
HAS_DVE = [k not in ("c", "bq", "g") for k, _ in JOBS]
ACT_N = np.cumsum(HAS_ACT).tolist()
DVE_N = np.cumsum(HAS_DVE).tolist()
NFEAT = sum(HAS_W)
NV = 8
U_IN = NV + NFEAT
U_OUT = KC
U_EXP = 2 * FE + KC
RING0 = [0, U_IN + U_OUT + EXPERTS[0] * U_EXP]
NVU = NV - 2
UD0 = [0, NVU + U_OUT + EXPERTS[0] * U_EXP]
UD_ITEMS = UD0[1] + NVU + U_OUT
PF0 = [0, U_OUT + EXPERTS[0] * KC]

ITEMS = ([("eb", 0), ("kd", 0), ("qt", 0)] + [("kt", i) for i in range(1, NBLK)]
         + [("pj", j) for j in range(BLK)] + [("sj", j) for j in range(DEC)])
NI = len(ITEMS)
FIRST, REST = ITEMS[:2 + NBLK], ITEMS[2 + NBLK:]
EARLY = 7
ITEM_AT = {x: n for n, x in enumerate(ITEMS)}
CAP = 160
N_EXP = 8
PER_EXP = -(-T // CAP)
MAX_ITEMS = N_EXP + 2 * T // CAP
CAP2 = CAP - P
UNITS = []
for _f in range(FE + 1):
    if _f < FE:
        UNITS += [("gate", _f), ("up", _f)]
    if _f >= 1:
        UNITS.append(("down", _f - 1))
U_ITEM = len(UNITS)
NSPLIT = 3
AHEAD = 2
assert U_EXP % NSPLIT == 0
UNIT_AT = {u: n for n, u in enumerate(UNITS)}
SLOT_USES = [len(range(s, U_ITEM, R)) for s in range(R)]
CT = 3
CT_HEADS = (4, 2, 2)

CONSTS = [("ones", P), ("lnc", SEQ), ("smask", PAST), ("smask_new", NB * NS), ("cos", T), ("sin", T), ("mask16", P),
          ("mask8", NS), ("ident", P), ("bones", P),
          ("rot", P), ("reset", T), ("maskb", NB), ("riota", 8), ("before", P), ("slots", CAP), ("rows", 2), ("heads4", 4), ("heads2", 2),
          ("to_row", 64 + 4 * (BLK - 1)), ("of_row16", P), ("of_row8", NS), ("rows4", 4), ("rows2", 2)]
COFF, _o = {}, 0
for _n, _w in CONSTS:
    COFF[_n] = (_o, _w)
    _o += _w
NCONST = _o
VECS = [("g_mix", KC), ("g_ffn", KC), ("b_gate", 1), ("g_gla", 1), ("g_hgrn", 1), ("g_q", 1), ("g_k", 1)]
VOFF, _o = {}, 0
for _n, _w in VECS:
    VOFF[_n] = (_o, _w)
    _o += _w
NVEC = _o


def multiplicity(dist):
    n = np.zeros(dist.shape, np.float64)
    for window, dil in GROUPS:
        n += (dist >= 0) & (dist <= window) & (dist % dil == 0)
    return n


def log_mult(dist, valid):
    n = np.where(valid, multiplicity(dist), 0)
    return np.where(n > 0, np.log(np.maximum(n, 1)), -1e30).astype(np.float32)


def shape_constants():
    c = {}
    p = np.arange(P)[:, None]
    u = np.arange(SEQ)[None, :]
    c["lnc"] = log_mult(SEQ - P + p - u, SEQ - P + p - u >= 0)
    row = p % 32
    t = row % DEC
    live = row < 2 * DEC
    d = PAST + t - np.arange(PAST)[None, :]
    c["smask"] = np.where(live, log_mult(d, d >= 0), 0).astype(np.float32)
    key = np.arange(NS)[None, :]
    new = []
    for b in range(NB):
        d = t - key % DEC
        new.append(np.where(live, log_mult(d, (d >= 0) & (key // DEC == b)), 0).astype(np.float32))
    c["smask_new"] = np.concatenate(new, 1)
    pos = np.concatenate([np.arange(SEQ), np.tile(PAST + np.arange(DEC), NB)]).astype(np.float32)
    rot_dim = DH // 4
    inv = (np.float32(500000.0) ** (-np.arange(0, rot_dim, 2, dtype=np.float32) / np.float32(rot_dim))).astype(np.float32)
    ang = pos[:, None] * inv[None, :]
    cos, sin = np.ones((P, T), np.float32), np.zeros((P, T), np.float32)
    rot = np.zeros((P, P), np.float32)
    for h in range(2):
        for i in range(rot_dim // 2):
            a, b = h * DH + i, h * DH + rot_dim // 2 + i
            cos[a] = cos[b] = np.cos(ang[:, i])
            sin[a] = sin[b] = np.sin(ang[:, i])
            rot[b, a] = -1.0
            rot[a, b] = 1.0
    c["cos"], c["sin"], c["rot"] = cos, sin, rot
    q = np.arange(P)[None, :]
    c["mask16"] = ((p // BLK == q // BLK) & (q >= p)).astype(np.float32)
    q = np.arange(NS)[None, :]
    c["mask8"] = ((p // DEC == q // DEC) & (q >= p)).astype(np.float32)
    c["ident"] = np.eye(P, dtype=np.float32)
    c["ones"] = np.ones((P, P), np.float32)
    c["bones"] = (p // DH == np.arange(P)[None] // DH).astype(np.float32)
    reset = np.ones(T, np.float32)
    reset[0:SEQ:P] = 0
    reset[SEQ::DEC] = 0
    c["reset"] = np.broadcast_to(reset[None], (P, T))
    c["maskb"] = (p // DEC == np.arange(NB)[None]).astype(np.float32)
    c["riota"] = np.broadcast_to(8.0 - np.arange(8)[None], (P, 8))
    c["before"] = (p < np.arange(P)[None]).astype(np.float32)
    c["slots"] = np.broadcast_to(np.arange(CAP)[None], (P, CAP))
    c["rows"] = np.concatenate([p, P + p], 1)
    for nh in (4, 2):
        c[f"heads{nh}"] = (p // (P // nh) == np.arange(nh)[None]).astype(np.float32)
        c[f"rows{nh}"] = (p % 4 * nh // 4 == np.arange(nh)[None]).astype(np.float32)
    q = np.arange(64 + 4 * (BLK - 1))[None, :] - 4 * (BLK - 1)
    c["to_row"] = (q == p // 32).astype(np.float32)
    c["of_row8"] = (p // 4 == np.arange(NS)[None] % DEC).astype(np.float32)
    c["of_row16"] = (p // 4 == np.arange(P)[None] % BLK).astype(np.float32)
    return np.ascontiguousarray(np.concatenate([c[n].astype(np.float32) for n, _ in CONSTS], 1))


def build(nc, d):
    ctx = ExitStack()
    with ctx:
        def sb(name, cols):
            return ctx.enter_context(nc.sbuf_tensor(name, [P, cols], F32))

        def sem(name):
            return ctx.enter_context(nc.semaphore(name))

        def tiles(ap, n):
            return ap.rearrange("p (n t) -> p n t", n=n)

        X = tiles(sb("residual", KC * T), KC)
        ring = tiles(sb("weight_ring", R * SLOT), R)
        C = sb("constants", NCONST)
        const = {n: C[:, o:o + w] for n, (o, w) in COFF.items()}
        VEC = sb("vectors", DEPTH * NVEC)
        LB = sb("lower_bounds", 32)
        WU = sb("gla_gate_up", DEPTH * P)
        SM = sb("small", 64 + CT * 12)
        item_tab = ctx.enter_context(nc.sbuf_tensor("item_table", [1, MAX_ITEMS + 2], mybir.dt.int32))
        N_LIN, N_SCR = 13 * T, 12736
        N_PROJ = 7 * T
        with ExitStack() as over:
            over.enter_context(nc.sbuf_tensor("below_proj_1", [P, (TT + 1) * D_MODEL + N_LIN], F32))
            Ph = tiles(over.enter_context(nc.sbuf_tensor("proj_in_hi", [P, KC * T], F32R)), KC)
            over.enter_context(nc.sbuf_tensor("below_proj_2", [P, 8 * T + N_PROJ], F32))
            Pl = tiles(over.enter_context(nc.sbuf_tensor("proj_in_lo", [P, KC * T], F32R)), KC)
            Uh, Ul = (tiles(over.enter_context(nc.sbuf_tensor(n, [P, 2 * 1024], F32R)), 2) for n in ("proj_weights_hi", "proj_weights_lo"))
        with ExitStack() as over:
            Hh, Hl = (tiles(over.enter_context(nc.sbuf_tensor(n, [P, KC * T], F32R)), KC) for n in ("ffn_in_hi", "ffn_in_lo"))
            hidh, hidl = (tiles(over.enter_context(nc.sbuf_tensor(n, [P, FE * T], F32R)), FE) for n in ("hidden_hi", "hidden_lo"))
            ft = tiles(over.enter_context(nc.sbuf_tensor("ffn_temps", [P, 4 * T], F32)), 4)
            Wh, Wl = (tiles(over.enter_context(nc.sbuf_tensor(n, [P, NSPLIT * SLOT], F32R)), NSPLIT) for n in ("weights_hi", "weights_lo"))
        with ExitStack() as over:
            over.enter_context(nc.sbuf_tensor("below_experts", [P, (TT + 1) * D_MODEL + N_LIN], F32))
            Yh, Yl = (tiles(over.enter_context(nc.sbuf_tensor(n, [P, 2 * D_MODEL], F32R)), 2) for n in ("item_out_hi", "item_out_lo"))
            SelT = tiles(over.enter_context(nc.sbuf_tensor("slots_tokens", [P, 2 * T], F32R)), 2)
        V = tiles(sb("values", (TT + 1) * D_MODEL), TT + 1)
        LIN = sb("linear", N_LIN)
        Q, K, B = (tiles(LIN[:, i * 3 * T:(i + 1) * 3 * T], 3) for i in range(3))
        G = tiles(LIN[:, 9 * T:13 * T], 4)
        H = tiles(sb("normed_or_mixed", KC * T), KC)
        mix = H
        QK = tiles(sb("attn_qk", 8 * T), 8)
        SCR = sb("scratch", N_SCR)

        def vec(L, name):
            o, w = VOFF[name]
            return VEC[:, L * NVEC + o:L * NVEC + o + w]

        def carve(base, *sizes):
            out, o = [], 0
            for s in sizes:
                out.append(base[:, o:o + s])
                o += s
            return out

        eps_col = SM[:, 32:33]
        negmax = SM[:, 40:48]
        den = SM[:, 48:56]
        rden = SM[:, 56:64]
        ebl = tiles(SM[:, 64:64 + CT * 12], CT)
        lb = LB[:, 0:4]
        oml = LB[:, 4:8]
        e0, e1s, rinvs = (tiles(x, 2) for x in carve(SCR, 2 * T, 2 * T, 2 * T))
        rtmp = SCR[:, 6 * T:7 * T]
        lr_sb = G[0:RANK, 3, :]
        sq = tiles(SCR[:, 64:64 + 4 * T], 4)
        rinv = SCR[:, 5 * T:6 * T]
        (qe_, kdt_, kt_, qt, dring_, a_, kd, vbd, pring_) = carve(
            SCR, CT * T, (TT + 1) * P, (NBLK - 1) * SEQ, SEQ, 3 * T, 4 * T, T, 512, 2 * T)
        Qbd = [ring[:, i - 1, 1024:1024 + TT * 64] if i <= 5 else qt[:, (i - 6) * 256:(i - 5) * 256] for i in range(1, NBLK)]
        vbds = (vbd, kd[:, 0:512])
        Qe = tiles(qe_, CT)
        KdT = tiles(kdt_, TT + 1)
        Kt = kt_.rearrange("p (i c s) -> p i c s", i=NBLK - 1, c=TT)
        Dr = tiles(dring_, 3)
        A = tiles(a_, 4)
        Pr = tiles(pring_, 2)
        osq, orinv = Pr[:, 0, :], Pr[:, 1, :]
        S = H[:, 4:8, :].rearrange("p a t -> p (a t)")[:, 0:CT * 4 * DV].rearrange("p (c k v) -> p c k v", c=CT, k=4)
        S0 = H[:, 4:8, :].rearrange("p a t -> p (a t)")[:, 768:768 + CT * NB * DV].rearrange(
            "p (c b v) -> p c b v", c=CT, b=NB)
        (p_, pt_, *pieces) = carve(SCR, 2 * (PAST + NS), 2 * 9 * P, 2048, 2048, 2048, 2048)
        pieces += carve(LIN, 2048, 2048, 2048)
        NPC = len(pieces)
        Pp = tiles(p_[:, 0:2048], 4)
        Ps = tiles(p_, 2)
        PTp = tiles(pt_[:, 0:1024], 2)
        PTs = tiles(pt_, 2)
        Os = LIN[:, 7168:7168 + P]
        Qs = LIN[:, 6144:7168].rearrange("p (b h q) -> p b h q", b=NB, h=4)
        sqf = tiles(SCR[:, 11 * T:15 * T], 4)
        rinv_f = SCR[:, 6 * T:7 * T]
        H_tok = V
        xg_, hidg_, tg_, yt_, sel_, selw_, selt = carve(
            SCR, KC * CAP, FE * CAP, 2 * CAP, KC * CAP, (TT + 1) * CAP, 2 * T, T)
        Xg, hidg, tg, Yt = tiles(xg_, KC), tiles(hidg_, FE), tiles(tg_, 2), tiles(yt_, KC)
        Sel, SelW = tiles(sel_, TT + 1), tiles(selw_, 2)
        slot_w = LB[:, 10:12]
        rows4 = tiles(LIN[:, 0:4 * T], 4)
        RW = LIN[:, 4 * T:4 * T + 512]
        WRT = LIN[:, 4 * T + 512:4 * T + 576]

        ps = ctx.enter_context(nc.psum_tensor("ps", [P, 8, 512], F32))

        def pair(k):
            return ps[:, 2 * k:2 * k + 2, 0:HALF]

        def split(ap):
            return ap.rearrange("p (a t) -> p a t", a=2)

        router_in = sem("router_in")
        x_in, c_in, rest_in, w_land = [sem(f"x_in{i}") for i in range(4)], sem("vectors_in"), sem("consts_in"), [sem(f"weights_in{i}") for i in range(R)]
        s0_in = [sem("gla_state_in"), sem("hgrn_state_in")]
        piece_in = [sem(f"cache_piece_in{i}") for i in range(NPC)]
        stored_s, shifted, stored_y = sem("states_out"), sem("caches_shifted"), sem("y_out")
        stored_kv = sem("new_kv_out")
        lb_exp, lb_ready, eps_ready, kt_zero = (sem(n) for n in ("lb_exp", "lb_ready", "eps_ready", "kt_zeroed"))
        sq_ready, sq_used, rinv_ready, h_ready = (sem(n) for n in ("sq_ready", "sq_used", "rinv_ready", "h_ready"))
        v_ready, v_half = sem("v_ready"), sem("v_product")
        unit_done, pe_job, act_job, dve_job = (sem(n) for n in ("unit_done", "pe_job", "act_job", "dve_job"))
        out_evac = sem("out_evac")
        dch, ach = sem("dve_chain"), sem("act_chain")
        lf_abs, lf_ready = sem("lf_abs"), sem("logf_ready")
        diff_ready, exp_ready, term_ready = sem("diff_ready"), sem("exp_ready"), sem("term_ready")
        prod_used, off_done, diag_done, samp_done = (sem(n) for n in ("prod_used", "off_done", "diag_done", "samp_done"))
        kdt_ps, kdt_ready, a_ready, as_ready = (sem(n) for n in ("kdt_ps", "kdt_ready", "a_ready", "as_ready"))
        e_ready, es_ready, at_done, ats_done = (sem(n) for n in (
            "in_block_rows", "in_block_rows_samples", "in_block_spread", "in_block_spread_samples"))
        upd_done, s_ready, vbd_ready, vbd_used, supd_done, sn_ready = (sem(n) for n in (
            "upd_done", "s_ready", "vbd_ready", "vbd_used", "supd_done", "sn_ready"))
        o_done, osq_ready, oss_done, orinv_ready, mixl_ready = (sem(n) for n in (
            "o_done", "osq_ready", "oss_done", "orinv_ready", "mixl_ready"))
        sc_done, sc_free, mx_ready, p_ready, pn_ready, pt_ps, pt_ready, pv_done, mixc_ready = (sem(n) for n in (
            "sc_done", "sc_free", "mx_ready", "p_ready", "pn_ready", "pt_ps", "pt_ready", "pv_done", "mixc_ready"))
        qs_ready, spv_half, os_ready, os_turned = (sem(n) for n in ("qs_ready", "spv_half", "sample_out_ready", "sample_out_turned"))
        ssc_done, ssc_free, smx_ready, sp_ready, spt_ps, spt_ready, spv_done, smix_ready = (sem(n) for n in (
            "ssc_done", "ssc_free", "smx_ready", "sp_ready", "spt_ps", "spt_ready", "spv_done", "smix_ready"))
        sig_ready = sem("sig_ready")
        pf_ready, phi_ready, uhi_ready, u_split = (sem(n) for n in (
            "proj_float_ready", "proj_hi_ready", "proj_weights_hi_ready", "proj_weights_split"))
        hf_ready, hhi_ready, whi_ready, w_split, prod_ready, hidhi_ready, hidlo_ready = (sem(n) for n in (
            "h_float_ready", "h_hi_ready", "weights_hi_ready", "weights_split", "hidden_float", "hidden_hi", "hidden_lo"))
        htok_ps, htok_ready, rl_done, rexp, rexp_done, chosen, ranked, coded, rows_ps, rows_ready, items_ready = (
            sem(n) for n in ("htok_ps", "htok_ready", "logits_done", "gate_diff", "gate_exp", "chosen", "ranked", "coded",
                             "rows_ps", "rows_ready", "items_ready"))
        yhi_ready, slotw_ready = sem("item_out_hi_ready"), sem("slot_weights_ready")
        silu_ready, hid_ready, yt_ready, ytok_ps, ytok_ready = (sem(n) for n in (
            "silu_ready", "hid_ready", "yt_ready", "ytok_ps", "ytok_ready"))
        sel_ready, selw_ready, gathered, xg_ready, scattered, experts_done = (sem(n) for n in (
            "sel_ready", "selw_ready", "gathered", "xg_ready", "scattered", "experts_done"))

        block = ctx.enter_context(nc.Block())

        def ud_ffn(L):
            return UD0[L] + NVU + U_OUT

        def pf_ffn(L):
            return PF0[L] + U_OUT

        released = []
        for L in range(DEPTH):
            for half in range(2):
                released += [(unit_done, UD0[L] + 3 * half + u + 1) for u in range(3)] + [(v_half, 10 * L + 5 * half + 5)]
            released += [(pe_job, L * NJ + n + 1) for n in range(NJ) if HAS_W[n]]
            released += [(unit_done, UD0[L] + NVU + u + 1) for u in range(U_OUT + (EXPERTS[0] * U_EXP if L == 0 else 0))]
        landings = [len(range(s, len(released), R)) for s in range(R)]

        piece_order = [(b - (part >= 2), part) for b in range(NB + 1) for part in range(4)
                       if 0 <= b - (part >= 2) < NB]

        def cache_piece(L, b, part):
            n = piece_order.index((b, part))
            return L * len(piece_order) + n, n % NPC

        last_piece, piece_count = {}, {}
        uses, user = [0] * NPC, [None] * NPC
        for L in range(DEPTH):
            for b, part in piece_order:
                m, slot = cache_piece(L, b, part)
                last_piece[m] = user[slot]
                user[slot] = (L, b, part)
                uses[slot] += 1
                piece_count[m] = uses[slot]

        def piece_landed(eng, L, b, part):
            m, slot = cache_piece(L, b, part)
            eng.wait_ge(piece_in[slot], 16 * piece_count[m])
            return pieces[slot]

        def chunk_rows(h, n):
            w = P // n
            return slice(h * w, h * w + w)

        @block.sync
        def _(sp):
            for i in range(4):
                sp.dma_start(X[:, 2 * i:2 * i + 2, :], d["x"][:, 2 * i:2 * i + 2]).then_inc(x_in[i], 16)
            for dst, src in ((C[:, 0:P], d["consts"][:, 0:P]), (VEC[:, :], d["vecs"]), (LB[:, 16:20], d["lb_logits"]),
                             (WU[0:RANK, :], d["w_up"])):
                sp.dma_start(dst, src).then_inc(c_in, 16)

            def slot_for(n):
                if n >= R:
                    s, v = released[n - R]
                    sp.wait_ge(s, v)
                return n % R

            old_k, new_k = (d[x].rearrange("l b p h s -> (l b) p h s") for x in ("kcache", "ok_s"))
            old_v, new_v = (d[x].rearrange("l b p c e -> (l b) p c e") for x in ("vcache", "ov_s"))

            def shift(q, values):
                if values:
                    o, n_ = (x[bass.ds(q, 1)].rearrange("o p c e -> (o p) (c e)") for x in (old_v, new_v))
                    sp.dma_start(n_[0:P - 1], o[1:P]).then_inc(shifted, 16)
                else:
                    o, n_ = (x[bass.ds(q, 1)].rearrange("o p h s -> (o p) h s") for x in (old_k, new_k))
                    sp.dma_start(n_[:, :, 0:PAST - DEC], o[:, :, DEC:PAST]).then_inc(shifted, 16)

            for L in range(DEPTH):
                n = RING0[L]
                for u in range(NV):
                    s = slot_for(n)
                    sp.dma_start(ring[:, s, 0:1024], d["w_v"][L, u]).then_inc(w_land[s], 16)
                    if L == 0 and u == 1:
                        sp.dma_start(C[:, P:], d["consts"][:, P:]).then_inc(rest_in, 16)
                    n += 1
                f = 0
                for kind, i in JOBS:
                    if kind in ("gu", "s", "r"):
                        continue
                    s = slot_for(n)
                    sp.dma_start(ring[:, s, 0:1024], d["w_feat"][L, f]).then_inc(w_land[s], 16)
                    f += 1
                    n += 1
                    if f % 3 == 0 and 1 <= f // 3 <= 6:
                        k = f // 3 - 1
                        shift((0, 13)[L] + k // 2, k % 2)
                for u in range(U_OUT):
                    s = slot_for(n)
                    sp.dma_start(ring[:, s, 0:1024], d["w_out"][L, u]).then_inc(w_land[s], 16)
                    n += 1
                    if u == R - 1:
                        sp.wait_ge(sn_ready, CT * (L + 1))
                        sp.wait_ge(mixl_ready, 4 * (L + 1))
                        for at, (b, part) in enumerate(piece_order):
                            m, slot = cache_piece(L, b, part)
                            if at >= NPC:
                                _, bb, pp = last_piece[m]
                                sp.wait_ge((ssc_done, ssc_done, spv_half, spv_done)[pp], L * NB + bb + 1)
                            if part < 2:
                                sp.dma_start(tiles(pieces[slot], 2), d["kcache"][L, b][:, 2 * part:2 * part + 2]).then_inc(piece_in[slot], 16)
                            else:
                                k = 4 * (part - 2)
                                sp.dma_start(tiles(pieces[slot], 4), d["vcache"][L, b][:, k:k + 4]).then_inc(piece_in[slot], 16)
                if L:
                    continue
                base_ud, base_ring = ud_ffn(L), n
                with sp.Fori(0, EXPERTS[L]) as e:
                    for j in range(U_EXP):
                        s = (base_ring + j) % R
                        sp.wait_ge(unit_done, e * U_EXP + (base_ud + j - R + 1))
                        if j < 2 * FE:
                            src = d["w_gu"][bass.ds(e * (2 * FE) + j, 1)].rearrange("o p c -> (o p) c")
                            sp.dma_start(ring[:, s, 0:1024], src).then_inc(w_land[s], 16)
                            if j % 2 == 0 and j < 20:
                                shift(e * 5 + (3 + j // 4), (j // 2) % 2)
                        else:
                            src = d["w_dn"][bass.ds(e * KC + (j - 2 * FE), 1)].rearrange("o p c -> (o p) c")
                            sp.dma_start(ring[:, s, :], src).then_inc(w_land[s], 16)
            sp.wait_ge(unit_done, UD0[1] + NVU + 1)
            sp.dma_start(WRT, d["w_router"]).then_inc(router_in, 16)
            sp.wait_ge(unit_done, UD_ITEMS)
            sp.wait_ge(items_ready, 1)
            n_items = sp.value_load(item_tab[0:1, MAX_ITEMS:MAX_ITEMS + 1], min_val=N_EXP, max_val=MAX_ITEMS)
            with sp.Fori(0, n_items) as i:
                x = sp.value_load(item_tab[0:1, bass.ds(i, 1)], min_val=0, max_val=N_EXP - 1)
                for j, (kind, f) in enumerate(UNITS):
                    s = j % R
                    last = j - R if j >= R else max(range(s, U_ITEM, R)) - U_ITEM
                    sp.wait_ge(unit_done, i * U_ITEM + (UD_ITEMS + last + 1))
                    if kind == "down":
                        src = d["w_dn_moe"][bass.ds(x * FE + f, 1)]
                    else:
                        src = d["w_gu"][bass.ds(x * (2 * FE) + (EXPERTS[0] * 2 * FE + 2 * f + (kind == "up")), 1)]
                    sp.dma_start(ring[:, s, 0:1024], src.rearrange("o p c -> (o p) c")).then_inc(w_land[s], 16)
            sp.wait_ge(experts_done, 1)
            sp.wait_ge(shifted, 16 * 2 * DEPTH * NB)
            sp.dma_start(d["y"], X[:, :, :]).then_inc(stored_y, 16)
            sp.wait_ge(stored_y, 16)

        @block.gpsimd
        def _(pool):
            pool.wait_ge(rest_in, 16)
            for L in range(DEPTH):
                for c in range(KC):
                    pool.wait_ge(phi_ready, L * KC + c + 1)
                    nc.gpsimd.tensor_tensor(Pl[:, c, :], sq[:, c % 4, :], Ph[:, c, :], ALU.subtract).then_inc(h_ready, 1)
                pool.wait_ge(pe_job, (L + 1) * NJ)
                pool.dma_start(S0[:, 0, :, :], d["s0_gla"][L]).then_inc(s0_in[0], 16)
                pool.dma_start(S0[:, 1:3, :, :], d["s0_hgrn"][L]).then_inc(s0_in[1], 16)
                pool.wait_ge(dve_job, (L + 1) * DVE_N[-1])
                pool.wait_ge(v_ready, 10 * (L + 1))
                pool.dma_start(d["ok_p"][L], QK[:, 4:8, 0:SEQ]).then_inc(stored_kv, 16)
                pool.dma_start(d["ov_p"][L], V[:, 0:TT, 512:1024]).then_inc(stored_kv, 16)
                for ct in range(CT):
                    Bp = B[:, ct, 0:SEQ].rearrange("p (c s) -> p c s", c=TT)
                    Bs = B[:, ct, SEQ:T].rearrange("p (b s) -> p b s", b=NB)
                    Bb = B[:, ct, 0:SEQ].rearrange("p (n s) -> p n s", s=BLK)
                    for kind, i in ITEMS:
                        it = L * CT * NI + ct * NI + ITEM_AT[(kind, i)]
                        if kind == "eb":
                            continue
                        D = Dr[:, it % 3, :]
                        if it >= 3:
                            pool.wait_ge(term_ready, it - 2)
                        if kind == "kt" and ct == 0:
                            nc.gpsimd.memset(Kt[:, i - 1, :, BLK * i:P], 0.0).then_inc(kt_zero, 1)
                        Dp = D[:, 0:SEQ].rearrange("p (c s) -> p c s", c=TT)
                        Ds = D[:, SEQ:T].rearrange("p (b s) -> p b s", b=NB)
                        if kind == "kd":
                            nc.gpsimd.tensor_tensor(Dp, Bp[:, :, P - 1:P].to_broadcast([P, TT, P]), Bp, ALU.subtract)
                            op = nc.gpsimd.tensor_tensor(Ds, Bs[:, :, DEC - 1:DEC].to_broadcast([P, NB, DEC]), Bs, ALU.subtract)
                        elif kind == "qt":
                            for c in range(TT):
                                b1 = Bp[:, c, BLK:P].rearrange("p (n s) -> p n s", s=BLK)
                                r1 = Bp[:, c, 0:P - BLK].rearrange("p (n s) -> p n s", s=BLK)[:, :, BLK - 1:BLK]
                                op = nc.gpsimd.tensor_tensor(
                                    Dp[:, c, BLK:P].rearrange("p (n s) -> p n s", s=BLK), b1,
                                    r1.to_broadcast([P, NBLK - 1, BLK]), ALU.subtract)
                        elif kind == "kt":
                            w = BLK * i
                            op = nc.gpsimd.tensor_tensor(Dp[:, :, 0:w], Bp[:, :, w - 1:w].to_broadcast([P, TT, w]),
                                                         Bp[:, :, 0:w], ALU.subtract)
                        elif kind == "pj":
                            w = BLK - i
                            op = nc.gpsimd.tensor_tensor(
                                D[:, 0:32 * w].rearrange("p (n s) -> p n s", s=w), Bb[:, :, i:BLK],
                                Bb[:, :, i:i + 1].to_broadcast([P, SEQ // BLK, w]), ALU.subtract)
                        else:
                            w = DEC - i
                            op = nc.gpsimd.tensor_tensor(
                                D[:, 0:NB * w].rearrange("p (n s) -> p n s", s=w), Bs[:, :, i:DEC],
                                Bs[:, :, i:i + 1].to_broadcast([P, NB, w]), ALU.subtract)
                        op.then_inc(diff_ready, 1)
                    for h in range(CT_HEADS[ct]):
                        hh = (0, 4, 6)[ct] + h
                        if L * 8 + hh >= 2:
                            pool.wait_ge(vbd_used, L * 8 + hh - 1)
                        pool.wait_ge(kdt_ps, CT * L + ct + 1)
                        v = V[0:NS, TT, hh * DV:hh * DV + DV].rearrange("p (o v) -> p o v", o=1)
                        nc.gpsimd.tensor_tensor(
                            vbds[hh % 2][0:NS, :].rearrange("p (b v) -> p b v", b=NB), v.to_broadcast([NS, NB, DV]),
                            const["maskb"][0:NS, :].rearrange("p (b o) -> p b o", o=1).to_broadcast([NS, NB, DV]),
                            ALU.mult).then_inc(vbd_ready, 1)
                pool.wait_ge(s_ready, CT * (L + 1))
                pool.dma_start(d["os_gla_p"][L], S[:, 0, 3, :]).then_inc(stored_s, 16)
                pool.dma_start(d["os_hgrn_p"][L], S[:, 1:3, 3, :]).then_inc(stored_s, 16)
                pool.wait_ge(sn_ready, CT * (L + 1))
                pool.dma_start(d["os_gla_s"][L], S0[:, 0, :, :]).then_inc(stored_s, 16)
                pool.dma_start(d["os_hgrn_s"][L], S0[:, 1:3, :, :]).then_inc(stored_s, 16)
                for b in range(NB):
                    s = SEQ + DEC * b
                    pool.dma_start(d["ok_s"][L, b][:, :, PAST - DEC:PAST], QK[:, 4:8, s:s + DEC]).then_inc(stored_kv, 16)
                    pool.dma_start(d["ov_s"][L, b][P - 1], V[DEC * b:DEC * b + DEC, TT, 512:1024]).then_inc(stored_kv, 16)
                pool.wait_ge(stored_kv, (L + 1) * 16 * (2 + 2 * NB))
                pool.wait_ge(stored_s, (L + 1) * 64)
                if L == 0:
                    for c in range(KC):
                        pool.wait_ge(hhi_ready, c + 1)
                        nc.gpsimd.tensor_tensor(Hl[:, c, :], ft[:, c % 4, :], Hh[:, c, :], ALU.subtract).then_inc(h_ready, 1)

        @block.scalar
        def _(act):
            chain = [0]

            def link(op):
                op.then_inc(ach, 1)
                chain[0] += 1
                act.wait_ge(ach, chain[0])

            def norm(k, buf, out, wait_x):
                for c in range(KC):
                    wait_x(c)
                    if c >= 4:
                        act.wait_ge(sq_used, KC * k + c - 3)
                    nc.scalar.activation(buf[:, c % 4, :], X[:, c, :], ACT.Square).then_inc(sq_ready, 1)
                act.wait_ge(sq_used, KC * k + KC)
                link(nc.scalar.activation(split(out), pair(0), ACT.Ln, bias=eps_col, scale=1.0 / D_MODEL))
                nc.scalar.activation(out, out, ACT.Exp, scale=-0.5).then_inc(rinv_ready, 1)

            act.wait_ge(c_in, 16 * 4)
            act.wait_ge(lb_ready, 1)
            nc.scalar.activation(LB[:, 20:24], LB[:, 24:28], ACT.Exp).then_inc(lb_exp, 1)
            act.wait_ge(eps_ready, 1)
            for L in range(DEPTH):
                def wait_mix(c, L=L):
                    if L == 0:
                        act.wait_ge(x_in[c // 2], 16)
                    else:
                        act.wait_ge(out_evac, pf_ffn(0) + KC + c + 1)
                norm(2 * L, sq, rinv, wait_mix)

                def hi(u, L=L):
                    n = RING0[L] + u
                    if u >= 2:
                        act.wait_ge(*released[n - 2])
                    act.wait_ge(w_land[n % R], 16 * (n // R + 1))
                    nc.scalar.activation(Uh[:, u % 2, :], ring[:, n % R, 0:1024], ACT.Copy).then_inc(uhi_ready, 1)

                hi(0)
                for c in range(KC):
                    act.wait_ge(pf_ready, L * KC + c + 1)
                    nc.scalar.activation(Ph[:, c, :], sq[:, c % 4, :], ACT.Copy).then_inc(phi_ready, 1)
                    if c == 1:
                        hi(1)
                for n in range(10):
                    if n % 5 == 0:
                        for u in ((2, 3, 4), (5, 6, 7, 8))[n // 5]:
                            hi(u)
                    act.wait_ge(v_half, 10 * L + n + 1)
                    half, tt = n // 5, n % 5
                    rows = P if tt < TT else NS
                    if L and n == 0:
                        act.wait_ge(stored_kv, 16 * (2 + 2 * NB))
                    nc.scalar.activation(V[0:rows, tt, half * 512:half * 512 + 512], ps[P - rows:P, n % 8, :],
                                         ACT.Copy).then_inc(v_ready, 1)
                for n, (kind, i) in enumerate(JOBS):
                    if HAS_W[n] and NV + sum(HAS_W[:n]) + 1 < U_IN:
                        hi(NV + sum(HAS_W[:n]) + 1)
                    if not HAS_ACT[n]:
                        continue
                    if (kind, i) == ("g", 0):
                        act.wait_ge(lf_abs, L + 1)
                        link(nc.scalar.activation(rtmp, rtmp, ACT.Exp, scale=-1.0))
                        nc.scalar.activation(rtmp, rtmp, ACT.Ln, bias=1.0).then_inc(lf_ready, 1)
                        nc.scalar.activation(B[:, 1, :], B[:, 1, :], ACT.Ln)
                        nc.scalar.activation(B[:, 2, :], B[:, 2, :], ACT.Ln).then_inc(lf_ready, 1)
                    act.wait_ge(pe_job, L * NJ + n + 1)
                    src = pair((n + 1) % 4)
                    if kind in ("bf", "bq", "g"):
                        if n >= 3:
                            act.wait_ge(dve_job, L * DVE_N[-1] + DVE_N[n - 3])
                        if kind == "bf":
                            nc.scalar.activation(split(e1s[:, n % 2, :]), src, ACT.Sigmoid, scale=-1.0)
                            op = nc.scalar.activation(split(e0[:, n % 2, :]), src, ACT.Sigmoid)
                        else:
                            dst = Q[:, 1 + i, :] if kind == "bq" else G[:, i, :]
                            op = nc.scalar.activation(split(dst), src, ACT.Silu)
                        op.then_inc(act_job, 1)
                    elif kind == "c":
                        if i < 2:
                            act.wait_ge(dve_job, L * DVE_N[-1] + DVE_N[JOB_AT[("g", 3)]])
                        else:
                            act.wait_ge(dve_job, L * DVE_N[-1] + DVE_N[JOB_AT[("s", i - 2)]])
                        nc.scalar.activation(split(e0[:, i % 2, :]), src, ACT.Copy)
                        nc.scalar.activation(split(e1s[:, i % 2, :]), src, ACT.Square).then_inc(act_job, 1)
                    else:
                        link(nc.scalar.activation(split(rinvs[:, i % 2, :]), src, ACT.Ln, bias=eps_col, scale=1.0 / DH))
                        nc.scalar.activation(rinvs[:, i % 2, :], rinvs[:, i % 2, :], ACT.Exp, scale=-0.5).then_inc(act_job, 1)
                def exps(ct, items, L=L):
                    for kind, i in items:
                        n = L * CT * NI + ct * NI + ITEM_AT[(kind, i)]
                        D = Dr[:, n % 3, :]
                        if kind == "eb":
                            act.wait_ge(dve_job, (L + 1) * DVE_N[-1])
                            if n >= 3:
                                act.wait_ge(term_ready, n - 2)
                            nc.scalar.activation(D, B[:, ct, :], ACT.Exp).then_inc(exp_ready, 1)
                            continue
                        act.wait_ge(diff_ready, (L * CT + ct) * (NI - 1) + ITEM_AT[(kind, i)])
                        if kind == "kd":
                            v = D
                        elif kind == "qt":
                            v = D[:, 0:SEQ].rearrange("p (c s) -> p c s", c=TT)[:, :, BLK:P]
                        elif kind == "kt":
                            v = D[:, 0:SEQ].rearrange("p (c s) -> p c s", c=TT)[:, :, 0:BLK * i]
                        elif kind == "pj":
                            v = D[:, 0:32 * (BLK - i)]
                        else:
                            v = D[:, 0:NB * (DEC - i)]
                        nc.scalar.activation(v, v, ACT.Exp).then_inc(exp_ready, 1)

                exps(0, FIRST)
                for ct in range(CT):
                    act.wait_ge(kdt_ps, CT * L + ct + 1)
                    nc.scalar.activation(KdT[:, 0:TT, :], ps[:, 0, :].rearrange("p (c s) -> p c s", c=TT), ACT.Copy)
                    nc.scalar.activation(KdT[0:NS, TT, :], ps[0:NS, 1, 0:P], ACT.Copy).then_inc(kdt_ready, 1)
                    exps(ct, REST)
                    if ct + 1 < CT:
                        exps(ct + 1, FIRST[:EARLY])
                    for k in range(CT_HEADS[ct] // 2):
                        m = (0, 2, 3)[ct] + k
                        bp, bs = 3 + 2 * k, 4 + 2 * k
                        act.wait_ge(o_done, 4 * L + m + 1)
                        if k:
                            act.wait_ge(mixl_ready, 4 * L + m)
                        act.wait_ge(term_ready, L * CT * NI + ct * NI + NI)
                        nc.scalar.activation(osq[:, 0:SEQ], ps[:, bp, :], ACT.Square)
                        nc.scalar.activation(osq[:, SEQ:T], ps[:, bs, 0:NS], ACT.Square).then_inc(osq_ready, 1)
                        if k == 0 and ct + 1 < CT:
                            exps(ct + 1, FIRST[EARLY:])
                        act.wait_ge(oss_done, 4 * L + m + 1)
                        nc.scalar.activation(orinv[:, 0:SEQ], ps[:, 7, :], ACT.Ln, bias=eps_col, scale=1.0 / DV)
                        link(nc.scalar.activation(orinv[:, SEQ:T], ps[:, 0, 0:NS], ACT.Ln, bias=eps_col, scale=1.0 / DV))
                        nc.scalar.activation(orinv, orinv, ACT.Exp, scale=-0.5).then_inc(orinv_ready, 1)
                n0 = 32 * L
                for n in range(32 + 3):
                    if n < 32:
                        w = P * (n % 4 + 1)
                        act.wait_ge(mx_ready, n0 + n + 1)
                        nc.scalar.activation(Pp[:, n % 4, 0:w], Pp[:, n % 4, 0:w], ACT.Exp, bias=negmax[:, n % 4:n % 4 + 1],
                                             accum_out=den[:, n % 4:n % 4 + 1]).then_inc(p_ready, 1)
                    k = n - 2
                    if 0 <= k < 32:
                        w = P * (k % 4 + 1)
                        act.wait_ge(pt_ps, n0 + k + 1)
                        if k >= 2:
                            act.wait_ge(pv_done, n0 + k - 1)
                        nc.scalar.activation(PTp[:, k % 2, 0:w], ps[:, 2 + k % 2, 0:w], ACT.Copy).then_inc(pt_ready, 1)
                    k = n - 3
                    if 0 <= k < 32 and k % 8 == 7:
                        act.wait_ge(pv_done, n0 + k + 1)
                        hp = k // 8
                        if hp == 0:
                            act.wait_ge(stored_s, 64 * (L + 1))
                        nc.scalar.activation(mix[:, 4 + hp, 0:SEQ], ps[:, 4 + hp % 2, :], ACT.Copy).then_inc(mixc_ready, 1)
                for b in range(NB + 1):
                    if b >= 1:
                        n = NB * L + b - 1
                        act.wait_ge(spt_ps, n + 1)
                        pt = PTs[:, (b - 1) % 2, :]
                        nc.scalar.activation(pt[:, 0:1024], ps[:, 3:5, :].rearrange("p a t -> p (a t)"), ACT.Copy)
                        nc.scalar.activation(pt[0:NS, 1024:1152], ps[0:NS, 5, 0:P], ACT.Copy).then_inc(spt_ready, 1)
                    if b < NB:
                        n = NB * L + b
                        act.wait_ge(smx_ready, n + 1)
                        nc.scalar.activation(Ps[:, b % 2, :], Ps[:, b % 2, :], ACT.Exp, bias=negmax[:, 4 + b % 2:5 + b % 2],
                                             accum_out=den[:, 4 + b % 2:5 + b % 2]).then_inc(sp_ready, 1)
                norm(2 * L + 1, sqf, rinv_f, lambda c: act.wait_ge(out_evac, PF0[L] + c + 1))
                if L == 0:
                    act.wait_ge(stored_kv, 16 * (2 + 2 * NB))
                    for c in range(KC):
                        act.wait_ge(hf_ready, c + 1)
                        nc.scalar.activation(Hh[:, c, :], ft[:, c % 4, :], ACT.Copy).then_inc(hhi_ready, 1)
                    n0 = RING0[0] + U_IN + U_OUT

                    def hi(e, j):
                        n, w = n0 + j, 1024 if j < 2 * FE else SLOT
                        act.wait_ge(w_land[n % R], e * (16 * U_EXP // R) + 16 * (n // R + 1))
                        act.wait_ge(unit_done, e * U_EXP + (ud_ffn(0) + j - NSPLIT + 1))
                        nc.scalar.activation(Wh[:, j % NSPLIT, 0:w], ring[:, n % R, 0:w], ACT.Copy).then_inc(whi_ready, 1)

                    with act.Fori(0, EXPERTS[0]) as e:
                        for j in range(AHEAD):
                            hi(e, j)
                        for j in range(U_EXP):
                            if j + AHEAD < U_EXP:
                                hi(e, j + AHEAD)
                            i = j // 2
                            if j < 2 * FE and j % 2 == 0:
                                act.wait_ge(unit_done, e * U_EXP + (ud_ffn(0) + j + 1))
                                if i >= 2:
                                    act.wait_ge(prod_ready, e * FE + (i - 1))
                                nc.scalar.activation(split(ft[:, i % 2, :]), pair(j % 4), ACT.Silu).then_inc(sig_ready, 1)
                            elif j < 2 * FE:
                                act.wait_ge(prod_ready, e * FE + (i + 1))
                                nc.scalar.activation(hidh[:, i, :], ft[:, 2 + i % 2, :], ACT.Copy).then_inc(hidhi_ready, 1)
            act.wait_ge(stored_kv, 2 * 16 * (2 + 2 * NB))
            for tt in range(TT + 1):
                rows = P if tt < TT else NS
                act.wait_ge(htok_ps, tt + 1)
                k = 2 * (tt % 2)
                nc.scalar.activation(H_tok[0:rows, tt, :].rearrange("p (a c) -> p a c", a=2), ps[0:rows, 4 + k:6 + k, :],
                                     ACT.Copy).then_inc(htok_ready, 1)
            act.wait_ge(rexp, 1)
            nc.scalar.activation(RW[:, 80:85], RW[:, 80:85], ACT.Exp).then_inc(rexp_done, 1)

            def copy_xg(count):
                act.wait_ge(gathered, count)
                for k in range(0, KC, 3):
                    m = min(3, KC - k)
                    op = nc.scalar.activation(Xg[:, k:k + m, :], ps[:, 5 + k // 3, 0:m * CAP].rearrange("p (k s) -> p k s", k=m), ACT.Copy)
                op.then_inc(xg_ready, 1)

            def copy_tok(count):
                act.wait_ge(ytok_ps, count)
                act.wait_ge(slotw_ready, 2 * count)
                for st, w, bank in ((0, P, 5), (1, CAP2, 0)):
                    nc.scalar.activation(Yh[0:w, st, :].rearrange("p (a c) -> p a c", a=2), ps[0:w, bank:bank + 2, :], ACT.Copy,
                                         scale=slot_w[0:w, st:st + 1]).then_inc(yhi_ready, 1)

            def item(i, before):
                for f in range(FE):
                    act.wait_ge(unit_done, i * U_ITEM + (UD_ITEMS + UNIT_AT[("up", f)] + 1))
                    if f >= 2:
                        act.wait_ge(hid_ready, i * FE + (f - 1))
                    nc.scalar.activation(tg[:, f % 2, :], ps[:, 3 + f % 2, 0:CAP], ACT.Silu).then_inc(silu_ready, 1)
                    if f == 0 and before is not None:
                        copy_tok(i)
                act.wait_ge(unit_done, i * U_ITEM + (UD_ITEMS + UNIT_AT[("up", FE - 1)] + 1))
                copy_xg(i + 2)
                act.wait_ge(unit_done, i * U_ITEM + (UD_ITEMS + U_ITEM))
                for k in range(0, KC, 3):
                    m = min(3, KC - k)
                    op = nc.scalar.activation(Yt[:, k:k + m, :], ps[:, k // 3, 0:m * CAP].rearrange("p (k s) -> p k s", k=m), ACT.Copy)
                op.then_inc(yt_ready, 1)

            copy_xg(1)
            act.wait_ge(items_ready, 1)
            last_item = act.value_load(item_tab[0:1, MAX_ITEMS + 1:MAX_ITEMS + 2], min_val=N_EXP - 1, max_val=MAX_ITEMS - 1)
            item(0, None)
            with act.Fori(0, last_item) as before:
                item(before + 1, before)
            copy_tok(last_item + 1)

        @block.tensor
        def _(pe):
            def gemm(out_pair, w, rhs, k, kn):
                for a in range(2):
                    op = nc.tensor.matmul(out_pair[:, a, :], w, rhs[:, a * HALF:a * HALF + HALF], start=k == 0, stop=k == kn - 1)
                return op

            def gemm3(out, w, r, k, kn):
                for n, (x, y) in enumerate(((w[0], r[0]), (w[0], r[1]), (w[1], r[0]))):
                    op = nc.tensor.matmul(out, x, y, start=k == 0 and n == 0, stop=k == kn - 1 and n == 2)
                return op

            def landed(n):
                pe.wait_ge(w_land[n % R], 16 * (n // R + 1))
                return ring[:, n % R, :]

            def split_unit(n, kn):
                L = n >= RING0[1]
                u = n - RING0[L]
                pe.wait_ge(u_split, L * U_IN + u + 1)
                return [x[:, u % 2, :].rearrange("p (k c) -> p k c", k=kn) for x in (Uh, Ul)]

            def norm(k, buf):
                for c in range(KC):
                    pe.wait_ge(sq_ready, KC * k + c + 1)
                    gemm(pair(0), const["ones"], buf[:, c % 4, :], c, KC).then_inc(sq_used, 1)

            pe.wait_ge(c_in, 16 * 4)
            for L in range(DEPTH):
                if L:
                    pe.wait_ge(out_evac, pf_ffn(0) + EXPERTS[0] * KC)
                norm(2 * L, sq)
                ring_n = RING0[L]
                for half in range(2):
                    for u in range(4):
                        w = split_unit(ring_n, 2)
                        ring_n += 1
                        for kk in range(2):
                            k = 2 * u + kk
                            if half == 0:
                                pe.wait_ge(h_ready, 2 * L * KC + k + 1)
                            for tt in range(5):
                                n = half * 5 + tt
                                if k == 0 and n >= 8:
                                    pe.wait_ge(v_ready, 10 * L + n - 7)
                                t = tt * P if tt < TT else T - P
                                h = [x[:, k, t:t + P] for x in (Ph, Pl)]
                                for m, (x, y) in enumerate(((0, 0), (0, 1), (1, 0))):
                                    op = nc.tensor.matmul(ps[:, n % 8, :], h[x], w[y][:, kk, :],
                                                          start=k == 0 and m == 0, stop=k == KC - 1 and m == 2)
                                if k == KC - 1:
                                    op.then_inc(v_half, 1)
                        if u < 3:
                            op.then_inc(unit_done, 1)
                pe.wait_ge(rest_in, 16)
                for n, (kind, i) in enumerate(JOBS):
                    out = pair((n + 1) % 4)
                    if n < 4:
                        pe.wait_ge(v_ready, 10 * L + (4, 6, 8, 10)[n])
                    else:
                        m = n - 4
                        if JOBS[m][0] in ("bf", "bq", "g", "c", "s"):
                            pe.wait_ge(act_job, L * ACT_N[-1] + ACT_N[m])
                        else:
                            pe.wait_ge(dve_job, L * DVE_N[-1] + DVE_N[m])
                    if HAS_W[n]:
                        w = split_unit(ring_n, KC)
                        ring_n += 1
                        for k in range(KC):
                            for a in range(2):
                                t = slice(a * HALF, a * HALF + HALF)
                                op = gemm3(out[:, a, :], [x[:, k, :] for x in w], [x[:, k, t] for x in (Ph, Pl)], k, KC)
                    elif kind == "gu":
                        pe.wait_ge(dve_job, L * DVE_N[-1] + DVE_N[JOB_AT[("lr", 0)]])
                        op = gemm(out, WU[0:RANK, L * P:L * P + P], lr_sb, 0, 1)
                    elif kind == "s":
                        pe.wait_ge(act_job, L * ACT_N[-1] + ACT_N[JOB_AT[("c", i)]])
                        op = gemm(out, const["bones"], e1s[:, i % 2, :], 0, 1)
                    else:
                        pe.wait_ge(dve_job, L * DVE_N[-1] + DVE_N[JOB_AT[("s", i)]])
                        op = gemm(out, const["rot"], QK[:, i, :], 0, 1)
                    op.then_inc(pe_job, 1)

                pe.wait_ge(s0_in[0], 16 * (L + 1))
                pe.wait_ge(s0_in[1], 16 * (L + 1))
                for ct in range(CT):
                    nh = CT_HEADS[ct]
                    it0 = L * CT * NI + ct * NI
                    heads = [(h, chunk_rows(h, nh), ((0, 4, 6)[ct] + h) * DV) for h in range(nh)]
                    pe.wait_ge(term_ready, it0 + ITEM_AT[("kd", 0)] + 1)
                    if ct == 0:
                        pe.wait_ge(dve_job, (L + 1) * DVE_N[-1])
                    else:
                        pe.wait_ge(mixl_ready, 4 * L + (2, 3)[ct - 1])
                    for c in range(TT):
                        nc.tensor.transpose(ps[:, 0, c * P:c * P + P], kd[:, c * P:c * P + P], const["ident"])
                    nc.tensor.transpose(ps[0:NS, 1, 0:P], kd[:, SEQ:T], const["ident"]).then_inc(kdt_ps, 1)
                    for i in range(1, NBLK):
                        pe.wait_ge(term_ready, it0 + ITEM_AT[("kt", i)] + 1)
                        for c in range(TT):
                            w = nh * BLK
                            m = P if i * BLK > P // 2 else P // 2
                            op = nc.tensor.matmul(ps[0:m, 4 + c, i * w:i * w + w], Kt[:, i - 1, c, 0:m], Qbd[i - 1][:, c * w:c * w + w],
                                                  start=True, stop=True)
                    op.then_inc(off_done, 1)
                    pe.wait_ge(kdt_ready, CT * L + ct + 1)
                    for j in range(BLK):
                        pe.wait_ge(term_ready, it0 + ITEM_AT[("pj", j)] + 1)
                        o = 4 * (BLK - 1 - j)
                        nc.tensor.matmul(ps[0:64, 0, :], const["to_row"][:, o:o + 64], Pr[:, j % 2, 0:SEQ],
                                         start=j == 0, stop=j == BLK - 1).then_inc(prod_used, 1)
                    for j in range(DEC):
                        pe.wait_ge(term_ready, it0 + ITEM_AT[("sj", j)] + 1)
                        o = 4 * (BLK - 1 - j)
                        nc.tensor.matmul(ps[0:64, 1, 0:NS], const["to_row"][:, o:o + 64], Pr[:, j % 2, 0:NS],
                                         start=j == 0, stop=j == DEC - 1).then_inc(prod_used, 1)
                    for h in range(nh):
                        pe.wait_ge(e_ready, 8 * L + (0, 4, 6)[ct] + h + 1)
                        if h == 2:
                            pe.wait_ge(es_ready, CT * L + ct + 1)
                        nc.tensor.matmul(ps[:, (h + 2) % 4, :], const["of_row16"][0:64], A[0:64, h, 0:SEQ],
                                         start=True, stop=True).then_inc(at_done, 1)
                    pe.wait_ge(es_ready, CT * L + ct + 1)
                    pe.wait_ge(a_ready, 8 * L + (4, 6, 8)[ct])
                    for h in range(nh):
                        op = nc.tensor.matmul(ps[0:NS, 0, h * NS:h * NS + NS], const["of_row8"][0:64], A[0:64, h, SEQ:T], start=True, stop=True)
                    op.then_inc(ats_done, 1)
                    pe.wait_ge(as_ready, CT * L + ct + 1)
                    for c in range(TT):
                        for h, r, vo in heads:
                            op = nc.tensor.matmul(ps[r, 1, c * DV:c * DV + DV], KdT[:, c, r], V[:, c, vo:vo + DV],
                                                  start=True, stop=True)
                    op.then_inc(upd_done, 1)
                    for h, r, vo in heads:
                        pe.wait_ge(vbd_ready, 8 * L + vo // DV + 1)
                        nc.tensor.matmul(ps[r, 2, :], KdT[0:NS, TT, r], vbds[vo // DV % 2][0:NS, :], start=True, stop=True).then_inc(vbd_used, 1)
                    pe.wait_ge(s_ready, CT * L + ct + 1)
                    for k in range(nh // 2):
                        m = (0, 2, 3)[ct] + k
                        bp, bs = 3 + 2 * k, 4 + 2 * k
                        for hb in range(2):
                            h, r, vo = heads[2 * k + hb]
                            o = slice(hb * DV, hb * DV + DV)
                            for c in range(TT):
                                t = slice(c * P, c * P + P)
                                nc.tensor.matmul(ps[o, bp, t], V[:, c, vo:vo + DV], A[:, h, t], start=True, stop=c == 0)
                                if c:
                                    nc.tensor.matmul(ps[o, bp, t], S[r, ct, c - 1, :], Qe[r, ct, t], start=False, stop=True)
                            nc.tensor.matmul(ps[o, bs, 0:NS], V[:, TT, vo:vo + DV], A[:, h, SEQ:T],
                                             start=True, stop=False, skip_group_check=True)
                            for b in range(NB):
                                t = DEC * b
                                op = nc.tensor.matmul(ps[o, bs, t:t + DEC], S0[r, ct, b, :], Qe[r, ct, SEQ + t:SEQ + t + DEC],
                                                      start=False, stop=True, skip_group_check=True)
                        op.then_inc(o_done, 1)
                        pe.wait_ge(osq_ready, 4 * L + m + 1)
                        nc.tensor.matmul(ps[:, 7, :], const["bones"], osq[:, 0:SEQ], start=True, stop=True)
                        nc.tensor.matmul(ps[:, 0, 0:NS], const["bones"], osq[:, SEQ:T], start=True, stop=True).then_inc(oss_done, 1)

                pe.wait_ge(mixl_ready, 4 * (L + 1))
                pe.wait_ge(sn_ready, CT * (L + 1))
                n0 = 32 * L
                for n in range(32 + 3):
                    if n < 32:
                        h, qt_ = n // 4, n % 4
                        r = slice((h % 2) * DH, (h % 2) * DH + DH)
                        w = P * (qt_ + 1)
                        if n >= 2:
                            pe.wait_ge(sc_free, n0 + n - 1)
                        nc.tensor.matmul(ps[:, n % 2, 0:w], QK[r, h // 2, qt_ * P:qt_ * P + P], QK[r, 4 + h // 2, 0:w],
                                         start=True, stop=True).then_inc(sc_done, 1)
                    k = n - 2
                    if 0 <= k < 32:
                        pe.wait_ge(pn_ready, n0 + k + 1)
                        if k >= 2:
                            pe.wait_ge(pt_ready, n0 + k - 1)
                        for kb in range(k % 4 + 1):
                            op = nc.tensor.transpose(ps[:, 2 + k % 2, kb * P:kb * P + P], Pp[:, k % 4, kb * P:kb * P + P],
                                                     const["ident"])
                        op.then_inc(pt_ps, 1)
                    k = n - 3
                    if 0 <= k < 32:
                        h, qt_ = k // 4, k % 4
                        if k % 8 == 0 and k >= 16:
                            pe.wait_ge(mixc_ready, 4 * L + k // 8 - 1)
                        pe.wait_ge(pt_ready, n0 + k + 1)
                        o = slice((h % 2) * DH, (h % 2) * DH + DH)
                        for kb in range(qt_ + 1):
                            op = nc.tensor.matmul(ps[o, 4 + (h // 2) % 2, qt_ * P:qt_ * P + P], V[:, kb, 512 + h * DH:512 + h * DH + DH],
                                                  PTp[:, k % 2, kb * P:kb * P + P], start=kb == 0, stop=kb == qt_)
                        op.then_inc(pv_done, 1)
                pe.wait_ge(qs_ready, L + 1)
                pe.wait_ge(mixc_ready, 4 * (L + 1))
                for b in range(NB + 2):
                    q = (b - 1) % 2
                    if 1 <= b <= NB:
                        n = NB * L + b - 1
                        pe.wait_ge(sp_ready, n + 1)
                        if b >= 2:
                            pe.wait_ge(spt_ready, n)
                        for c in range(8):
                            nc.tensor.transpose(ps[:, 3 + c // 4, (c % 4) * P:(c % 4) * P + P], Ps[:, q, c:PAST:8], const["ident"])
                        nc.tensor.transpose(ps[0:NS, 5, 0:P], Ps[:, q, PAST:PAST + NS], const["ident"]).then_inc(spt_ps, 1)
                    if b >= 2:
                        pe.wait_ge(os_ready, NB * L + b - 1)
                        nc.tensor.transpose(ps[:, 6 + b % 2, 0:P], Os, const["ident"]).then_inc(os_turned, 1)
                    if b < NB:
                        n = NB * L + b
                        kc = [tiles(piece_landed(pe, L, b, part), 2) for part in range(2)]
                        if b:
                            pe.wait_ge(ssc_free, n)
                        for hp in range(4):
                            o = slice(32 * hp, 32 * hp + 32)
                            for a in range(2):
                                nc.tensor.matmul(ps[o, a, :], Qs[:, b, hp, :], kc[hp // 2][:, hp % 2, a * 512:a * 512 + 512], start=True, stop=True)
                            op = nc.tensor.matmul(ps[o, 2, 0:NS], Qs[:, b, hp, :], QK[:, 4 + hp, SEQ:T], start=True, stop=True)
                        op.then_inc(ssc_done, 1)
                    if 1 <= b <= NB:
                        n = NB * L + b - 1
                        pe.wait_ge(spt_ready, n + 1)
                        if b >= 3:
                            pe.wait_ge(smix_ready, n - 1)
                        pt, out = tiles(PTs[:, q, :], 9), ps[:, 6 + q, :]
                        for half in range(2):
                            vc = tiles(piece_landed(pe, L, b - 1, 2 + half), 4)
                            for c in range(4):
                                op = nc.tensor.matmul(out, pt[:, 4 * half + c, :], vc[:, c, :], start=(half, c) == (0, 0), stop=False)
                            if half:
                                op = nc.tensor.matmul(out, pt[0:NS, 8, :], V[0:NS, TT, 512:1024], start=False, stop=True)
                            op.then_inc((spv_half, spv_done)[half], 1)
                pe.wait_ge(smix_ready, NB * (L + 1))
                for m in range(U_OUT):
                    w = landed(ring_n)[:, 0:1024].rearrange("p (k c) -> p k c", k=KC)
                    ring_n += 1
                    if m >= 4:
                        pe.wait_ge(out_evac, PF0[L] + m - 3)
                    for k in range(KC):
                        op = gemm(pair(m % 4), w[:, k, :], mix[:, k, :], k, KC)
                    op.then_inc(unit_done, 1)
                pe.wait_ge(out_evac, PF0[L] + U_OUT)
                norm(2 * L + 1, sqf)
                if L:
                    continue
                pf = pf_ffn(L)
                with pe.Fori(0, EXPERTS[L]) as e:
                    for j in range(U_EXP):
                        pe.wait_ge(w_split, e * U_EXP + (j + 1))
                        if j < 4:
                            pe.wait_ge(out_evac, e * KC + pf)
                        elif j < 2 * FE + 4:
                            pe.wait_ge(prod_ready, e * FE + ((j - 4) // 2 + 1))
                        else:
                            pe.wait_ge(out_evac, e * KC + (pf + j - 2 * FE - 3))
                        kn, src, wd = (KC, (Hh, Hl), 1024) if j < 2 * FE else (FE, (hidh, hidl), SLOT)
                        w = [x[:, j % NSPLIT, 0:wd].rearrange("p (k c) -> p k c", k=kn) for x in (Wh, Wl)]
                        for k in range(kn):
                            if j == 0:
                                pe.wait_ge(h_ready, (2 * L + 1) * KC + k + 1)
                            if j == 2 * FE:
                                pe.wait_ge(hidlo_ready, e * FE + (k + 1))
                            for a in range(2):
                                t = slice(a * HALF, a * HALF + HALF)
                                op = gemm3(pair(j % 4)[:, a, :], [x[:, k, :] for x in w], [x[:, k, t] for x in src], k, kn)
                        op.then_inc(unit_done, 1)
            pe.wait_ge(router_in, 16)
            for k in range(KC):
                pe.wait_ge(h_ready, 3 * KC + k + 1)
                for tt in range(TT + 1):
                    rows = P if tt < TT else NS
                    op = nc.tensor.matmul(ps[0:rows, 2, tt * 8:tt * 8 + 8], H[:, k, tt * P:tt * P + rows],
                                          WRT[:, k * 8:k * 8 + 8], start=k == 0 and tt == 0, stop=k == KC - 1, skip_group_check=True)
            op.then_inc(rl_done, 1)
            for tt in range(TT + 1):
                rows = P if tt < TT else NS
                if tt >= 2:
                    pe.wait_ge(htok_ready, tt - 1)
                for k in range(KC):
                    op = nc.tensor.transpose(ps[0:rows, 4 + 2 * (tt % 2) + k // 4, (k % 4) * P:(k % 4) * P + P],
                                             H[:, k, tt * P:tt * P + rows], const["ident"])
                op.then_inc(htok_ps, 1)
            pe.wait_ge(chosen, 1)
            M = RW[:, 176:216]
            for tt in range(TT + 1):
                for t2 in range(tt):
                    nc.tensor.matmul(ps[:, 0, tt * 8:tt * 8 + 8], const["ones"], M[:, t2 * 8:t2 * 8 + 8], start=t2 == 0, stop=False)
                nc.tensor.matmul(ps[:, 0, tt * 8:tt * 8 + 8], const["before"], M[:, tt * 8:tt * 8 + 8], start=tt == 0, stop=True)
            for tt in range(TT + 1):
                op = nc.tensor.matmul(ps[:, 0, 40:48], const["ones"], M[:, tt * 8:tt * 8 + 8], start=tt == 0, stop=tt == TT)
            op.then_inc(ranked, 1)
            pe.wait_ge(coded, 1)
            pe.wait_ge(htok_ready, TT + 1)
            for r in range(4):
                if r == 3:
                    pe.wait_ge(rows_ready, 1)
                a = (r % 3) * 2
                for tt in range(TT + 1):
                    rows = P if tt < TT else NS
                    out = ps[:, 2 + a, tt * P:tt * P + P] if tt < TT else ps[:, 3 + a, 0:NS]
                    op = nc.tensor.matmul(out, RW[0:rows, 256 + 5 * r + tt:257 + 5 * r + tt].to_broadcast([rows, P]),
                                          const["ident"][0:rows, 0:rows], start=True, stop=True)
                op.then_inc(rows_ps, 1)
            pe.wait_ge(rows_ready, 4)

            def gather(count):
                pe.wait_ge(sel_ready, count)
                for k in range(KC):
                    out = ps[:, 5 + k // 3, (k % 3) * CAP:(k % 3) * CAP + CAP]
                    for tt in range(TT + 1):
                        rows = P if tt < TT else NS
                        op = nc.tensor.matmul(out, H_tok[0:rows, tt, k * P:k * P + P], Sel[0:rows, tt, :],
                                              start=tt == 0, stop=tt == TT)
                op.then_inc(gathered, 1)

            def transpose_out(count):
                pe.wait_ge(yt_ready, count)
                for k in range(KC):
                    nc.tensor.transpose(ps[:, 5 + k // 4, (k % 4) * P:(k % 4) * P + P], Yt[:, k, 0:P], const["ident"])
                for k in range(KC):
                    op = nc.tensor.transpose(ps[0:CAP2, k // 4, (k % 4) * P:(k % 4) * P + P], Yt[:, k, P:CAP], const["ident"])
                op.then_inc(ytok_ps, 1)

            def scatter(x, n):
                k, a = n // 2, n % 2
                if n >= 3:
                    pe.wait_ge(out_evac, x * (2 * KC) + (pfi + n - 2))
                out, t = ps[:, 5 + n % 3, 0:HALF], slice(a * HALF, a * HALF + HALF)
                for st, w in ((0, P), (1, CAP2)):
                    for part, y in enumerate((Yh, Yl)):
                        op = nc.tensor.matmul(out, y[0:w, st, k * P:k * P + P], SelT[0:w, st, t],
                                              start=(st, part) == (0, 0), stop=(st, part) == (1, 1))
                op.then_inc(scattered, 1)

            def item(i, before):
                pe.wait_ge(xg_ready, i + 1)
                for j, (kind, f) in enumerate(UNITS):
                    s = j % R
                    if kind == "down" and f == 0 and before is not None:
                        pe.wait_ge(ytok_ready, i)
                    if kind == "down" and before is not None and f < KC:
                        if f == 0:
                            pe.wait_ge(selw_ready, i)
                        for n in (2 * f, 2 * f + 1):
                            scatter(before, n)
                    if (kind, f) == ("down", KC):
                        if before is not None:
                            pe.wait_ge(out_evac, i * (2 * KC) + pfi)
                        gather(i + 2)
                    pe.wait_ge(w_land[s], i * (16 * SLOT_USES[s]) + 16 * (landings[s] + j // R + 1))
                    w = ring[:, s, 0:1024].rearrange("p (k c) -> p k c", k=KC)
                    if kind != "down":
                        if f >= 2:
                            pe.wait_ge(hid_ready, i * FE + (f - 1))
                        o = CAP * (kind == "up")
                        for k in range(KC):
                            op = nc.tensor.matmul(ps[:, 3 + f % 2, o:o + CAP], w[:, k, :], Xg[:, k, :], start=k == 0, stop=k == KC - 1)
                    else:
                        pe.wait_ge(hid_ready, i * FE + (f + 1))
                        for k in range(KC):
                            op = nc.tensor.matmul(ps[:, k // 3, (k % 3) * CAP:(k % 3) * CAP + CAP], w[:, k, :], hidg[:, f, :],
                                                  start=f == 0 and k % 3 == 0, stop=f == FE - 1, skip_group_check=True)
                    op.then_inc(unit_done, 1)
                    if (kind, f) == ("up", 0) and before is not None:
                        transpose_out(i)

            pfi = pf_ffn(1)
            gather(1)
            pe.wait_ge(items_ready, 1)
            last_item = pe.value_load(item_tab[0:1, MAX_ITEMS + 1:MAX_ITEMS + 2], min_val=N_EXP - 1, max_val=MAX_ITEMS - 1)
            item(0, None)
            with pe.Fori(0, last_item) as before:
                item(before + 1, before)
            transpose_out(last_item + 1)
            pe.wait_ge(ytok_ready, last_item + 1)
            pe.wait_ge(selw_ready, last_item + 1)
            for n in range(2 * KC):
                scatter(last_item, n)

        @block.vector
        def _(dve):
            v = nc.vector
            n_chain = [0]

            def link(op):
                op.then_inc(dch, 1)
                n_chain[0] += 1
                dve.wait_ge(dch, n_chain[0])

            v.memset(eps_col, EPS).then_inc(eps_ready, 1)
            dve.wait_ge(c_in, 16 * 4)
            l0, l1 = LB[:, 16:18], LB[:, 18:20]
            link(v.tensor_tensor(LB[:, 28:30], l0, l1, ALU.max))
            link(v.tensor_tensor(LB[:, 24:26], l0, LB[:, 28:30], ALU.subtract))
            v.tensor_tensor(LB[:, 26:28], l1, LB[:, 28:30], ALU.subtract).then_inc(lb_ready, 1)
            dve.wait_ge(lb_exp, 1)
            w0, w1 = LB[:, 20:22], LB[:, 22:24]
            link(v.tensor_tensor(LB[:, 28:30], w0, w1, ALU.add))
            link(v.reciprocal(LB[:, 30:32], LB[:, 28:30]))
            link(v.tensor_tensor(w0, w0, LB[:, 30:32], ALU.mult))
            link(v.tensor_tensor(w1, w1, LB[:, 30:32], ALU.mult))
            link(v.tensor_tensor(LB[:, 0:2], w0, w0, ALU.subtract))
            link(v.tensor_tensor(LB[:, 28:30], w0, w1, ALU.add))
            link(v.tensor_tensor(LB[:, 2:4], LB[:, 28:30], w0, ALU.subtract))
            link(v.tensor_scalar(oml, lb, -1.0, 1.0, ALU.mult, ALU.add))

            def normed(k, r, gains):
                dve.wait_ge(rinv_ready, k + 1)
                for c in range(KC):
                    v.scalar_tensor_tensor(H[:, c, :], X[:, c, :], gains[:, c:c + 1], r, ALU.mult, ALU.mult).then_inc(h_ready, 1)

            def job(op):
                op.then_inc(dve_job, 1)

            for L in range(DEPTH):
                def lo(u, L=L):
                    dve.wait_ge(uhi_ready, L * U_IN + u + 1)
                    v.tensor_tensor(Ul[:, u % 2, :], ring[:, (RING0[L] + u) % R, 0:1024], Uh[:, u % 2, :], ALU.subtract).then_inc(u_split, 1)

                dve.wait_ge(rinv_ready, 2 * L + 1)
                for c in range(KC):
                    if c >= 4:
                        dve.wait_ge(h_ready, 2 * L * KC + c - 3)
                    v.scalar_tensor_tensor(sq[:, c % 4, :], X[:, c, :], vec(L, "g_mix")[:, c:c + 1], rinv,
                                           ALU.mult, ALU.mult).then_inc(pf_ready, 1)
                    if c in (1, 3):
                        lo(c // 2)
                v.memset(V[NS:P, TT, :], 0.0)
                for u in range(2, NV + 1):
                    lo(u)
                dve.wait_ge(rest_in, 16)
                for n, (kind, i) in enumerate(JOBS):
                    if HAS_W[n] and NV + sum(HAS_W[:n]) + 1 < U_IN:
                        lo(NV + sum(HAS_W[:n]) + 1)
                    if (kind, i) == ("g", 1):
                        dve.wait_ge(lf_ready, 2 * L + 1)
                        link(v.scalar_tensor_tensor(rtmp, B[:, 0, :], 0.0, rtmp, ALU.min, ALU.subtract))
                        link(v.tensor_scalar(rtmp, rtmp, 1.0 / 16.0, None, ALU.mult))
                        link(v.tensor_tensor_scan(B[:, 0, :], const["reset"], rtmp, 0.0, ALU.mult, ALU.add))
                        dve.wait_ge(lf_ready, 2 * L + 2)
                        for ct in (1, 2):
                            link(v.tensor_tensor_scan(B[:, ct, :], const["reset"], B[:, ct, :], 0.0, ALU.mult, ALU.add))
                    if not HAS_DVE[n]:
                        continue
                    src = pair((n + 1) % 4)
                    s = n % 2
                    if kind in ("bf", "bq", "g", "s"):
                        dve.wait_ge(act_job, L * ACT_N[-1] + ACT_N[n])
                    else:
                        dve.wait_ge(pe_job, L * NJ + n + 1)
                    if kind == "lr":
                        job(v.tensor_copy(split(lr_sb), src[0:RANK]))
                    elif kind == "bf":
                        f, kk = e0[:, s, :], e1s[:, s, :]
                        v.tensor_scalar(B[:, 1 + i, :], f, oml[:, 2 * L + i:2 * L + i + 1], lb[:, 2 * L + i:2 * L + i + 1], ALU.mult, ALU.add)
                        job(v.tensor_scalar(K[:, 1 + i, :], kk, oml[:, 2 * L + i:2 * L + i + 1], None, ALU.mult))
                    elif kind == "aq":
                        job(v.tensor_scalar(split(Q[:, 0, :]), src, float(DK_A) ** -0.5, None, ALU.mult))
                    elif kind == "gu":
                        job(v.tensor_scalar(split(B[:, 0, :]), src, vec(L, "b_gate"), None, ALU.add))
                        dve.wait_ge(dve_job, L * DVE_N[-1] + DVE_N[n])
                        link(v.tensor_scalar(rtmp, B[:, 0, :], -1.0, None, ALU.mult))
                        v.tensor_tensor(rtmp, B[:, 0, :], rtmp, ALU.max).then_inc(lf_abs, 1)
                    elif kind == "ak":
                        job(v.tensor_copy(split(K[:, 0, :]), src))
                    elif kind == "s":
                        gain = vec(L, "g_q" if i < 4 else "g_k")
                        job(v.scalar_tensor_tensor(QK[:, i, :], e0[:, i % 2, :], gain, rinvs[:, i % 2, :], ALU.mult, ALU.mult))
                    else:
                        dst = QK[:, i, :]
                        if i:
                            dve.wait_ge(dve_job, L * DVE_N[-1] + DVE_N[n - 1])
                        v.tensor_tensor(split(rtmp), src, split(const["sin"]), ALU.mult)
                        link(v.tensor_tensor(dst, dst, const["cos"], ALU.mult))
                        job(v.tensor_tensor(dst, dst, rtmp, ALU.add))
                dve.wait_ge(dve_job, (L + 1) * DVE_N[-1])
                v.memset(A[NS:P, :, SEQ:T], 0.0)
                def terms(ct, items, L=L):
                    nh = CT_HEADS[ct]
                    it0 = L * CT * NI + ct * NI
                    np_ = L * CT * (BLK + DEC) + ct * (BLK + DEC)
                    Qp = Q[:, ct, 0:SEQ].rearrange("p (n s) -> p n s", s=BLK)
                    Kp = K[:, ct, 0:SEQ].rearrange("p (n s) -> p n s", s=BLK)
                    Qd = Q[:, ct, SEQ:T].rearrange("p (n s) -> p n s", s=DEC)
                    Kd_ = K[:, ct, SEQ:T].rearrange("p (n s) -> p n s", s=DEC)
                    for kind, i in items:
                        it = it0 + ITEM_AT[(kind, i)]
                        D = Dr[:, it % 3, :]
                        Dp = D[:, 0:SEQ].rearrange("p (c s) -> p c s", c=TT)
                        dve.wait_ge(exp_ready, it + 1)
                        if kind == "eb":
                            v.tensor_copy(ebl[:, ct, 0:TT], D[:, P - 1:SEQ:P])
                            v.tensor_copy(ebl[:, ct, TT:12], D[:, SEQ + DEC - 1:T:DEC])
                            op = v.tensor_tensor(Qe[:, ct, :], Q[:, ct, :], D, ALU.mult)
                        elif kind == "kd":
                            if ct:
                                dve.wait_ge(vbd_used, 8 * L + (0, 4, 6)[ct])
                            op = v.tensor_tensor(kd, K[:, ct, :], D, ALU.mult)
                        elif kind == "qt":
                            if ct:
                                dve.wait_ge(off_done, CT * L + ct)
                            link(v.tensor_tensor(Dp[:, :, BLK:P], Q[:, ct, 0:SEQ].rearrange("p (c s) -> p c s", c=TT)[:, :, BLK:P],
                                                 Dp[:, :, BLK:P], ALU.mult))
                            heads = const[f"heads{nh}"]
                            for b in range(1, NBLK):
                                op = v.tensor_tensor(
                                    Qbd[b - 1][:, 0:TT * nh * BLK].rearrange("p (c h t) -> p c h t", c=TT, h=nh),
                                    Dp[:, :, b * BLK:b * BLK + BLK].rearrange("p c (o t) -> p c o t", o=1).to_broadcast([P, TT, nh, BLK]),
                                    heads.rearrange("p (o h u) -> p o h u", o=1, u=1).to_broadcast([P, TT, nh, BLK]), ALU.mult)
                        elif kind == "kt":
                            w = BLK * i
                            if ct == 0:
                                dve.wait_ge(kt_zero, L * (NBLK - 1) + i)
                            op = v.tensor_tensor(Kt[:, i - 1, :, 0:w], K[:, ct, 0:SEQ].rearrange("p (c s) -> p c s", c=TT)[:, :, 0:w],
                                                 Dp[:, :, 0:w], ALU.mult)
                        else:
                            blk, nblk, q_, k_ = (BLK, SEQ // BLK, Qp, Kp) if kind == "pj" else (DEC, NB, Qd, Kd_)
                            w = blk - i
                            m = i if kind == "pj" else BLK + i
                            if m >= 2:
                                dve.wait_ge(prod_used, np_ + m - 1)
                            prod = Pr[:, m % 2, 0:nblk * blk].rearrange("p (n s) -> p n s", s=blk)[:, :, i:blk]
                            if (kind, i) == ("pj", 1):
                                v.memset(Pr[:, 1, 0:SEQ].rearrange("p (n s) -> p n s", s=BLK)[:, :, 0:1], 0.0)
                            dd = D[:, 0:nblk * w].rearrange("p (n s) -> p n s", s=w)
                            link(v.tensor_tensor(prod, dd, k_[:, :, i:i + 1].to_broadcast([P, nblk, w]), ALU.mult))
                            op = v.tensor_tensor(prod, prod, q_[:, :, i:blk], ALU.mult)
                        op.then_inc(term_ready, 1)

                terms(0, FIRST)
                for ct in range(CT):
                    nh = CT_HEADS[ct]
                    np_ = L * CT * (BLK + DEC) + ct * (BLK + DEC)
                    terms(ct, REST)
                    dve.wait_ge(prod_used, np_ + BLK + DEC)
                    own = const[f"rows{nh}"][0:64]
                    for h in range(nh):
                        v.tensor_scalar(A[0:64, h, 0:SEQ], ps[0:64, 0, :], own[:, h:h + 1], None, ALU.mult).then_inc(e_ready, 1)
                    for h in range(nh):
                        op = v.tensor_scalar(A[0:64, h, SEQ:T], ps[0:64, 1, 0:NS], own[:, h:h + 1], None, ALU.mult)
                    op.then_inc(es_ready, 1)
                    dve.wait_ge(off_done, CT * L + ct + 1)
                    n_at = 8 * L + (0, 4, 6)[ct]
                    for h in range(nh):
                        a3 = A[:, h, 0:SEQ].rearrange("p (c s) -> p c s", c=TT)
                        dve.wait_ge(at_done, n_at + h + 1)
                        link(v.tensor_tensor(a3, ps[:, (h + 2) % 4, :].rearrange("p (c s) -> p c s", c=TT),
                                             const["mask16"].rearrange("p (o s) -> p o s", o=1).to_broadcast([P, TT, P]), ALU.mult))
                        for r, i0 in ((slice(0, P // 2), 1), (slice(P // 2, P), NBLK // 2 + 1)):
                            off = ps[r, 4:8, 0:NBLK * nh * BLK].rearrange("p c (i h t) -> p c i h t", i=NBLK, h=nh)[:, :, i0:NBLK, h, :]
                            a4 = a3[r, :, i0 * BLK:P].rearrange("p c (i t) -> p c i t", t=BLK)
                            op = v.tensor_tensor(a4, a4, off, ALU.add)
                        op.then_inc(a_ready, 1)
                    dve.wait_ge(ats_done, CT * L + ct + 1)
                    v.tensor_tensor(A[0:NS, 0:nh, SEQ:T], ps[0:NS, 0, 0:nh * NS].rearrange("p (h s) -> p h s", h=nh),
                                    const["mask8"][0:NS, :].rearrange("p (o s) -> p o s", o=1).to_broadcast([NS, nh, NS]),
                                    ALU.mult).then_inc(as_ready, 1)
                    dve.wait_ge(upd_done, CT * L + ct + 1)
                    link(v.tensor_copy(S[:, ct, 0, :], ps[:, 1, 0:DV]))
                    for c in range(1, TT):
                        op = v.scalar_tensor_tensor(S[:, ct, c, :], S[:, ct, c - 1, :], ebl[:, ct, c:c + 1],
                                                    ps[:, 1, c * DV:c * DV + DV], ALU.mult, ALU.add)
                        if c < TT - 1:
                            link(op)
                    op.then_inc(s_ready, 1)
                    if ct + 1 < CT:
                        terms(ct + 1, FIRST)
                    for k in range(nh // 2):
                        m = (0, 2, 3)[ct] + k
                        bp, bs = 3 + 2 * k, 4 + 2 * k
                        dve.wait_ge(orinv_ready, 4 * L + m + 1)
                        gain = vec(L, "g_gla" if ct == 0 else "g_hgrn")
                        v.scalar_tensor_tensor(mix[:, m, 0:SEQ], ps[:, bp, :], gain, orinv[:, 0:SEQ], ALU.mult, ALU.mult)
                        link(v.scalar_tensor_tensor(mix[:, m, SEQ:T], ps[:, bs, 0:NS], gain, orinv[:, SEQ:T], ALU.mult, ALU.mult))
                        v.tensor_tensor(mix[:, m, :], mix[:, m, :], G[:, m, :], ALU.mult).then_inc(mixl_ready, 1)
                    dve.wait_ge(vbd_used, 8 * L + (4, 6, 8)[ct])
                    s0 = S0[:, ct, :, :]
                    link(v.tensor_tensor(s0, s0, ebl[:, ct, TT:12].rearrange("p (b o) -> p b o", o=1).to_broadcast([P, NB, DV]), ALU.mult))
                    v.tensor_tensor(s0, s0, ps[:, 2, :].rearrange("p (b v) -> p b v", b=NB), ALU.add).then_inc(sn_ready, 1)
                dve.wait_ge(mixl_ready, 4 * (L + 1))
                link(v.memset(LIN[:, 6144:7168], 0.0))
                for hb in range(2):
                    r = slice(hb * DH, hb * DH + DH)
                    for hp in range(4):
                        op = v.tensor_copy(Qs[r, :, hp, hb * DEC:hb * DEC + DEC], QK[r, hp, SEQ:T].rearrange("p (b t) -> p b t", b=NB))
                op.then_inc(qs_ready, 1)
                n0 = 32 * L
                for n in range(32 + 1):
                    if n < 32:
                        w = P * (n % 4 + 1)
                        pn, s = Pp[:, n % 4, 0:w], n % 4
                        dve.wait_ge(sc_done, n0 + n + 1)
                        if n >= 4:
                            dve.wait_ge(pt_ps, n0 + n - 3)
                        v.scalar_tensor_tensor(pn, ps[:, n % 2, 0:w], DH ** -0.5, const["lnc"][:, SEQ - w:SEQ],
                                               ALU.mult, ALU.add).then_inc(sc_free, 1)
                        dve.wait_ge(sc_free, n0 + n + 1)
                        v.tensor_reduce(negmax[:, s:s + 1], pn, AX.X, ALU.max, negate=True).then_inc(mx_ready, 1)
                    k = n - 1
                    if k >= 0:
                        w = P * (k % 4 + 1)
                        pk, s = Pp[:, k % 4, 0:w], k % 4
                        dve.wait_ge(p_ready, n0 + k + 1)
                        link(v.reciprocal(rden[:, s:s + 1], den[:, s:s + 1]))
                        v.tensor_scalar(pk, pk, rden[:, s:s + 1], None, ALU.mult).then_inc(pn_ready, 1)
                for b in range(NB + 2):
                    if b >= 2:
                        dve.wait_ge(spv_done, NB * L + b - 1)
                        if b >= 3:
                            dve.wait_ge(os_turned, NB * L + b - 2)
                        for hp in range(4):
                            r = slice(32 * hp, 32 * hp + 32)
                            op = v.tensor_scalar(Os[r], ps[r, 6 + b % 2, hp * P:hp * P + P], rden[r, 4 + b % 2:5 + b % 2], None, ALU.mult)
                        op.then_inc(os_ready, 1)
                        dve.wait_ge(os_ready, NB * L + b - 1)
                    if b < NB:
                        n = NB * L + b
                        pn, s = Ps[:, b % 2, :], 4 + b % 2
                        dve.wait_ge(ssc_done, n + 1)
                        if b >= 2:
                            dve.wait_ge(spt_ps, n - 1)
                        v.scalar_tensor_tensor(pn[:, 0:PAST], ps[:, 0:2, :].rearrange("p a t -> p (a t)"), DH ** -0.5,
                                               const["smask"], ALU.mult, ALU.add)
                        v.scalar_tensor_tensor(pn[:, PAST:PAST + NS], ps[:, 2, 0:NS], DH ** -0.5,
                                               const["smask_new"][:, b * NS:b * NS + NS], ALU.mult, ALU.add).then_inc(ssc_free, 1)
                        dve.wait_ge(ssc_free, n + 1)
                        v.tensor_reduce(negmax[:, s:s + 1], pn, AX.X, ALU.max, negate=True).then_inc(smx_ready, 1)
                    if b >= 2:
                        dve.wait_ge(os_turned, NB * L + b - 1)
                        o = ps[:, 6 + b % 2, 0:P].rearrange("p (h q) -> p h q", h=4)
                        t = SEQ + DEC * (b - 2)
                        v.tensor_copy(mix[0:DH, 4:8, t:t + DEC], o[0:DH, :, 0:DEC])
                        v.tensor_copy(mix[DH:P, 4:8, t:t + DEC], o[DH:P, :, DEC:2 * DEC]).then_inc(smix_ready, 1)
                    if b < NB:
                        dve.wait_ge(sp_ready, n + 1)
                        link(v.reciprocal(rden[:, s:s + 1], den[:, s:s + 1]))
                for m in range(U_OUT):
                    dve.wait_ge(unit_done, UD0[L] + NVU + m + 1)
                    v.tensor_tensor(split(X[:, m, :]), split(X[:, m, :]), pair(m % 4), ALU.add).then_inc(out_evac, 1)
                if L:
                    normed(2 * L + 1, rinv_f, vec(L, "g_ffn"))
                    continue
                dve.wait_ge(stored_kv, 16 * (2 + 2 * NB))
                dve.wait_ge(rinv_ready, 2 * L + 2)
                for c in range(KC):
                    if c >= 4:
                        dve.wait_ge(h_ready, (2 * L + 1) * KC + c - 3)
                    v.scalar_tensor_tensor(ft[:, c % 4, :], X[:, c, :], vec(L, "g_ffn")[:, c:c + 1], rinv_f,
                                           ALU.mult, ALU.mult).then_inc(hf_ready, 1)

                def lo(e, j):
                    n, w = RING0[0] + U_IN + U_OUT + j, 1024 if j < 2 * FE else SLOT
                    dve.wait_ge(whi_ready, e * U_EXP + (j + 1))
                    v.tensor_tensor(Wl[:, j % NSPLIT, 0:w], ring[:, n % R, 0:w], Wh[:, j % NSPLIT, 0:w], ALU.subtract).then_inc(w_split, 1)

                with dve.Fori(0, EXPERTS[L]) as e:
                    for j in range(AHEAD):
                        lo(e, j)
                    for j in range(U_EXP):
                        if j + AHEAD < U_EXP:
                            lo(e, j + AHEAD)
                        i, m = j // 2, j - 2 * FE
                        if m >= 0:
                            dve.wait_ge(unit_done, e * U_EXP + (ud_ffn(L) + j + 1))
                            v.tensor_tensor(split(X[:, m, :]), split(X[:, m, :]), pair(j % 4), ALU.add).then_inc(out_evac, 1)
                        elif j % 2:
                            f = ft[:, 2 + i % 2, :]
                            dve.wait_ge(sig_ready, e * FE + (i + 1))
                            dve.wait_ge(unit_done, e * U_EXP + (ud_ffn(L) + j + 1))
                            v.tensor_tensor(split(f), pair(j % 4), split(ft[:, i % 2, :]), ALU.mult).then_inc(prod_ready, 1)
                            dve.wait_ge(hidhi_ready, e * FE + (i + 1))
                            v.tensor_tensor(hidl[:, i, :], f, hidh[:, i, :], ALU.subtract).then_inc(hidlo_ready, 1)

            def t3(o):
                return RW[:, o:o + 40].rearrange("p (t e) -> p t e", e=8)

            def t1(o):
                return RW[:, o:o + 5]

            def over_e(o):
                return t1(o).rearrange("p (t o) -> p t o", o=1).to_broadcast([P, 5, 8])

            def over_t(ap):
                return ap.rearrange("p (o e) -> p o e", o=1).to_broadcast([P, 5, 8])

            lg, eq, first, second, both, code = t3(0), t3(40), t3(95), t3(135), t3(176), t3(216)
            code1, code2, w1_, w2_ = (t1(256 + 5 * r) for r in range(4))
            m1, m2, dif = t1(85), t1(90), t1(80)
            link(v.memset(RW[:, 0:40], 0.0))
            dve.wait_ge(rl_done, 1)
            v.tensor_copy(RW[:, 0:32], ps[:, 2, 0:32])
            link(v.tensor_copy(RW[0:NS, 32:40], ps[0:NS, 2, 32:40]))
            for o_m, pick in ((85, first), (90, second)):
                link(v.tensor_reduce(t1(o_m), lg, AX.X, ALU.max))
                link(v.tensor_tensor(eq, lg, over_e(o_m), ALU.is_equal))
                link(v.tensor_tensor(eq, eq, over_t(const["riota"]), ALU.mult))
                link(v.tensor_reduce(dif, eq, AX.X, ALU.max))
                link(v.tensor_tensor(pick, eq, over_e(80), ALU.is_equal))
                if pick is first:
                    link(v.scalar_tensor_tensor(lg, pick, -3e38, lg, ALU.mult, ALU.add))
            v.tensor_tensor(dif, m2, m1, ALU.subtract).then_inc(rexp, 1)
            link(v.tensor_tensor(both, first, second, ALU.add))
            v.memset(RW[NS:P, 176 + 32:176 + 40], 0.0).then_inc(chosen, 1)
            dve.wait_ge(rexp_done, 1)
            link(v.tensor_scalar(w2_, dif, 1.0, None, ALU.add))
            link(v.reciprocal(w1_, w2_))
            link(v.tensor_tensor(w2_, dif, w1_, ALU.mult))
            dve.wait_ge(ranked, 1)
            cnt, npass, upto, start = (RW[:, 280 + 8 * r:288 + 8 * r] for r in range(4))
            link(v.tensor_copy(cnt, ps[:, 0, 40:48]))
            link(v.memset(npass, 1.0))
            for m in range(1, PER_EXP):
                link(v.scalar_tensor_tensor(npass, cnt, float(m * CAP), npass, ALU.is_gt, ALU.add))
            link(v.tensor_tensor_scan(upto, const["ones"][:, 0:8], npass, 0.0, ALU.mult, ALU.add))
            link(v.tensor_tensor(start, upto, npass, ALU.subtract))
            link(v.tensor_scalar(start, start, float(CAP), None, ALU.mult))
            link(v.tensor_tensor(code, ps[:, 0, 0:40].rearrange("p (t e) -> p t e", e=8), over_t(start), ALU.add))
            link(v.tensor_tensor(first, first, code, ALU.mult))
            link(v.tensor_reduce(code1, first, AX.X, ALU.add))
            link(v.tensor_tensor(second, second, code, ALU.mult))
            v.tensor_reduce(code2, second, AX.X, ALU.add).then_inc(coded, 1)
            tab = RW[0:1, 320:320 + MAX_ITEMS * 8].rearrange("p (i e) -> p i e", e=8)
            link(v.tensor_tensor(tab, upto[0:1].rearrange("p (o e) -> p o e", o=1).to_broadcast([1, MAX_ITEMS, 8]),
                                 const["slots"][0:1, 0:MAX_ITEMS].rearrange("p (i o) -> p i o", o=1).to_broadcast([1, MAX_ITEMS, 8]), ALU.is_le))
            of_item = RW[0:1, 320 + MAX_ITEMS * 8:320 + MAX_ITEMS * 9]
            link(v.tensor_reduce(of_item, tab, AX.X, ALU.add))
            link(v.tensor_scalar(of_item, of_item, float(N_EXP - 1), None, ALU.min))
            v.tensor_copy(item_tab[0:1, 0:MAX_ITEMS], of_item)
            v.tensor_copy(item_tab[0:1, MAX_ITEMS:MAX_ITEMS + 1], upto[0:1, 7:8])
            v.tensor_scalar(item_tab[0:1, MAX_ITEMS + 1:MAX_ITEMS + 2], upto[0:1, 7:8], -1.0, None, ALU.add).then_inc(items_ready, 1)
            dve.wait_ge(coded, 1)

            rows_col = LB[:, 8:10]
            link(v.tensor_copy(rows_col, const["rows"]))

            def sel_steps(chained):
                out = []
                for tt in range(TT + 1):
                    out.append(lambda tt=tt: chained(v.tensor_scalar(Sel[:, tt, :], const["slots"], code1[:, tt:tt + 1], None, ALU.is_equal)))
                    out.append(lambda tt=tt: v.scalar_tensor_tensor(Sel[:, tt, :], const["slots"], code2[:, tt:tt + 1], Sel[:, tt, :],
                                                                    ALU.is_equal, ALU.add))
                return out

            for r in range(4):
                dve.wait_ge(rows_ps, r + 1)
                a = (r % 3) * 2
                v.tensor_copy(rows4[:, r, 0:SEQ], ps[:, 2 + a, :])
                v.tensor_copy(rows4[:, r, SEQ:T], ps[:, 3 + a, 0:NS]).then_inc(rows_ready, 1)
            dve.wait_ge(rows_ready, 4)
            for s in sel_steps(link):
                op = s()
            op.then_inc(sel_ready, 1)
            dve.wait_ge(items_ready, 1)
            last_item = dve.value_load(item_tab[0:1, MAX_ITEMS + 1:MAX_ITEMS + 2], min_val=N_EXP - 1, max_val=MAX_ITEMS - 1)
            c0, pfi = n_chain[0], pf_ffn(1)
            PER_ITEM = 6 + 2 + (TT + 1)

            def add_out(x, n):
                k, a = n // 2, n % 2
                res = X[:, k, a * HALF:a * HALF + HALF]
                dve.wait_ge(scattered, x * (2 * KC) + (n + 1))
                v.tensor_tensor(res, res, ps[:, 5 + n % 3, 0:HALF], ALU.add).then_inc(out_evac, 1)

            def rest_of_tok(x):
                for st, w, bank in ((0, P, 5), (1, CAP2, 0)):
                    dve.wait_ge(yhi_ready, 2 * x + (st + 1))
                    op = v.scalar_tensor_tensor(Yl[0:w, st, :].rearrange("p (a c) -> p a c", a=2), ps[0:w, bank:bank + 2, :],
                                                slot_w[0:w, st:st + 1], Yh[0:w, st, :].rearrange("p (a c) -> p a c", a=2),
                                                ALU.mult, ALU.subtract)
                op.then_inc(ytok_ready, 1)

            def item(i, before):
                k_chain = [0]

                def chained(op):
                    op.then_inc(dch, 1)
                    k_chain[0] += 1
                    dve.wait_ge(dch, i * PER_ITEM + (c0 + k_chain[0]))

                def weighted(st):
                    w = P if st == 0 else CAP2
                    a, b = SelW[0:w, st, :], selt[0:w, :]
                    col = rows_col[0:w, st:st + 1]
                    chained(v.scalar_tensor_tensor(a, rows4[0:w, 0, :], col, rows4[0:w, 2, :], ALU.is_equal, ALU.mult))
                    chained(v.scalar_tensor_tensor(b, rows4[0:w, 1, :], col, rows4[0:w, 3, :], ALU.is_equal, ALU.mult))
                    chained(v.tensor_tensor(a, a, b, ALU.add))
                    if before is not None:
                        dve.wait_ge(ytok_ready, i)
                    v.tensor_reduce(slot_w[0:w, st:st + 1], a, AX.X, ALU.add).then_inc(slotw_ready, 1)
                    op = v.tensor_scalar(SelT[0:w, st, :], a, 0.0, None, ALU.is_gt)
                    if st:
                        op.then_inc(selw_ready, 1)
                        dve.wait_ge(selw_ready, i + 1)

                def hidden(f):
                    dve.wait_ge(silu_ready, i * FE + (f + 1))
                    v.tensor_tensor(hidg[:, f, :], tg[:, f % 2, :], ps[:, 3 + f % 2, CAP:2 * CAP], ALU.mult).then_inc(hid_ready, 1)

                sels = sel_steps(chained)
                for f in range(FE):
                    hidden(f)
                    if f == 0 and before is not None:
                        rest_of_tok(before)
                    if f == 0:
                        dve.wait_ge(gathered, i + 1)
                        chained(v.tensor_scalar(RW[:, 256:266], RW[:, 256:266], float(-CAP), None, ALU.add))
                    if 1 <= f <= KC and before is not None:
                        for n in (2 * f - 2, 2 * f - 1):
                            add_out(before, n)
                    if 2 <= f < 2 + TT + 1:
                        op = [s() for s in sels[2 * f - 4:2 * f - 2]][-1]
                        if f == TT + 2:
                            op.then_inc(sel_ready, 1)
                    if f >= FE - 2:
                        weighted(f - (FE - 2))
                chained(v.tensor_scalar(rows_col, rows_col, float(CAP), None, ALU.add))

            item(0, None)
            with dve.Fori(0, last_item) as before:
                item(before + 1, before)
            rest_of_tok(last_item)
            for n in range(2 * KC):
                add_out(last_item, n)
            v.tensor_copy(rows_col, const["rows"]).then_inc(experts_done, 1)



def lay_inputs(i):
    f = np.ascontiguousarray

    def unit(w):
        k, n = w.shape
        return f(w.reshape(k // P, P, n // P, P).transpose(2, 1, 0, 3).reshape(n // P, P, k))

    out = {"consts": shape_constants()}
    x = np.concatenate([i["x_prompt"].reshape(SEQ, D_MODEL), i["x_sample"].reshape(NS, D_MODEL)], 0)
    out["x"] = f(x.T.reshape(KC, P, T).transpose(1, 0, 2))
    w_in = i["w_in"]
    widths = [128, 128, 256, 16, 256, 256, 256, 256, 256, 512, 512, 512]
    cuts = np.cumsum(widths)[:-1].tolist()
    parts = [np.split(w_in[L], cuts, axis=1) for L in range(DEPTH)]
    feat, val = [], []
    for L in range(DEPTH):
        a_q, a_k, a_v, a_lr, a_g, b_q, b_f, b_i, b_g, c_q, c_k, c_v = parts[L]
        wide_lr = np.concatenate([a_lr, np.zeros((D_MODEL, P - RANK), a_lr.dtype)], 1)
        by_kind = {"lr": wide_lr, "bf": b_f, "aq": a_q, "ak": a_k, "bq": b_q, "g": np.concatenate([a_g, b_g], 1),
                   "c": np.concatenate([c_q, c_k], 1)}
        feat.append(unit(np.concatenate([by_kind[kind][:, j * P:j * P + P] for (kind, j), w in zip(JOBS, HAS_W) if w], 1)))
        v = np.concatenate([a_v, b_i, c_v], 1)
        val.append(v.reshape(4, 2, P, 2, 512).transpose(3, 0, 2, 1, 4).reshape(NV, P, 1024))
    out["w_feat"], out["w_v"] = (f(np.stack(a)) for a in (feat, val))
    out["w_out"] = np.stack([unit(i["w_out"][L]) for L in range(DEPTH)])
    half = FE * P
    gates, ups, downs = [], [], []
    for h in range(2):
        gates.append(i["ffn_w_gate"][0][:, h * half:(h + 1) * half])
        ups.append(i["ffn_w_up"][0][:, h * half:(h + 1) * half])
        downs.append(i["ffn_w_down"][0][h * half:(h + 1) * half])
    gates += list(i["moe_w_gate"][0])
    ups += list(i["moe_w_up"][0])
    out["w_gu"] = np.concatenate([np.stack([unit(g), unit(u)], 1).reshape(2 * FE, P, D_MODEL) for g, u in zip(gates, ups)], 0)
    out["w_dn"] = np.concatenate([unit(w) for w in downs], 0)
    out["w_dn_moe"] = f(i["moe_w_down"][0].reshape(N_EXP * FE, P, D_MODEL))
    out["w_router"] = f(i["moe_w_router"][0].reshape(KC, P, 8).transpose(1, 0, 2).reshape(P, 64))
    out["w_up"] = f(i["gla_w_gate_up"].transpose(1, 0, 2).reshape(RANK, DEPTH * P))
    out["lb_logits"] = f(i["hgrn_lb_logits"].reshape(DEPTH, 2, P).transpose(2, 0, 1).reshape(P, 4))
    cols = []
    for L in range(DEPTH):
        cols += [i["norm_mix_g"][L].reshape(KC, P).T, i["norm_ffn_g"][L].reshape(KC, P).T, i["gla_b_gate"][L].reshape(P, 1)]
        cols += [np.tile(i[n][L], 2).reshape(P, 1) for n in ("gla_norm_g", "hgrn_norm_g", "attn_q_norm_g", "attn_k_norm_g")]
    out["vecs"] = f(np.concatenate(cols, 1))
    out["s0_gla"] = f(i["state_gla"].transpose(0, 2, 3, 1, 4).reshape(DEPTH, P, NB, DV))
    out["s0_hgrn"] = f(i["state_hgrn"].transpose(0, 2, 3, 1, 4).reshape(DEPTH, 2, P, NB, DV).transpose(0, 2, 1, 3, 4))
    out["kcache"] = f(i["cache_k_win"].reshape(DEPTH, NB, PAST, 4, P).transpose(0, 1, 4, 3, 2))
    out["vcache"] = f(i["cache_v_win"].reshape(DEPTH, NB, P, 8, 512))
    return out


OUTS = {
    "y": (P, KC, T), "os_gla_p": (DEPTH, P, DV), "os_hgrn_p": (DEPTH, P, 2, DV),
    "ok_p": (DEPTH, P, 4, SEQ), "ov_p": (DEPTH, P, TT, 512),
    "os_gla_s": (DEPTH, P, NB, DV), "os_hgrn_s": (DEPTH, P, 2, NB, DV),
    "ok_s": (DEPTH, NB, P, 4, PAST), "ov_s": (DEPTH, NB, P, 8, 512),
}


def lay_outputs(r):
    y = r["y"].transpose(1, 0, 2).reshape(D_MODEL, T).T
    return (
        np.ascontiguousarray(y[:SEQ]).reshape(1, SEQ, D_MODEL),
        np.ascontiguousarray(y[SEQ:]).reshape(NB, DEC, D_MODEL),
        r["os_gla_p"].reshape(DEPTH, 1, HEADS_A, DK_A, DV),
        r["os_hgrn_p"].transpose(0, 2, 1, 3).reshape(DEPTH, 1, HEADS_B, DK_B, DV),
        r["ok_p"].transpose(0, 3, 2, 1).reshape(DEPTH, 1, SEQ, AH, DH),
        r["ov_p"].transpose(0, 2, 1, 3).reshape(DEPTH, 1, SEQ, AH, DH),
        r["os_gla_s"].reshape(DEPTH, HEADS_A, DK_A, NB, DV).transpose(0, 3, 1, 2, 4),
        r["os_hgrn_s"].transpose(0, 2, 1, 3, 4).reshape(DEPTH, HEADS_B, DK_B, NB, DV).transpose(0, 3, 1, 2, 4),
        r["ok_s"].transpose(0, 1, 4, 3, 2).reshape(DEPTH, NB, PAST, AH, DH),
        r["ov_s"].reshape(DEPTH, NB, PAST, AH, DH),
    )


def kernel(**inputs):
    import concourse.bacc as bacc
    from concourse.bass_utils import run_bass_kernel_spmd

    nc = bacc.Bacc("TRN2", target_bir_lowering=False, num_devices=1)
    arrays = lay_inputs({n: np.asarray(a) for n, a in inputs.items()})
    d = {n: nc.dram_tensor(n, a.shape, F32, kind="ExternalInput").ap() for n, a in arrays.items()}
    d |= {n: nc.dram_tensor(n, s, F32, kind="ExternalOutput").ap() for n, s in OUTS.items()}
    build(nc, d)
    r = run_bass_kernel_spmd(nc, [arrays], core_ids=[0])
    return lay_outputs({n: np.asarray(r.results[0][n]) for n in OUTS})
```
